# Optimizing a Trainium2 kernel written in Bass

```python
import jax
import jax.numpy as jnp
from jax import lax
import numpy as np

D_MODEL = 1024
BATCH = 1
SEQ = 512
DEPTH = 1

GRID_W = 64
CTX_LEN = 256
N_DIR = 2
N_MOD = 6
NORM_EPS = 1e-6

RWKV_HEAD = 64
RWKV_HEADS = 8
D_RWKV = RWKV_HEADS * RWKV_HEAD
LORA_W = 64
LORA_A = 64
LORA_G = 128
RWKV_COLS = 3 * D_RWKV + LORA_W + LORA_A + LORA_G
GN_EPS = 64e-5

MLSTM_HEADS = 4
MLSTM_DQK = 64
MLSTM_DV = 128
D_MLSTM_QK = MLSTM_HEADS * MLSTM_DQK
D_MLSTM = MLSTM_HEADS * MLSTM_DV
MLSTM_CHUNK = 64

IN_SIZES = (RWKV_COLS, 2 * D_MLSTM_QK, D_MLSTM, N_DIR * MLSTM_HEADS, N_DIR * MLSTM_HEADS, D_MLSTM, D_MODEL, D_MODEL)
IN_COLS = RWKV_COLS + 2 * D_MLSTM_QK + 2 * D_MLSTM + 2 * N_DIR * MLSTM_HEADS + 2 * D_MODEL

PEER_HEADS = 8
N_KEYS = 128
N_EXPERTS = N_KEYS * N_KEYS
PEER_TOPK = 16
PEER_QDIM = 256
KEY_DIM = PEER_QDIM // 2
PEER_BLOCK = 128

kernel_name = "hybrid_rwkv7_mlstm_peer_dit_layer"

def split_sizes(z, sizes):
    return jnp.split(z, np.cumsum(sizes)[:-1].tolist(), axis=-1)

def rmsnorm(z, g):
    zf = z.astype(jnp.float32)
    y = zf * lax.rsqrt(jnp.mean(zf * zf, axis=-1, keepdims=True) + NORM_EPS)
    return y.astype(z.dtype) * g

def modulate(h, shift, scale):
    return h * (1.0 + scale) + shift

def centred_conv3(z, w, axis):
    n = z.shape[axis]
    pad = [(0, 0)] * z.ndim
    pad[axis] = (1, 1)
    zp = jnp.pad(z, pad)
    prev = lax.slice_in_dim(zp, 0, n, axis=axis)
    nxt = lax.slice_in_dim(zp, 2, n + 2, axis=axis)
    return w[0] * prev + w[1] * z + w[2] * nxt

def both_dirs(z):
    return jnp.stack([z, jnp.flip(z, axis=1)], axis=2)

def orient(z):
    return jnp.stack([z[:, :, 0], jnp.flip(z[:, :, 1], axis=1)], axis=2)

def rwkv_branch(feats, S0, lp, need_out):
    B, T, _ = feats.shape
    r, k, v, wd, ad, gd = split_sizes(feats.astype(jnp.float32), (D_RWKV, D_RWKV, D_RWKV, LORA_W, LORA_A, LORA_G))
    w_log = -jax.nn.softplus(-(lp["rwkv_w0"] + jnp.einsum("btr,zrc->btzc", jnp.tanh(wd), lp["rwkv_w_up"]))) - 0.5
    decay = jnp.exp(-jnp.exp(w_log))
    a = jax.nn.sigmoid(lp["rwkv_a0"] + jnp.einsum("btr,zrc->btzc", ad, lp["rwkv_a_up"]))
    kk = (k * lp["rwkv_k_k"]).reshape(B, T, RWKV_HEADS, RWKV_HEAD)
    kk = (kk / jnp.maximum(jnp.linalg.norm(kk, axis=-1, keepdims=True), 1e-12)).reshape(B, T, D_RWKV)
    k_eff = k[:, :, None] * (1.0 + (a - 1.0) * lp["rwkv_k_a"])

    def heads(z):
        return jnp.moveaxis(z.reshape(B, T, N_DIR, RWKV_HEADS, RWKV_HEAD), 1, 0)

    xs = (heads(orient(k_eff)), heads(both_dirs(v)), heads(orient(decay)), heads(both_dirs(kk)), heads(orient(a)))
    if need_out:
        xs = xs + (heads(both_dirs(r)),)

    def step(S, inp):
        k_t, v_t, w_t, kk_t, a_t = inp[:5]
        s_kk = jnp.einsum("...vk,...k->...v", S, kk_t)
        S = S * w_t[..., None, :] - s_kk[..., :, None] * (kk_t * a_t)[..., None, :] + v_t[..., :, None] * k_t[..., None, :]
        if need_out:
            return S, jnp.einsum("...vk,...k->...v", S, inp[5])
        return S, None

    S, out = lax.scan(step, S0, xs)
    if not need_out:
        return None, S
    out = orient(jnp.moveaxis(out, 0, 1))
    mu = jnp.mean(out, axis=-1, keepdims=True)
    var = jnp.mean((out - mu) ** 2, axis=-1, keepdims=True)
    ln_w = lp["rwkv_ln_w"].reshape(RWKV_HEADS, RWKV_HEAD)
    ln_b = lp["rwkv_ln_b"].reshape(RWKV_HEADS, RWKV_HEAD)
    gn = (out - mu) * lax.rsqrt(var + GN_EPS) * ln_w + ln_b
    rh = r.reshape(B, T, 1, RWKV_HEADS, RWKV_HEAD)
    kh = k_eff.reshape(B, T, N_DIR, RWKV_HEADS, RWKV_HEAD)
    vh = v.reshape(B, T, 1, RWKV_HEADS, RWKV_HEAD)
    bonus = jnp.sum(rh * kh * lp["rwkv_r_k"].reshape(RWKV_HEADS, RWKV_HEAD), axis=-1, keepdims=True) * vh
    y = jnp.sum(gn + bonus, axis=2).reshape(B, T, D_RWKV)
    g = jax.nn.sigmoid(gd) @ lp["rwkv_g_up"]
    return (y * g).astype(feats.dtype), S

def mlstm_branch(qk, v, i_pre, f_pre, o_pre, state0, lp, need_out):
    B, T, _ = v.shape
    H = MLSTM_HEADS
    nc = T // MLSTM_CHUNK
    q, k = jnp.split(jax.nn.silu(qk.astype(jnp.float32)), 2, axis=-1)
    q = both_dirs(q.reshape(B, T, H, MLSTM_DQK))
    k = both_dirs(k.reshape(B, T, H, MLSTM_DQK) * MLSTM_DQK ** -0.5)
    vv = both_dirs(v.astype(jnp.float32).reshape(B, T, H, MLSTM_DV))
    ig = orient(i_pre.astype(jnp.float32).reshape(B, T, N_DIR, H) + lp["mlstm_i_b"])
    lf = orient(jax.nn.log_sigmoid(f_pre.astype(jnp.float32).reshape(B, T, N_DIR, H) + lp["mlstm_f_b"]))

    def chunks(z):
        z = z.reshape((B, nc, MLSTM_CHUNK) + z.shape[2:])
        return jnp.moveaxis(jnp.moveaxis(z, 1, 0), 2, 4)

    causal = jnp.tril(jnp.ones((MLSTM_CHUNK, MLSTM_CHUNK), dtype=bool))

    def step(carry, inp):
        C, n, m = carry
        kc, vc, ic, fc = inp[:4]
        b = jnp.cumsum(fc, axis=-1)
        b_end = b[..., -1]
        g_end = b_end[..., None] - b + ic
        m_new = jnp.maximum(b_end + m, jnp.max(g_end, axis=-1))
        w_end = jnp.exp(g_end - m_new[..., None])
        keep = jnp.exp(b_end + m - m_new)
        C_new = keep[..., None, None] * C + jnp.einsum("...sv,...sd->...vd", vc * w_end[..., None], kc)
        n_new = keep[..., None] * n + jnp.einsum("...s,...sd->...d", w_end, kc)
        if not need_out:
            return (C_new, n_new, m_new), None
        qc = inp[4]
        log_d = jnp.where(causal, b[..., :, None] - b[..., None, :] + ic[..., None, :], -jnp.inf)
        inter = b + m[..., None]
        m_row = jnp.maximum(inter, jnp.max(log_d, axis=-1))
        s = jnp.einsum("...jd,...sd->...js", qc, kc) * jnp.exp(log_d - m_row[..., None])
        a_inter = jnp.exp(inter - m_row)
        num = jnp.einsum("...js,...sv->...jv", s, vc) + a_inter[..., None] * jnp.einsum("...vd,...jd->...jv", C, qc)
        den = jnp.sum(s, axis=-1) + a_inter * jnp.einsum("...d,...jd->...j", n, qc)
        h = num / jnp.maximum(jnp.abs(den), jnp.exp(-m_row))[..., None]
        return (C_new, n_new, m_new), h

    xs = (chunks(k), chunks(vv), chunks(ig), chunks(lf))
    if need_out:
        xs = xs + (chunks(q),)
    state, h = lax.scan(step, state0, xs)
    if not need_out:
        return None, state
    h = jnp.moveaxis(jnp.moveaxis(h, 4, 2), 0, 1).reshape(B, T, N_DIR, H, MLSTM_DV)
    h = orient(h)
    h = h * lax.rsqrt(jnp.mean(h * h, axis=-1, keepdims=True) + NORM_EPS) * lp["mlstm_norm_g"].reshape(H, MLSTM_DV)
    y = jnp.sum(h, axis=2).reshape(B, T, D_MLSTM) * jax.nn.sigmoid(o_pre.astype(jnp.float32))
    return y.astype(v.dtype), state

def token_mixer(P, rwkv_s0, mlstm_s0, lp, on_grid, need_out):
    B, T, _ = P.shape
    rw, qk, mv, ml_i, ml_f, ml_o, gate_a, gate_b = split_sizes(P, IN_SIZES)
    if on_grid:
        rows = T // GRID_W
        rw = centred_conv3(rw.reshape(B, rows, GRID_W, -1), lp["rwkv_conv"], 2).reshape(B, T, -1)

        def to_col(z):
            return z.reshape(B, rows, GRID_W, -1).transpose(0, 2, 1, 3)

        qk = centred_conv3(to_col(qk), lp["mlstm_conv"], 2).reshape(B, T, -1)
        mv, ml_i, ml_f, ml_o = [to_col(z).reshape(B, T, -1) for z in (mv, ml_i, ml_f, ml_o)]
    else:
        rw = centred_conv3(rw, lp["rwkv_conv"], 1)
        qk = centred_conv3(qk, lp["mlstm_conv"], 1)
    y_a, rwkv_s = rwkv_branch(rw, rwkv_s0, lp, need_out)
    y_b, mlstm_s = mlstm_branch(qk, mv, ml_i, ml_f, ml_o, mlstm_s0, lp, need_out)
    if not need_out:
        return None, rwkv_s, mlstm_s
    if on_grid:
        y_b = y_b.reshape(B, GRID_W, rows, -1).transpose(0, 2, 1, 3).reshape(B, T, -1)
    merged = jax.nn.sigmoid(gate_a) * (y_a @ lp["w_branch_a"]) + jax.nn.sigmoid(gate_b) * (y_b @ lp["w_branch_b"])
    return merged @ lp["w_out"], rwkv_s, mlstm_s

def peer_ffn(h, wq, keys, u, v):
    B, T, D = h.shape
    nb = (B * T) // PEER_BLOCK

    def block(hb):
        q = (hb @ wq).reshape(PEER_BLOCK, PEER_HEADS, 2, KEY_DIM)
        s = jnp.einsum("mhpd,hpkd->mhpk", q, keys).astype(jnp.float32)
        s1, i1 = lax.top_k(s[:, :, 0], PEER_TOPK)
        s2, i2 = lax.top_k(s[:, :, 1], PEER_TOPK)
        cand = (s1[..., :, None] + s2[..., None, :]).reshape(PEER_BLOCK, PEER_HEADS, PEER_TOPK * PEER_TOPK)
        sc, ci = lax.top_k(cand, PEER_TOPK)
        idx = (jnp.take_along_axis(i1, ci // PEER_TOPK, axis=-1) * N_KEYS
               + jnp.take_along_axis(i2, ci % PEER_TOPK, axis=-1)).reshape(PEER_BLOCK, -1)
        g = jax.nn.softmax(sc, axis=-1).reshape(PEER_BLOCK, -1)
        act = jax.nn.gelu(jnp.einsum("med,md->me", u[idx], hb), approximate=False)
        return jnp.einsum("me,med->md", (g * act).astype(hb.dtype), v[idx])

    return lax.map(block, h.reshape(nb, PEER_BLOCK, D)).reshape(B, T, D)

def setup_inputs(seed: int = 0) -> dict:
    key = jax.random.key(seed)
    ks = jax.random.split(key, 32)
    L = DEPTH

    def nrm(k, shape, s):
        return jax.random.normal(k, shape, jnp.float32) * s

    shift_init = jnp.array([0.25, 0.5, 0.25], jnp.float32)[None, :, None]
    return {
        "x": nrm(ks[0], (BATCH, SEQ, D_MODEL), 1.0),
        "c": nrm(ks[1], (BATCH, D_MODEL), 1.0),
        "ctx": nrm(ks[2], (BATCH, CTX_LEN, D_MODEL), 1.0),
        "c_ctx": nrm(ks[3], (D_MODEL,), 1.0),
        "ada_w": nrm(ks[4], (L, D_MODEL, N_MOD * D_MODEL), 0.3 * D_MODEL ** -0.5),
        "ada_b": nrm(ks[5], (L, N_MOD * D_MODEL), 0.02),
        "norm1_g": 1.0 + nrm(ks[6], (L, D_MODEL), 0.1),
        "w_in": nrm(ks[7], (L, D_MODEL, IN_COLS), D_MODEL ** -0.5),
        "rwkv_conv": shift_init + nrm(ks[8], (L, 3, RWKV_COLS), 0.05),
        "rwkv_w0": jax.random.uniform(ks[9], (L, N_DIR, D_RWKV), jnp.float32, minval=-6.0, maxval=1.0),
        "rwkv_w_up": nrm(ks[10], (L, N_DIR, LORA_W, D_RWKV), 0.5 * LORA_W ** -0.5),
        "rwkv_a0": nrm(ks[11], (L, N_DIR, D_RWKV), 0.5),
        "rwkv_a_up": nrm(ks[12], (L, N_DIR, LORA_A, D_RWKV), 0.5 * LORA_A ** -0.5),
        "rwkv_g_up": nrm(ks[13], (L, LORA_G, D_RWKV), LORA_G ** -0.5),
        "rwkv_k_k": 0.85 + nrm(ks[14], (L, D_RWKV), 0.05),
        "rwkv_k_a": 1.0 + nrm(ks[15], (L, D_RWKV), 0.05),
        "rwkv_r_k": nrm(ks[16], (L, D_RWKV), 0.1),
        "rwkv_ln_w": 1.0 + nrm(ks[17], (L, D_RWKV), 0.1),
        "rwkv_ln_b": nrm(ks[18], (L, D_RWKV), 0.01),
        "mlstm_conv": shift_init + nrm(ks[19], (L, 3, 2 * D_MLSTM_QK), 0.05),
        "mlstm_i_b": nrm(ks[20], (L, N_DIR, MLSTM_HEADS), 0.5),
        "mlstm_f_b": 3.0 + nrm(ks[21], (L, N_DIR, MLSTM_HEADS), 0.5),
        "mlstm_norm_g": 1.0 + nrm(ks[22], (L, D_MLSTM), 0.1),
        "w_branch_a": nrm(ks[23], (L, D_RWKV, D_MODEL), D_RWKV ** -0.5),
        "w_branch_b": nrm(ks[24], (L, D_MLSTM, D_MODEL), D_MLSTM ** -0.5),
        "w_out": nrm(ks[25], (L, D_MODEL, D_MODEL), D_MODEL ** -0.5),
        "norm2_g": 1.0 + nrm(ks[26], (L, D_MODEL), 0.1),
        "peer_wq": nrm(ks[27], (L, D_MODEL, PEER_HEADS * PEER_QDIM), D_MODEL ** -0.5),
        "peer_keys": nrm(ks[28], (L, PEER_HEADS, 2, N_KEYS, KEY_DIM), KEY_DIM ** -0.5),
        "peer_u": nrm(ks[29], (L, N_EXPERTS, D_MODEL), D_MODEL ** -0.5),
        "peer_v": nrm(ks[30], (L, N_EXPERTS, D_MODEL), PEER_HEADS ** -0.5),
        "final_g": 1.0 + nrm(ks[31], (D_MODEL,), 0.1),
    }

def reference(x, c, ctx, c_ctx, ada_w, ada_b, norm1_g, w_in, rwkv_conv, rwkv_w0, rwkv_w_up, rwkv_a0,
              rwkv_a_up, rwkv_g_up, rwkv_k_k, rwkv_k_a, rwkv_r_k, rwkv_ln_w, rwkv_ln_b, mlstm_conv,
              mlstm_i_b, mlstm_f_b, mlstm_norm_g, w_branch_a, w_branch_b, w_out, norm2_g, peer_wq,
              peer_keys, peer_u, peer_v, final_g):
    B = x.shape[0]
    silu_c = jax.nn.silu(c)
    silu_cc = jax.nn.silu(c_ctx)
    for i in range(DEPTH):
        last = i == DEPTH - 1
        lp = {
            "rwkv_conv": rwkv_conv[i], "rwkv_w0": rwkv_w0[i], "rwkv_w_up": rwkv_w_up[i],
            "rwkv_a0": rwkv_a0[i], "rwkv_a_up": rwkv_a_up[i], "rwkv_g_up": rwkv_g_up[i],
            "rwkv_k_k": rwkv_k_k[i], "rwkv_k_a": rwkv_k_a[i], "rwkv_r_k": rwkv_r_k[i],
            "rwkv_ln_w": rwkv_ln_w[i], "rwkv_ln_b": rwkv_ln_b[i], "mlstm_conv": mlstm_conv[i],
            "mlstm_i_b": mlstm_i_b[i], "mlstm_f_b": mlstm_f_b[i], "mlstm_norm_g": mlstm_norm_g[i],
            "w_branch_a": w_branch_a[i], "w_branch_b": w_branch_b[i], "w_out": w_out[i],
        }
        sh1, sc1, gt1, sh2, sc2, gt2 = [z[:, None] for z in jnp.split(silu_c @ ada_w[i] + ada_b[i], N_MOD, axis=-1)]
        csh1, csc1, cgt1, csh2, csc2, cgt2 = jnp.split(silu_cc @ ada_w[i] + ada_b[i], N_MOD, axis=-1)

        rwkv0 = jnp.zeros((B, N_DIR, RWKV_HEADS, RWKV_HEAD, RWKV_HEAD), jnp.float32)
        mlstm0 = (jnp.zeros((B, N_DIR, MLSTM_HEADS, MLSTM_DV, MLSTM_DQK), jnp.float32),
                  jnp.zeros((B, N_DIR, MLSTM_HEADS, MLSTM_DQK), jnp.float32),
                  jnp.zeros((B, N_DIR, MLSTM_HEADS), jnp.float32))
        hc = modulate(rmsnorm(ctx, norm1_g[i]), csh1, csc1)
        out_c, rwkv_s, mlstm_s = token_mixer(hc @ w_in[i], rwkv0, mlstm0, lp, False, not last)

        hx = modulate(rmsnorm(x, norm1_g[i]), sh1, sc1)
        out_x, _, _ = token_mixer(hx @ w_in[i], rwkv_s, mlstm_s, lp, True, True)
        x = x + gt1 * out_x
        x = x + gt2 * peer_ffn(modulate(rmsnorm(x, norm2_g[i]), sh2, sc2), peer_wq[i], peer_keys[i], peer_u[i], peer_v[i])

        if not last:
            ctx = ctx + cgt1 * out_c
            ctx = ctx + cgt2 * peer_ffn(modulate(rmsnorm(ctx, norm2_g[i]), csh2, csc2), peer_wq[i], peer_keys[i], peer_u[i], peer_v[i])
    return rmsnorm(x, final_g)


_drawn_inputs = setup_inputs


def setup_inputs(seed=0):
    import zlib

    import numpy as np

    out = dict(_drawn_inputs(seed))
    spreads = {}
    factors = {'c_ctx': 4.706,
     'ada_b': 3.251,
     'rwkv_w_up': 8.0,
     'rwkv_a0': 3.786,
     'rwkv_a_up': 4.893,
     'rwkv_k_k': 8.0,
     'rwkv_k_a': 8.0,
     'rwkv_r_k': 4.343,
     'rwkv_ln_w': 6.656,
     'rwkv_ln_b': 56.789,
     'mlstm_i_b': 64.0,
     'mlstm_f_b': 59.432,
     'mlstm_norm_g': 6.015,
     'norm2_g': 4.462}
    for name, (base, spread) in spreads.items():
        noise = np.random.default_rng([zlib.crc32(name.encode()), seed]).standard_normal(out[name].shape)
        drawn = base * np.exp(spread * noise) if base else spread * noise
        out[name] = jnp.asarray(drawn.astype(out[name].dtype))
    for name, factor in factors.items():
        out[name] = (out[name] * factor).astype(out[name].dtype)
    return out
```

```python
from contextlib import ExitStack

import numpy as np

import concourse.bass as bass
from concourse import mybir

F32 = mybir.dt.float32
U32 = mybir.dt.uint32
ALU = mybir.AluOpType
ACT = mybir.ActivationFunctionType
AX = mybir.AxisListType

P = 128
D = 1024
KT = D // P
TX, TC = 512, 256
GRID_W = 64
ROWS = TX // GRID_W
N_MOD = 6
NORM_EPS = 1e-6
NEG = -1e30

D_RWKV = 512
RW_TILES = 14
PAIRS = 4
C = 64
GN_EPS = 64e-5
DECAY = float(np.exp(-0.5))

MH = 4
DQK, DV = 64, 128
MC = 128
GROWS = 36
QK_TILES = 4

PH, NK, TOPK = 8, 128, 16


class Count:

    def __init__(self, eng, sem):
        self.eng, self.sem, self.n = eng, sem, 0

    def __call__(self, ins):
        ins.then_inc(self.sem, 1)
        self.n += 1
        self.eng.wait_ge(self.sem, self.n)


class Steps:

    def __init__(self, sem, names):
        self.sem, self.names = sem, list(names)

    def start(self, eng):
        eng.sem_inc(self.sem, 1)

    def wait(self, eng, i, name):
        eng.wait_ge(self.sem, i * len(self.names) + (self.names.index(name) + 2))

    def wait_last(self, eng, i):
        eng.wait_ge(self.sem, i * len(self.names) + 1)

    def mark(self, ins):
        ins.then_inc(self.sem, 1)


class Buffers:

    def __init__(self):
        self.used = []

    def semaphore(self, nc, name):
        s = nc.alloc_semaphore(name)
        self.used.append(s)
        return s

    def clear_semaphores(self, nc):
        nc.clear_and_free_semaphores(self.used)
        self.used = []
        nc.all_engine_barrier()


def alloc(nc, ctx):
    def sb(name, shape, dt=F32):
        return ctx.enter_context(nc.sbuf_tensor(name, shape, dt))
    return sb


def phase_modulation(nc, a, b):
    GROUP = 4
    with ExitStack() as ctx:
        sb = alloc(nc, ctx)

        def sem(name):
            return b.semaphore(nc, name)

        cc = sb("cc", [P, KT, 2])
        th = sb("cc_th", [P, KT, 2])
        sc = sb("cc_silu", [P, KT, 2])
        w_ring = sb("ada_ring", [P, GROUP, KT, P])
        bias = sb("ada_bias", [P, N_MOD * KT])
        g1 = sb("g1", [P, KT])
        sq = sb("sq", [P, KT, TX + TC])
        xx = sb("x_in", [P, KT, TX])
        xc = sb("xc", [P, KT, TC])
        rs = sb("rs", [P, TX + TC])
        scale = sb("scale1", [P, 2, KT])
        ps_mod = ctx.enter_context(nc.psum_tensor("ps_mod", [P, 512], F32))
        ps_sx = ctx.enter_context(nc.psum_tensor("ps_sx", [P, TX], F32))
        ps_sc = ctx.enter_context(nc.psum_tensor("ps_sc", [P, 512], F32))
        small_in, x_in = sem("mod_small_in"), sem("mod_x_in")
        ring_in = [sem(f"ada_in{k}") for k in range(GROUP)]
        tanh_done, silu_done = sem("mod_tanh"), sem("mod_silu")
        mm_done, mod_done = sem("mod_mm"), sem("mod_evac")
        sq_done, sum_done, sqrt_done = sem("sq_done"), sem("sum_done"), sem("sqrt_done")
        dve = sem("mod_dve")
        n_loop = N_MOD * KT // GROUP
        block = ctx.enter_context(nc.Block())

        @block.sync
        def _(sp):
            sp.dma_start(cc[:], a["cc"]).then_inc(small_in, 16)
            sp.dma_start(bias[:], a["ada_b"]).then_inc(small_in, 16)
            sp.dma_start(g1[:], a["norm1_g"]).then_inc(small_in, 16)
            sp.dma_start(xx[:], a["xT"]).then_inc(x_in, 16)
            sp.dma_start(xc[:], a["ctxT"]).then_inc(x_in, 16)
            for k in range(GROUP):
                sp.dma_start(w_ring[:, k], a["ada_w"][k]).then_inc(ring_in[k], 16)
            with sp.Fori(1, n_loop) as i:
                for k in range(GROUP):
                    sp.wait_ge(mm_done, i * GROUP - GROUP + 1 + k)
                    sp.dma_start(w_ring[:, k], a["ada_w"][i * GROUP + k]).then_inc(ring_in[k], 16)

        @block.scalar
        def _(act):
            act.wait_ge(small_in, 48)
            act.activation(th[:], cc[:], ACT.Tanh, scale=0.5).then_inc(tanh_done, 1)
            act.wait_ge(x_in, 32)
            act.activation(sq[:, :, 0:TX], xx[:], ACT.Square).then_inc(sq_done, 1)
            act.activation(sq[:, :, TX:], xc[:], ACT.Square).then_inc(sq_done, 1)
            act.wait_ge(sum_done, 1)
            act.activation(rs[:, 0:TX], ps_sx[:], ACT.Sqrt, bias=b.eps[:, 0:1], scale=1.0 / D).then_inc(sqrt_done, 1)
            act.activation(rs[:, TX:], ps_sc[:, 0:TC], ACT.Sqrt, bias=b.eps[:, 0:1], scale=1.0 / D).then_inc(sqrt_done, 1)

        @block.tensor
        def _(pe):
            pe.wait_ge(sq_done, 2)
            for k in range(KT):
                pe.matmul(ps_sx[:], b.ones[:], sq[:, k, 0:TX], start=(k == 0), stop=(k == KT - 1))
            for k in range(KT):
                mm = pe.matmul(ps_sc[:, 0:TC], b.ones[:], sq[:, k, TX:], start=(k == 0), stop=(k == KT - 1))
            mm.then_inc(sum_done, 1)
            pe.wait_ge(silu_done, 1)
            with pe.Fori(0, n_loop) as i:
                pe.wait_ge(mod_done, i + 1)
                for g in range(GROUP):
                    pe.wait_ge(ring_in[g], i * 16 + 16)
                    for k in range(KT):
                        mm = pe.matmul(ps_mod[:, 2 * g:2 * g + 2], w_ring[:, g, k, :], sc[:, k, :],
                                       start=(k == 0), stop=(k == KT - 1))
                    mm.then_inc(mm_done, 1)

        @block.vector
        def _(v):
            link = Count(v, dve)
            v.wait_ge(small_in, 48)
            v.wait_ge(tanh_done, 1)
            link(v.scalar_tensor_tensor(out=sc[:], in0=th[:], scalar=1.0, in1=cc[:], op0=ALU.add, op1=ALU.mult))
            v.tensor_scalar(sc[:], sc[:], 0.5, None, ALU.mult).then_inc(silu_done, 1)
            v.sem_inc(mod_done, 1)
            with v.Fori(0, n_loop) as i:
                v.wait_ge(mm_done, i * GROUP + GROUP)
                v.tensor_tensor(b.mod[:, bass.ds(i * GROUP, GROUP), :],
                                ps_mod[:, 0:2 * GROUP].rearrange("p (g s) -> p g s", s=2),
                                bias[:, bass.ds(i * GROUP, GROUP)].unsqueeze(2).to_broadcast([P, GROUP, 2]),
                                ALU.add).then_inc(mod_done, 1)
            v.wait_ge(mod_done, n_loop + 1)
            for s in range(2):
                link(v.scalar_tensor_tensor(out=scale[:, s], in0=b.mod[:, KT:2 * KT, s], scalar=1.0, in1=g1[:],
                                            op0=ALU.add, op1=ALU.mult))
            v.wait_ge(sqrt_done, 2)
            link(v.reciprocal(rs[:], rs[:]))
            for s, (src, lo, hi) in enumerate(((xx, 0, TX), (xc, TX, TX + TC))):
                for k in range(KT):
                    v.scalar_tensor_tensor(out=b.hT[:, k, lo:hi], in0=src[:, k, :], scalar=scale[:, s, k:k + 1],
                                           in1=rs[:, lo:hi], op0=ALU.mult, op1=ALU.mult).then_inc(dve, 1)
                    link.n += 1
                    v.wait_ge(dve, link.n)
                    link(v.tensor_scalar(b.hT[:, k, lo:hi], b.hT[:, k, lo:hi], b.mod[:, k, s:s + 1], None, ALU.add))


def phase_projection(nc, a, b, h_dram):
    with ExitStack() as ctx:
        sb = alloc(nc, ctx)

        def sem(name):
            return b.semaphore(nc, name)

        ring = sb("win_ring", [P, 2, KT, P])
        wv = sb("win_v", [P, KT, MH * DV])
        wg = sb("win_gates", [P, KT, 2, GROWS])
        cw = sb("conv_r", [P, RW_TILES, 3])
        cq = sb("conv_q", [P, QK_TILES, 3])
        th = sb("qk_tanh", [P, QK_TILES, TX])
        hcol = sb("h_column_major", [P, KT, TX])
        ps_x = [ctx.enter_context(nc.psum_tensor(f"ps_px{k}", [P, TX], F32)) for k in range(2)]
        ps_c = [ctx.enter_context(nc.psum_tensor(f"ps_pc{k}", [P, 512], F32)) for k in range(2)]
        ps_v = [ctx.enter_context(nc.psum_tensor(f"ps_pv{k}", [P, 512], F32)) for k in range(2)]
        small_in, v_in = sem("proj_small_in"), sem("proj_v_in")
        ring_in = [sem(f"proj_in{k}") for k in range(2)]
        mm_done = [sem(f"proj_mm{k}") for k in range(2)]
        centre = [sem(f"proj_centre{k}") for k in range(2)]
        taps = [sem(f"proj_taps{k}") for k in range(2)]
        v_mm, v_out = sem("proj_v_mm"), sem("proj_v_out")
        g_mm, g_out = sem("proj_g_mm"), sem("proj_g_out")
        tanh_done, dve = sem("proj_tanh"), sem("proj_dve")
        col_done, h_out = sem("proj_col"), sem("proj_h_out")
        n_r, n_q = RW_TILES // 2, QK_TILES // 2
        block = ctx.enter_context(nc.Block())

        @block.gpsimd
        def _(g):
            for j in range(KT):
                g.tensor_copy(hcol[:, j, :].rearrange("p (w r) -> p w r", r=ROWS),
                              b.hT[:, j, 0:TX].rearrange("p (r w) -> p w r", w=GRID_W)).then_inc(col_done, 1)

        @block.sync
        def _(sp):
            for k in range(2):
                sp.dma_start(ring[:, k], a["w_rw"][k]).then_inc(ring_in[k], 16)
            sp.dma_start(cw[:], a["rwkv_conv"]).then_inc(small_in, 16)
            sp.dma_start(cq[:], a["mlstm_conv"]).then_inc(small_in, 16)
            with sp.Fori(1, n_r + n_q) as i:
                for k in range(2):
                    sp.wait_ge(mm_done[k], i)
                    sp.dma_start(ring[:, k], a["w_rw"][i * 2 + k]).then_inc(ring_in[k], 16)
            sp.dma_start(h_dram, b.hT[:, :, 0:TX]).then_inc(h_out, 16)
            sp.dma_start(wv[:], a["w_mv"]).then_inc(v_in, 16)
            sp.dma_start(wg[:], a["w_gates"]).then_inc(v_in, 16)
            sp.wait_ge(h_out, 16)

        @block.tensor
        def _(pe):
            with pe.Fori(0, n_r + n_q) as i:
                for k in range(2):
                    pe.wait_ge(ring_in[k], i * 16 + 16)
                    pe.wait_ge(taps[k], i + 1)
                    for j in range(KT):
                        pe.matmul(ps_x[k][:], ring[:, k, j, :], b.hT[:, j, 0:TX], start=(j == 0), stop=(j == KT - 1))
                    for j in range(KT):
                        mm = pe.matmul(ps_c[k][:, 0:TC], ring[:, k, j, :], b.hT[:, j, TX:],
                                       start=(j == 0), stop=(j == KT - 1))
                    mm.then_inc(mm_done[k], 1)
            pe.wait_ge(v_in, 32)
            pe.wait_ge(col_done, KT)
            for t in range((TX + TC) // MC):
                if t >= 2:
                    pe.wait_ge(v_out, t - 1)
                for j in range(KT):
                    if t < TX // MC:
                        lhs = hcol[:, j, t * MC:(t + 1) * MC]
                    else:
                        lhs = b.hT[:, j, t * MC:(t + 1) * MC]
                    mm = pe.matmul(ps_v[t % 2][:], lhs, wv[:, j, :], start=(j == 0), stop=(j == KT - 1))
                mm.then_inc(v_mm, 1)
            pe.wait_ge(taps[0], n_r + n_q + 1)
            pe.wait_ge(taps[1], n_r + n_q + 1)
            for gt in range(2):
                for lo, hi, bank in ((0, TX, ps_x[gt]), (TX, TX + TC, ps_c[gt])):
                    for j in range(KT):
                        mm = pe.matmul(bank[0:GROWS, 0:hi - lo], wg[:, j, gt, :], b.hT[:, j, lo:hi],
                                       start=(j == 0), stop=(j == KT - 1))
            mm.then_inc(g_mm, 1)

        @block.scalar
        def _(act):
            act.wait_ge(small_in, 32)
            for k in range(2):
                act.sem_inc(taps[k], 1)
            with act.Fori(0, n_r) as i:
                for k in range(2):
                    act.wait_ge(mm_done[k], i + 1)
                    t = i * 2 + k
                    act.activation(b.fX[:, bass.ds(t, 1), :], ps_x[k][:].unsqueeze(1), ACT.Copy,
                                   scale=cw[:, bass.ds(t, 1), 1]).then_inc(centre[k], 1)
                    act.activation(b.fC[:, bass.ds(t, 1), :], ps_c[k][:, 0:TC].unsqueeze(1), ACT.Copy,
                                   scale=cw[:, bass.ds(t, 1), 1]).then_inc(centre[k], 1)
            for i in range(n_q):
                for k in range(2):
                    act.wait_ge(mm_done[k], n_r + i + 1)
                    t = 2 * i + k
                    act.activation(b.qX[:, t, :].rearrange("p (w r) -> p r w", r=ROWS),
                                   ps_x[k][:].rearrange("p (r w) -> p r w", w=GRID_W), ACT.Copy,
                                   scale=cq[:, t, 1:2]).then_inc(centre[k], 1)
                    act.activation(b.qC[:, t, :], ps_c[k][:, 0:TC], ACT.Copy, scale=cq[:, t, 1:2]).then_inc(centre[k], 1)
            for t in range((TX + TC) // MC):
                act.wait_ge(v_mm, t + 1)
                act.activation(b.vM[:, t, :, 0:DV], ps_v[t % 2][:].rearrange("p (h v) -> p h v", v=DV),
                               ACT.Copy).then_inc(v_out, 1)
            act.wait_ge(g_mm, 1)
            for gt in range(2):
                act.activation(b.gates[:, gt, 0:TX].rearrange("p (w r) -> p r w", r=ROWS),
                               ps_x[gt][0:GROWS].rearrange("p (r w) -> p r w", w=GRID_W), ACT.Copy).then_inc(g_out, 1)
                act.activation(b.gates[:, gt, TX:], ps_c[gt][0:GROWS, 0:TC], ACT.Copy).then_inc(g_out, 1)
            act.wait_ge(taps[0], n_r + n_q + 1)
            act.wait_ge(taps[1], n_r + n_q + 1)
            act.activation(th[:], b.qX[:], ACT.Tanh, scale=0.5).then_inc(tanh_done, 1)
            act.wait_ge(dve, 1)
            act.activation(th[:, :, 0:TC], b.qC[:], ACT.Tanh, scale=0.5).then_inc(tanh_done, 1)

        @block.vector
        def _(v):
            v.memset(b.vM[:, :, :, DV:], 1.0).then_inc(sem("ones_column"), 1)
            one = sem("proj_vec")
            with v.Fori(0, n_r) as i:
                for k in range(2):
                    v.wait_ge(centre[k], i * 2 + 2)
                    t = i * 2 + k
                    z = ps_x[k][:].rearrange("p (r w) -> p r w", w=GRID_W)
                    o = b.fX[:, bass.ds(t, 1), :].rearrange("p o (r w) -> p (o r) w", w=GRID_W)
                    zc, oc = ps_c[k][:, 0:TC], b.fC[:, bass.ds(t, 1), :].rearrange("p o w -> p (o w)")
                    v.scalar_tensor_tensor(out=o[:, :, 1:], in0=z[:, :, :-1], scalar=cw[:, bass.ds(t, 1), 0],
                                           in1=o[:, :, 1:], op0=ALU.mult, op1=ALU.add)
                    v.scalar_tensor_tensor(out=oc[:, 1:], in0=zc[:, :-1], scalar=cw[:, bass.ds(t, 1), 0],
                                           in1=oc[:, 1:], op0=ALU.mult, op1=ALU.add).then_inc(one, 1)
                    v.wait_ge(one, i * 2 + k + 1)
                    v.scalar_tensor_tensor(out=o[:, :, :-1], in0=z[:, :, 1:], scalar=cw[:, bass.ds(t, 1), 2],
                                           in1=o[:, :, :-1], op0=ALU.mult, op1=ALU.add)
                    v.scalar_tensor_tensor(out=oc[:, :-1], in0=zc[:, 1:], scalar=cw[:, bass.ds(t, 1), 2],
                                           in1=oc[:, :-1], op0=ALU.mult, op1=ALU.add).then_inc(taps[k], 1)
            for i in range(n_q):
                for k in range(2):
                    v.wait_ge(centre[k], 2 * (n_r + i) + 2)
                    t = 2 * i + k
                    z = ps_x[k][:].rearrange("p (r w) -> p r w", w=GRID_W)
                    o = b.qX[:, t, :].rearrange("p (w r) -> p r w", r=ROWS)
                    zc, oc = ps_c[k][:, 0:TC], b.qC[:, t, :]
                    v.scalar_tensor_tensor(out=o[:, 1:, :], in0=z[:, :-1, :], scalar=cq[:, t, 0:1],
                                           in1=o[:, 1:, :], op0=ALU.mult, op1=ALU.add)
                    v.scalar_tensor_tensor(out=oc[:, 1:], in0=zc[:, :-1], scalar=cq[:, t, 0:1],
                                           in1=oc[:, 1:], op0=ALU.mult, op1=ALU.add).then_inc(one, 1)
                    v.wait_ge(one, RW_TILES + t + 1)
                    v.scalar_tensor_tensor(out=o[:, :-1, :], in0=z[:, 1:, :], scalar=cq[:, t, 2:3],
                                           in1=o[:, :-1, :], op0=ALU.mult, op1=ALU.add)
                    v.scalar_tensor_tensor(out=oc[:, :-1], in0=zc[:, 1:], scalar=cq[:, t, 2:3],
                                           in1=oc[:, :-1], op0=ALU.mult, op1=ALU.add).then_inc(taps[k], 1)
            v.wait_ge(taps[0], n_r + n_q + 1)
            v.wait_ge(taps[1], n_r + n_q + 1)
            link = Count(v, dve)
            for s, (z, n) in enumerate(((b.qX, TX), (b.qC, TC))):
                v.wait_ge(tanh_done, s + 1)
                zf, tf = z[:], th[:, :, 0:n]
                link(v.scalar_tensor_tensor(out=zf, in0=tf, scalar=1.0, in1=zf, op0=ALU.add, op1=ALU.mult))
                half = QK_TILES // 2
                link(v.tensor_scalar(z[:, 0:half], z[:, 0:half], 0.5, None, ALU.mult))
                link(v.tensor_scalar(z[:, half:], z[:, half:], 0.5 * DQK ** -0.5, None, ALU.mult))


HALF_DECAY = 0.5 * DECAY
LEVELS = [2, 4, 8, 16, 32]
M_NEG1_TS, M_NEG1_ST, M_STRICT, M_NEG_INCL, M_INCL, M_OFF = 0, 1, 2, 3, 4, 5
N_MASKS = 5 + len(LEVELS)


def rwkv_masks():
    r = np.arange(C)
    out = np.zeros((C, 2, N_MASKS, C), np.float32)
    for z in range(2):
        first = (lambda s, t: s < t) if z == 0 else (lambda s, t: s > t)
        s_t = first(r[:, None], r[None, :])
        t_s = s_t.T

        def off(size):
            same = (r[:, None] // (2 * size)) == (r[None, :] // (2 * size))
            return same & ((r[:, None] // size) != (r[None, :] // size))

        out[:, z, M_NEG1_TS] = -(off(1) & t_s).astype(np.float32)
        out[:, z, M_NEG1_ST] = -(off(1) & s_t).astype(np.float32)
        out[:, z, M_STRICT] = s_t
        out[:, z, M_NEG_INCL] = -(s_t | np.eye(C, dtype=bool)).astype(np.float32)
        out[:, z, M_INCL] = s_t | np.eye(C, dtype=bool)
        for n, size in enumerate(LEVELS):
            out[:, z, M_OFF + n] = off(size) & t_s
    return np.concatenate([out, out], 0)


def phase_rwkv_features(nc, a, b, f, T, tag):
    nch = T // C
    with ExitStack() as ctx:
        sb = alloc(nc, ctx)

        def sem(name):
            return b.semaphore(nc, name + tag)

        wa_up = sb("wa_up" + tag, [P, 2, D_RWKV])
        vecs = sb("rw_vecs" + tag, [P, 6, PAIRS])
        half = sb("rw_half" + tag, [P, 4, PAIRS])
        one_ka = sb("rw_1ka" + tag, [P, PAIRS])
        w65 = sb("w65" + tag, [P, PAIRS, nch, C + 1])
        first = sb("w65_first" + tag, [P, nch, C + 1])
        tmp = sb("rw_tmp" + tag, [P, PAIRS, T])
        th = sb("rw_th" + tag, [P, 2, T])
        ps = [ctx.enter_context(nc.psum_tensor(f"ps_rf{k}" + tag, [P, 512], F32)) for k in range(8)]
        vec_in = sem("rwf_in")
        tanh_wd, half_done, proj = sem("rwf_tanh"), sem("rwf_half"), sem("rwf_proj")
        th_done, dec_done, a_done = sem("rwf_th"), sem("rwf_decay"), sem("rwf_a")
        sq_in, sq_done, norm_mm, norm_max, norm_sqrt = (sem("rwf_kk"), sem("rwf_sq"), sem("rwf_norm"),
                                                        sem("rwf_max"), sem("rwf_sqrt"))
        dve, a_used, scanned = sem("rwf_dve"), sem("rwf_a_used"), sem("rwf_scanned")
        block = ctx.enter_context(nc.Block())

        @block.sync
        def _(sp):
            sp.dma_start(wa_up[:], a["wa_up"]).then_inc(vec_in, 16)
            sp.dma_start(vecs[:], a["rw_vecs"]).then_inc(vec_in, 16)

        @block.scalar
        def _(act):
            act.activation(f[0:64, 12, :], f[0:64, 12, :], ACT.Tanh).then_inc(tanh_wd, 1)
            act.wait_ge(half_done, 1)
            act.wait_ge(sq_in, 1)
            act.activation(tmp[:], b.kk[:, :, 0:T], ACT.Square).then_inc(sq_done, 1)
            for z in range(2):
                for c in range(PAIRS):
                    n = z * PAIRS + c
                    act.wait_ge(proj, n + 1)
                    act.activation(th[:, n % 2], ps[2 * (n % 2)][:, 0:T], ACT.Tanh, bias=half[:, z, c:c + 1],
                                   scale=0.5).then_inc(th_done, 1)
                    act.wait_ge(th_done, n + 1)
                    if z == 1:
                        act.wait_ge(scanned, c + 1)
                    act.activation(w65[:, c, :, 1:] if z == 0 else w65[:, c, :, 0:C],
                                   th[:, n % 2].rearrange("p (n t) -> p n t", t=C), ACT.Exp,
                                   bias=b.eps[:, 2:3], scale=-HALF_DECAY).then_inc(dec_done, 1)
                    act.activation(b.qa[:, z, c, 0:T], ps[2 * (n % 2) + 1][:, 0:T], ACT.Tanh,
                                   bias=half[:, 2 + z, c:c + 1], scale=0.5).then_inc(a_done, 1)
            act.wait_ge(norm_max, 1)
            act.activation(tmp[:], tmp[:], ACT.Sqrt).then_inc(norm_sqrt, 1)

        @block.tensor
        def _(pe):
            pe.wait_ge(vec_in, 32)
            pe.wait_ge(tanh_wd, 1)
            for n in range(2 * PAIRS):
                z, c = n // PAIRS, n % PAIRS
                if n >= 2:
                    pe.wait_ge(a_done, n - 1)
                pe.matmul(ps[2 * (n % 2)][:, 0:T], wa_up[0:64, z, c * P:(c + 1) * P], f[0:64, 12, :],
                          start=True, stop=True)
                pe.matmul(ps[2 * (n % 2) + 1][:, 0:T], wa_up[64:P, z, c * P:(c + 1) * P], f[64:P, 12, :],
                          start=True, stop=True).then_inc(proj, 1)
            pe.wait_ge(sq_done, 1)
            for c in range(PAIRS):
                mm = pe.matmul(ps[4 + c][:, 0:T], b.block_ones[:], tmp[:, c, :], start=True, stop=True)
            mm.then_inc(norm_mm, 1)

        @block.vector
        def _(v):
            link = Count(v, dve)
            v.wait_ge(vec_in, 32)
            link(v.tensor_scalar(half[:], vecs[:, 0:4, :], 0.5, None, ALU.mult))
            v.tensor_scalar(one_ka[:], vecs[:, 5, :], -1.0, 1.0, ALU.mult, ALU.add).then_inc(half_done, 1)
            v.wait_ge(half_done, 1)
            for c in range(PAIRS):
                m = v.tensor_scalar(b.kk[:, c, 0:T], f[:, 4 + c, :], vecs[:, 4, c:c + 1], None, ALU.mult)
            m.then_inc(sq_in, 1)
            link(v.memset(first[:], 0.0))
            link(v.memset(first[:, :, 0:1], 1.0))
            for z in range(2):
                slot = 0 if z == 0 else C
                if z == 1:
                    v.wait_ge(scanned, PAIRS)
                    v.wait_ge(dec_done, 2 * PAIRS)
                link(v.memset(w65[:, :, :, slot:slot + 1], 0.0))
                for c in range(PAIRS):
                    v.wait_ge(dec_done, z * PAIRS + c + 1)
                    w = w65[:, c].rearrange("p n t -> p (n t)")
                    g = b.G[:, z, c, 0:nch * (C + 1)]
                    if z:
                        w, g = w[:, ::-1], g[:, ::-1]
                    v.tensor_tensor_scan(out=g, data0=w, data1=first[:].rearrange("p n t -> p (n t)"), initial=0.0,
                                         op0=ALU.mult, op1=ALU.add).then_inc(scanned, 1)
            v.wait_ge(norm_mm, 1)
            v.wait_ge(sq_done, 1)
            for c in range(PAIRS):
                m = v.tensor_scalar(tmp[:, c, :], ps[4 + c][:, 0:T], 1e-24, None, ALU.max)
            m.then_inc(norm_max, 1)
            v.wait_ge(norm_sqrt, 1)
            link(v.reciprocal(tmp[:], tmp[:]))
            link(v.tensor_tensor(b.kk[:, :, 0:T], b.kk[:, :, 0:T], tmp[:], ALU.mult))
            for z in range(2):
                v.wait_ge(a_done, (z + 1) * PAIRS)
                qa, ke = b.qa[:, z, :, 0:T], b.ke[:, z, :, 0:T]
                link(v.tensor_scalar(qa, qa, 0.5, 0.5, ALU.mult, ALU.add))
                for c in range(PAIRS):
                    m = v.tensor_scalar(ke[:, c], qa[:, c], vecs[:, 5, c:c + 1], one_ka[:, c:c + 1], ALU.mult, ALU.add)
                link(m)
                link(v.tensor_tensor(ke, ke, f[:, 4:8, :], ALU.mult))
                link(v.tensor_tensor(qa, qa, b.kk[:, :, 0:T], ALU.mult))


def phase_rwkv_scan(nc, a, b, f, T, tag, need_out):
    nch = T // C
    with ExitStack() as ctx:
        sb = alloc(nc, ctx)

        def sem(name):
            return b.semaphore(nc, name + tag)

        def each(name, shape):
            return [sb(f"{name}{g}" + tag, shape) for g in range(2)]

        RW = 3 * C
        pr, qs, ks, vs = (each(n, [P, PAIRS, w]) for n, w in (("pr", RW), ("qs", C), ("ks", C), ("vs", C)))
        ginv = each("ginv", [P, PAIRS, C])
        lt, mt, at, bt, qt, kt, vv = (each(n, [P, PAIRS, C]) for n in ("lt", "mt", "at", "bt", "qt", "kt", "vv"))
        xx, rr, uu, st = (each(n, [P, PAIRS, C]) for n in ("xx", "rr", "uu", "st"))
        tt = each("tt", [P, PAIRS, 2, C])
        tm = each("tm", [P, PAIRS, C])
        psw = [[ctx.enter_context(nc.psum_tensor(f"ps_rs{g}{k}" + tag, [P, 2, 512], F32)) for k in range(2)]
               for g in range(2)]
        pe_names = ["Q", "K", "LV"] + [x + str(s) for s in LEVELS for x in "XY"] + ["R", "U"] + ["O"] * need_out + ["S"]
        dve_names = (["gi", "p", "q", "k"] + ["rho"] * need_out + ["tt_m", "tt"] + ["bt"] * need_out + ["mt"]
                     + ["at"] * need_out + ["t_m", "t"] + [x + str(s) for s in LEVELS for x in "xy"] + ["s1", "s2"])
        act_names = ["vs", "lt", "qt", "kt", "v", "r", "u"] + ["out"] * need_out
        pe_s = [Steps(sem(f"rws_pe{g}"), pe_names) for g in range(2)]
        dve_s = [Steps(sem(f"rws_dve{g}"), dve_names) for g in range(2)]
        act_s = [Steps(sem(f"rws_act{g}"), act_names) for g in range(2)]
        unit, state_in = sem("rws_unit"), sem("rws_state")
        turn = sem("rws_turn")
        block = ctx.enter_context(nc.Block())

        def start_of(i, g, stride, base=0):
            return i * stride + base if g == 0 else i * (-stride) + ((nch - 1) * stride + base)

        def mask(g, m, shape):
            ap = b.masks[:, g, m, :]
            for _ in shape[1:-1]:
                ap = ap.unsqueeze(1)
            return ap.to_broadcast(shape)

        def wide(g, k, lo):
            return psw[g][k][:, :, 0:2 * RW].rearrange("p b (m x) -> p b m x", x=RW)[:, :, :, lo:lo + C]

        def quad(t):
            return t[:].rearrange("p (b m) x -> p b m x", b=2)

        @block.scalar
        def _(act):
            for g in range(2):
                act_s[g].start(act)
                act.activation(pr[g][:, :, 2 * C:], b.unit[:].unsqueeze(1).to_broadcast([P, PAIRS, C]),
                               ACT.Copy).then_inc(unit, 1)
            with act.Fori(0, nch) as i:
                for g in range(2):
                    pe_s[g].wait_last(act, i)
                    act_s[g].mark(act.activation(vs[g][:], f[:, 8:12, bass.ds(start_of(i, g, C), C)], ACT.Copy))
                for g in range(2):
                    pe_s[g].wait(act, i, "Q")
                    dve_s[g].wait(act, i, "bt" if need_out else "tt_m")
                    act_s[g].mark(act.activation(quad(lt[g]), wide(g, 0, 0), ACT.Copy))
                    act_s[g].mark(act.activation(quad(qt[g]), wide(g, 0, 2 * C), ACT.Copy, scale=-1.0))
                for g in range(2):
                    pe_s[g].wait(act, i, "K")
                    dve_s[g].wait(act, i, "at" if need_out else "mt")
                    act_s[g].mark(act.activation(quad(kt[g]), wide(g, 1, 2 * C), ACT.Copy))
                for g in range(2):
                    pe_s[g].wait(act, i, "LV")
                    dve_s[g].wait(act, i, "t_m")
                    act_s[g].mark(act.activation(vv[g][:], psw[g][0][:, 0, :].rearrange(
                        "p (m x) -> p m x", m=PAIRS)[:, :, C:], ACT.Copy))
                for g in range(2):
                    pe_s[g].wait(act, i, "R")
                    act_s[g].mark(act.activation(rr[g][:], psw[g][0][:, 0, 0:PAIRS * C].rearrange(
                        "p (m x) -> p m x", m=PAIRS), ACT.Copy))
                for g in range(2):
                    pe_s[g].wait(act, i, "U")
                    act_s[g].mark(act.activation(uu[g][:], psw[g][1][:, 1, 0:PAIRS * C].rearrange(
                        "p (m x) -> p m x", m=PAIRS), ACT.Copy))
                if need_out:
                    for g in range(2):
                        pe_s[g].wait(act, i, "O")
                        act_s[g].mark(act.activation(b.rwo[:, g, :, bass.ds(start_of(i, g, C), C)],
                                                     psw[g][0][:, 0, 0:PAIRS * C].rearrange("p (m x) -> p m x", m=PAIRS),
                                                     ACT.Copy))

        @block.tensor
        def _(pe):
            for g in range(2):
                pe_s[g].start(pe)

            def heads():
                return ((m, h * C) for m in range(PAIRS) for h in range(2))

            pe.wait_ge(unit, 2)
            with pe.Fori(0, nch) as i:
                for k, (name, step, buf) in enumerate((("Q", "q", qs), ("K", "k", ks))):
                    for g in range(2):
                        if k == 0:
                            dve_s[g].wait(pe, i, "rho" if need_out else "k")
                            act_s[g].wait_last(pe, i)
                        pe.sem_inc(turn, 1)
                        for m, h in heads():
                            mm = pe.matmul(psw[g][k][h:h + C, m // 2, (m % 2) * RW:(m % 2 + 1) * RW],
                                           buf[g][h:h + C, m, :], pr[g][h:h + C, m, :], start=True, stop=True)
                        pe_s[g].mark(mm)
                for g in range(2):
                    dve_s[g].wait(pe, i, "bt" if need_out else "tt")
                    act_s[g].wait(pe, i, "qt")
                    pe.sem_inc(turn, 1)
                    for m, h in heads():
                        pe.matmul(psw[g][0][h:h + C, 0, m * 2 * C:m * 2 * C + C], pr[g][h:h + C, m, 0:C],
                                  qs[g][h:h + C, m, :], start=True, stop=True)
                        mm = pe.matmul(psw[g][0][h:h + C, 0, m * 2 * C + C:(m + 1) * 2 * C], vs[g][h:h + C, m, :],
                                       b.unit[h:h + C, :], start=True, stop=True)
                    pe_s[g].mark(mm)
                last = "t"
                for s in LEVELS:
                    for g in range(2):
                        dve_s[g].wait(pe, i, last)
                        pe.sem_inc(turn, 1)
                        for m, h in heads():
                            mm = pe.matmul(psw[g][0][h:h + C, 1, m * C:(m + 1) * C], lt[g][h:h + C, m, :],
                                           tt[g][h:h + C, m, 0, :], start=True, stop=True)
                        pe_s[g].mark(mm)
                    for g in range(2):
                        dve_s[g].wait(pe, i, f"x{s}")
                        if s == LEVELS[0]:
                            act_s[g].wait(pe, i, "kt")
                        pe.sem_inc(turn, 1)
                        for m, h in heads():
                            pe.matmul(psw[g][1][h:h + C, 0, m * 2 * C:m * 2 * C + C], tt[g][h:h + C, m, 1, :],
                                      xx[g][h:h + C, m, :], start=True, stop=True)
                            mm = pe.matmul(psw[g][1][h:h + C, 0, m * 2 * C + C:(m + 1) * 2 * C], xx[g][h:h + C, m, :],
                                           tt[g][h:h + C, m, 1, :], start=True, stop=True)
                        pe_s[g].mark(mm)
                    last = f"y{s}"
                for g in range(2):
                    act_s[g].wait(pe, i, "v")
                    pe.sem_inc(turn, 1)
                    for m, h in heads():
                        o = psw[g][0][h:h + C, 0, m * C:(m + 1) * C]
                        pe.matmul(o, pr[g][h:h + C, m, 0:C], st[g][h:h + C, m, :], start=True, stop=False)
                        mm = pe.matmul(o, mt[g][h:h + C, m, :], vv[g][h:h + C, m, :], start=False, stop=True)
                    pe_s[g].mark(mm)
                for g in range(2):
                    dve_s[g].wait(pe, i, last)
                    act_s[g].wait(pe, i, "r")
                    pe.sem_inc(turn, 1)
                    for m, h in heads():
                        mm = pe.matmul(psw[g][1][h:h + C, 1, m * C:(m + 1) * C], tt[g][h:h + C, m, 1, :],
                                       rr[g][h:h + C, m, :], start=True, stop=True)
                    pe_s[g].mark(mm)
                for g in range(2):
                    act_s[g].wait(pe, i, "u")
                    pe.sem_inc(turn, 1)
                    if need_out:
                        for m, h in heads():
                            o = psw[g][0][h:h + C, 0, m * C:(m + 1) * C]
                            pe.matmul(o, st[g][h:h + C, m, :], pr[g][h:h + C, m, C:2 * C], start=True, stop=False)
                            pe.matmul(o, vv[g][h:h + C, m, :], at[g][h:h + C, m, :], start=False, stop=False)
                            mm = pe.matmul(o, uu[g][h:h + C, m, :], bt[g][h:h + C, m, :], start=False, stop=True)
                        pe_s[g].mark(mm)
                    for m, h in heads():
                        o = psw[g][1][h:h + C, 1, m * C:(m + 1) * C]
                        pe.matmul(o, kt[g][h:h + C, m, :], vv[g][h:h + C, m, :], start=True, stop=False)
                        mm = pe.matmul(o, qt[g][h:h + C, m, :], uu[g][h:h + C, m, :], start=False, stop=True)
                    pe_s[g].mark(mm)

        @block.vector
        def _(v):
            for g in range(2):
                dve_s[g].start(v)
                if not need_out:
                    v.memset(pr[g][:, :, C:2 * C], 0.0).then_inc(state_in, 1)
                    v.memset(st[g][:], 0.0).then_inc(state_in, 1)
                else:
                    v.tensor_copy(st[g][:], b.state[:, g]).then_inc(state_in, 1)
            v.wait_ge(state_in, 2 if need_out else 4)
            small = [P, PAIRS, C]
            four = [P, 2, 2, C]
            with v.Fori(0, nch) as i:
                for g in range(2):
                    t0, g0 = start_of(i, g, C), start_of(i, g, C + 1)
                    cur = b.G[:, g, :, bass.ds(start_of(i, g, C + 1, 1 - g), C)]
                    prev = b.G[:, g, :, bass.ds(start_of(i, g, C + 1, g), C)]
                    if True:
                        pe_s[g].wait_last(v, i)
                        dve_s[g].wait_last(v, i)
                    dve_s[g].mark(v.reciprocal(ginv[g][:], cur))
                    dve_s[g].mark(v.tensor_tensor(pr[g][:, :, 0:C], b.kk[:, :, bass.ds(t0, C)], prev, ALU.mult))
                    dve_s[g].wait(v, i, "gi")
                    dve_s[g].mark(v.tensor_tensor(qs[g][:], b.qa[:, g, :, bass.ds(t0, C)], ginv[g][:], ALU.mult))
                    dve_s[g].mark(v.tensor_tensor(ks[g][:], b.ke[:, g, :, bass.ds(t0, C)], ginv[g][:], ALU.mult))
                    if need_out:
                        dve_s[g].mark(v.tensor_tensor(pr[g][:, :, C:2 * C], f[:, 0:4, bass.ds(t0, C)], cur, ALU.mult))
                for g in range(2):
                    pe_s[g].wait(v, i, "Q")
                    dve_s[g].mark(v.tensor_tensor(quad(tm[g]), wide(g, 0, 0), mask(g, M_NEG1_ST, four), ALU.mult))
                    dve_s[g].wait(v, i, "tt_m")
                    dve_s[g].mark(v.tensor_tensor(tt[g][:, :, 1, :], tm[g][:],
                                                  b.unit[:].unsqueeze(1).to_broadcast(small), ALU.add))
                    if need_out:
                        dve_s[g].mark(v.tensor_tensor(quad(bt[g]), wide(g, 0, C), mask(g, M_NEG_INCL, four), ALU.mult))
                for g in range(2):
                    pe_s[g].wait(v, i, "K")
                    dve_s[g].mark(v.tensor_tensor(quad(mt[g]), wide(g, 1, 0), mask(g, M_STRICT, four), ALU.mult))
                    if need_out:
                        dve_s[g].mark(v.tensor_tensor(quad(at[g]), wide(g, 1, C), mask(g, M_INCL, four), ALU.mult))
                for g in range(2):
                    pe_s[g].wait(v, i, "LV")
                    dve_s[g].wait(v, i, "tt")
                    dve_s[g].mark(v.tensor_tensor(tm[g][:], psw[g][0][:, 0, :].rearrange(
                        "p (m x) -> p m x", m=PAIRS)[:, :, 0:C], mask(g, M_NEG1_TS, small), ALU.mult))
                    dve_s[g].wait(v, i, "t_m")
                    dve_s[g].mark(v.tensor_tensor(tt[g][:, :, 0, :], tm[g][:],
                                                  b.unit[:].unsqueeze(1).to_broadcast(small), ALU.add))
                for n, s in enumerate(LEVELS):
                    for g in range(2):
                        pe_s[g].wait(v, i, f"X{s}")
                        dve_s[g].mark(v.tensor_tensor(xx[g][:], psw[g][0][:, 1, 0:PAIRS * C].rearrange(
                            "p (m x) -> p m x", m=PAIRS), mask(g, M_OFF + n, small), ALU.mult))
                    for g in range(2):
                        pe_s[g].wait(v, i, f"Y{s}")
                        dve_s[g].mark(v.tensor_tensor(tt[g][:].rearrange("p m k x -> p (m k x)"),
                                                      tt[g][:].rearrange("p m k x -> p (m k x)"),
                                                      psw[g][1][:, 0, :], ALU.subtract))
                for g in range(2):
                    pe_s[g].wait(v, i, "S")
                    dve_s[g].mark(v.tensor_tensor(tm[g][:], psw[g][1][:, 1, 0:PAIRS * C].rearrange(
                        "p (m x) -> p m x", m=PAIRS), st[g][:], ALU.add))
                    dve_s[g].wait(v, i, "s1")
                    dve_s[g].mark(v.tensor_tensor(
                        st[g][:], tm[g][:],
                        b.G[:, g, :, bass.ds(start_of(i, g, C + 1, C * (1 - g)), 1)].to_broadcast(small), ALU.mult))
            if not need_out:
                for g in range(2):
                    dve_s[g].wait_last(v, nch)
                    v.tensor_copy(b.state[:, g], st[g][:]).then_inc(state_in, 1)


def phase_rwkv_output(nc, a, b):
    f = b.fX
    with ExitStack() as ctx:
        sb = alloc(nc, ctx)

        def sem(name):
            return b.semaphore(nc, name)

        g_up = sb("g_up", [P, D_RWKV])
        vecs = sb("rwo_vecs", [P, 3, PAIRS])
        sq = sb("rwo_sq", [P, 2, PAIRS, TX])
        bonus = sb("rwo_bonus", [P, PAIRS, TX])
        gd = sb("rwo_gd", [P, TX])
        ps = [ctx.enter_context(nc.psum_tensor(f"ps_ro{k}", [P, TX], F32)) for k in range(8)]
        vec_in, tanh_done, gd_done = sem("rwo_in"), sem("rwo_tanh"), sem("rwo_gd_done")
        bonus_in, mean_mm, centred, squared = sem("rwo_bonus_in"), sem("rwo_mean"), sem("rwo_centred"), sem("rwo_squared")
        var_mm, rooted, gate_mm, evac, dve = (sem("rwo_var"), sem("rwo_root"), sem("rwo_gate"), sem("rwo_evac"),
                                              sem("rwo_dve"))
        block = ctx.enter_context(nc.Block())
        units = [(z, c) for z in range(2) for c in range(PAIRS)]

        @block.sync
        def _(sp):
            sp.dma_start(g_up[:], a["g_up"]).then_inc(vec_in, 16)
            sp.dma_start(vecs[:], a["rwo_vecs"]).then_inc(vec_in, 16)

        @block.scalar
        def _(act):
            act.activation(gd[:], f[:, 13, :], ACT.Tanh, scale=0.5).then_inc(tanh_done, 1)
            for n, (z, c) in enumerate(units):
                act.wait_ge(centred, n + 1)
                act.activation(sq[:, z, c], b.rwo[:, z, c], ACT.Square).then_inc(squared, 1)
            for n, (z, c) in enumerate(units):
                act.wait_ge(var_mm, n + 1)
                act.activation(sq[:, z, c], ps[n % 4][:], ACT.Sqrt, bias=b.eps[:, 1:2], scale=1.0 / C).then_inc(rooted, 1)

        @block.tensor
        def _(pe):
            for n, (z, c) in enumerate(units):
                if n >= 4:
                    pe.wait_ge(centred, n - 3)
                pe.matmul(ps[n % 4][:], b.block_ones[:], b.rwo[:, z, c], start=True, stop=True).then_inc(mean_mm, 1)
            for n, (z, c) in enumerate(units):
                pe.wait_ge(squared, n + 1)
                if n < 4:
                    pe.wait_ge(centred, n + 5)
                else:
                    pe.wait_ge(rooted, n - 3)
                pe.matmul(ps[n % 4][:], b.block_ones[:], sq[:, z, c], start=True, stop=True).then_inc(var_mm, 1)
            pe.wait_ge(bonus_in, 1)
            for c in range(PAIRS):
                mm = pe.matmul(ps[4 + c][:], b.block_ones[:], bonus[:, c], start=True, stop=True)
            mm.then_inc(gate_mm, 1)
            pe.wait_ge(vec_in, 32)
            pe.wait_ge(gd_done, 1)
            pe.wait_ge(evac, 1)
            for c in range(PAIRS):
                mm = pe.matmul(ps[4 + c][:], g_up[:, c * P:(c + 1) * P], gd[:], start=True, stop=True)
            mm.then_inc(gate_mm, 1)

        @block.vector
        def _(v):
            link = Count(v, dve)
            for n, (z, c) in enumerate(units):
                v.wait_ge(mean_mm, n + 1)
                v.scalar_tensor_tensor(out=b.rwo[:, z, c], in0=ps[n % 4][:], scalar=-1.0 / C, in1=b.rwo[:, z, c],
                                       op0=ALU.mult, op1=ALU.add).then_inc(centred, 1)
            link(v.tensor_tensor(bonus[:], b.ke[:, 0], b.ke[:, 1], ALU.add))
            link(v.tensor_tensor(bonus[:], bonus[:], f[:, 0:4, :], ALU.mult))
            v.wait_ge(vec_in, 32)
            for c in range(PAIRS):
                m = v.tensor_scalar(bonus[:, c], bonus[:, c], vecs[:, 0, c:c + 1], None, ALU.mult)
            m.then_inc(bonus_in, 1)
            v.wait_ge(tanh_done, 1)
            v.tensor_scalar(gd[:], gd[:], 0.5, 0.5, ALU.mult, ALU.add).then_inc(gd_done, 1)
            v.wait_ge(rooted, 8)
            link(v.reciprocal(sq[:], sq[:]))
            link(v.tensor_tensor(sq[:], sq[:], b.rwo[:], ALU.mult))
            link(v.tensor_tensor(b.ya[:], sq[:, 0], sq[:, 1], ALU.add))
            link(v.tensor_scalar(vecs[:, 2, :], vecs[:, 2, :], 2.0, None, ALU.mult))
            for c in range(PAIRS):
                m = v.tensor_scalar(b.ya[:, c], b.ya[:, c], vecs[:, 1, c:c + 1], vecs[:, 2, c:c + 1], ALU.mult, ALU.add)
            link(m)
            v.wait_ge(gate_mm, 1)
            for c in range(PAIRS):
                m = v.tensor_tensor(bonus[:, c], ps[4 + c][:], f[:, 8 + c, :], ALU.mult)
            m.then_inc(evac, 1)
            v.wait_ge(evac, 1)
            link(v.tensor_tensor(b.ya[:], b.ya[:], bonus[:], ALU.add))
            v.wait_ge(gate_mm, 2)
            for c in range(PAIRS):
                m = v.tensor_tensor(b.ya[:, c], ps[4 + c][:], b.ya[:, c], ALU.mult)
            link(m)


NEG_M, INTER, FLOOR = 0, 1, 2
COL_C, COL_W = 0, 1
LN_MAX = 85.0
UNITS = 2 * MH


def phase_mlstm_gates(nc, a, b):
    T = TX + TC
    NCH = T // MC
    with ExitStack() as ctx:
        sb = alloc(nc, ctx)

        def sem(name):
            return b.semaphore(nc, name)

        sg = sb("gate_scan", [GROWS, 2, T])
        bias = sb("gate_bias", [GROWS, 2])
        resets = sb("gate_resets", [GROWS, 2, NCH, MC])
        bsum = sb("gate_b", [GROWS, T])
        m = sb("gate_m", [GROWS, T])
        mp = sb("gate_mprev", [GROWS, NCH])
        c2 = sb("gate_c2", [GROWS, T])
        rows = sb("gate_rows", [GROWS, 5, T])
        ident = sb("gate_ident", [GROWS, GROWS])
        ps_t = ctx.enter_context(nc.psum_tensor("ps_gt", [P, 512], F32))
        small_in, dve, act_done, t_done = sem("mlg_in"), sem("mlg_dve"), sem("mlg_act"), sem("mlg_t")
        want = [sem(f"mlg_want{k}") for k in range(3)]
        rows_done = sem("mlg_rows")
        block = ctx.enter_context(nc.Block())
        f, ig = sg[:, 1, :], sg[:, 0, :]

        @block.sync
        def _(sp):
            sp.dma_start(bias[:], a["gate_bias"]).then_inc(small_in, 16)
            sp.dma_start(resets[:], a["gate_resets"]).then_inc(small_in, 16)
            sp.dma_start(ident[:], a["ident"][0:GROWS, 0:GROWS]).then_inc(small_in, 16)
            sp.dma_start(b.select[:], a["select"]).then_inc(small_in, 16)
            sp.dma_start(b.m_mask[:], a["m_mask"]).then_inc(small_in, 16)

        @block.scalar
        def _(act):
            act.wait_ge(want[0], 1)
            act.activation(bsum[:], f, ACT.Abs).then_inc(act_done, 1)
            act.wait_ge(act_done, 1)
            act.activation(bsum[:], bsum[:], ACT.Exp, scale=-1.0).then_inc(act_done, 1)
            act.wait_ge(act_done, 2)
            act.activation(bsum[:], bsum[:], ACT.Ln, bias=1.0).then_inc(act_done, 1)
            act.wait_ge(want[1], 1)
            act.activation(rows[:, INTER], rows[:, INTER], ACT.Exp).then_inc(act_done, 1)
            act.activation(rows[:, FLOOR], rows[:, FLOOR], ACT.Exp, scale=-1.0).then_inc(act_done, 1)
            act.activation(rows[:, 4], rows[:, 4], ACT.Exp).then_inc(act_done, 1)

        @block.vector
        def _(v):
            link = Count(v, dve)
            for lo, hi, rev in ((0, 32, False), (32, GROWS, True)):
                for dst, src in (((0, TC), (TX, T)), ((TC, T), (0, TX))):
                    s = b.gates[lo:hi, :, src[0]:src[1]]
                    m_ = v.tensor_copy(sg[lo:hi, :, dst[0]:dst[1]], s[:, :, ::-1] if rev else s)
            link(m_)
            v.wait_ge(small_in, 80)
            link(v.tensor_scalar(ig, ig, bias[:, 0:1], None, ALU.add))
            v.tensor_scalar(f, f, bias[:, 1:2], None, ALU.add).then_inc(want[0], 1)
            v.wait_ge(act_done, 3)
            link(v.scalar_tensor_tensor(out=f, in0=f, scalar=0.0, in1=bsum[:], op0=ALU.min, op1=ALU.subtract))
            link(v.tensor_tensor_scan(out=m[:], data0=f, data1=ig, initial=0.0, op0=ALU.add, op1=ALU.max))
            link(v.tensor_tensor_scan(out=bsum[:], data0=resets[:, 0].rearrange("p n t -> p (n t)"), data1=f,
                                      initial=0.0, op0=ALU.mult, op1=ALU.add))
            link(v.tensor_tensor(rows[:, 3], ig, bsum[:], ALU.subtract))
            link(v.memset(mp[:, 0:1], 0.0))
            link(v.tensor_copy(mp[:, 1:], m[:, MC - 1:T - 1:MC]))
            link(v.tensor_copy(c2[:], rows[:, 3]))
            link(v.tensor_tensor(c2[:, 0:T:MC], c2[:, 0:T:MC], mp[:], ALU.max))
            link(v.tensor_tensor_scan(out=rows[:, NEG_M], data0=resets[:, 1].rearrange("p n t -> p (n t)"),
                                      data1=c2[:], initial=0.0, op0=ALU.add, op1=ALU.max))
            big = [GROWS, NCH, MC]

            def chunks(ap):
                return ap.rearrange("p (n t) -> p n t", t=MC)

            link(v.tensor_tensor(chunks(rows[:, INTER]), mp[:].unsqueeze(2).to_broadcast(big),
                                 chunks(rows[:, NEG_M]), ALU.subtract))
            link(v.tensor_tensor(chunks(rows[:, 4]), chunks(rows[:, 3]),
                                 chunks(rows[:, NEG_M])[:, :, MC - 1:MC].to_broadcast(big), ALU.subtract))
            link(v.tensor_scalar(rows[:, FLOOR], m[:], -LN_MAX, None, ALU.max))
            v.tensor_scalar(rows[:, NEG_M], rows[:, NEG_M], -1.0, None, ALU.mult).then_inc(want[1], 1)
            v.wait_ge(want[1], 1)
            v.wait_ge(act_done, 6)
            for lo, hi in ((0, 32), (32, GROWS)):
                for k in range(5):
                    src = chunks(rows[lo:hi, k])
                    dst = (b.g_rows[lo:hi, k] if k < 3 else b.g_turn[lo:hi, k - 3])
                    m_ = v.tensor_copy(chunks(dst), src[:, :, ::-1] if lo else src)
            m_.then_inc(rows_done, 1)
            v.wait_ge(t_done, 1)
            v.tensor_copy(b.g_cols[:].rearrange("p n k r -> p (n k r)"),
                          ps_t[:, 0:NCH * 2 * GROWS]).then_inc(want[2], 1)

        @block.tensor
        def _(pe):
            pe.wait_ge(rows_done, 1)
            for n in range(NCH):
                for k in range(2):
                    o = (n * 2 + k) * GROWS
                    t = pe.transpose(ps_t[:, o:o + GROWS], b.g_turn[:, k, n * MC:(n + 1) * MC], ident[:])
            t.then_inc(t_done, 1)


def phase_mlstm(nc, a, b, q, T, v0, n0, tag, need_out):
    nch = T // MC
    with ExitStack() as ctx:
        sb = alloc(nc, ctx)

        def sem(name):
            return b.semaphore(nc, name + tag)

        kz = sb("kz" + tag, [P, 2, MH, MC])
        qc = sb("qc" + tag, [P, 2, MH // 2, MC])
        vc = sb("vc" + tag, [P, 2, MH, DV + 1])
        ktw = sb("ktw" + tag, [P, 2, P])
        pw = sb("pw" + tag, [P, 2, MC])
        qa = sb("mqa" + tag, [P, 2, MC])
        ab = sb("mab" + tag, [P, 2, MC])
        ps_b, ps_s, ps_n, ps_c = ([ctx.enter_context(nc.psum_tensor(f"ps_{n}{k}" + tag, [P, 512], F32))
                                   for k in range(2)] for n in ("mb", "ms", "mn", "mc"))

        def pipelined(first, second):
            names = []
            for u in range(UNITS + 1):
                if u < UNITS:
                    names += [f"{x}{u}" for x in first]
                if u:
                    names += [f"{x}{u - 1}" for x in second]
            return names

        pool_names = [x for z in range(2) for x in [f"k{z}0", f"k{z}1"] + [f"q{z}"] * need_out + [f"v{z}"]]
        pe_names = pipelined(["S"], ["N"])
        if need_out:
            act_names = pipelined(["kt", "e"], ["ab"])
            dve_names = []
            for u in range(UNITS + 1):
                dve_names += [f"m{u}", f"qa{u}"] * (u < UNITS)
                dve_names += [f"{x}{u - 1}" for x in ("mx", "rc", "h", "c")] * (u > 0)
                dve_names += [f"P{u}"] * (u < UNITS)
        else:
            act_names = [f"kt{u}" for u in range(UNITS)]
            dve_names = [f"c{u}" for u in range(UNITS)]
        pool_s, pe_s, act_s, dve_s = (Steps(sem(n), names) for n, names in (
            ("mls_pool", pool_names), ("mls_pe", pe_names), ("mls_act", act_names), ("mls_dve", dve_names)))
        zeroed, state_in = sem("mls_zero"), sem("mls_state")
        block = ctx.enter_context(nc.Block())
        units = [(u, u // MH, u % MH) for u in range(UNITS)]

        def start_of(i, z):
            return i * MC if z == 0 else i * (-MC) + (nch - 1) * MC

        def chunk_of(i, z):
            return i if z == 0 else i * (-1) + (nch - 1)

        @block.gpsimd
        def _(g):
            pool_s.start(g)
            g.memset(kz[:], 0.0).then_inc(zeroed, 1)
            g.wait_ge(zeroed, 1)
            with g.Fori(0, nch) as i:
                pe_s.wait_last(g, i)
                dve_s.wait_last(g, i)
                for z in range(2):
                    t0 = start_of(i, z)
                    for par in range(2):
                        lo = par * DQK
                        pool_s.mark(g.tensor_copy(kz[lo:lo + DQK, z, par::2, :], q[lo:lo + DQK, 2:4, bass.ds(t0, MC)]))
                        pool_s.wait(g, i, f"k{z}{par}")
                    if need_out:
                        pool_s.mark(g.tensor_copy(qc[:, z], q[:, 0:2, bass.ds(t0, MC)]))
                    pool_s.mark(g.tensor_copy(vc[:, z], b.vM[:, bass.ds(chunk_of(i, z) + v0, 1), :, :].rearrange(
                        "p n h v -> p (n h) v")))
                    pool_s.wait(g, i, f"v{z}")

        @block.tensor
        def _(pe):
            pe_s.start(pe)
            with pe.Fori(0, nch) as i:
                for u, z, h in units + [(UNITS, 0, 0)]:
                    k = u % 2
                    if u < UNITS:
                        if u == 0:
                            pool_s.wait(pe, i, "v1")
                        if u >= 2:
                            dve_s.wait(pe, i, f"c{u - 2}")
                        rows = b.g_rows[:, 1 - need_out:(3 if need_out else 2), bass.ds(i * MC + n0 * MC, MC)]
                        if need_out:
                            pe.matmul(ps_s[k][:, 0:MC], kz[:, z, h, :], qc[:, z, h // 2, :], start=True, stop=True)
                        pe.transpose(ps_s[k][:, MC:2 * MC], kz[:, z, h, :], b.ident[:])
                        pe_s.mark(pe.matmul(ps_b[k][:, (0 if need_out else MC):(3 if need_out else 2) * MC],
                                            b.select[:, u, :], rows, start=True, stop=True))
                    if u:
                        w, zw, hw = units[u - 1]
                        k = w % 2
                        if need_out:
                            dve_s.wait(pe, i, f"P{w}")
                            pe.matmul(ps_n[k][:, 0:MC], vc[:, zw, hw, 0:DV], pw[:, k], start=True, stop=False)
                            pe.matmul(ps_n[k][:, 0:MC], b.mC[:, w, 0:DV], qa[:, k], start=False, stop=True)
                            pe.matmul(ps_n[k][:, MC:2 * MC], b.ones[:], pw[:, k], start=True, stop=False)
                            pe.matmul(ps_n[k][:, MC:2 * MC], b.mC[:, w, DV:DV + 1].to_broadcast([P, P]), qa[:, k],
                                      start=False, stop=True)
                        act_s.wait(pe, i, f"kt{w}")
                        pe_s.mark(pe.matmul(ps_c[k][:, 0:DV + 1], ktw[:, k], vc[:, zw, hw, :], start=True, stop=True))

        @block.scalar
        def _(act):
            act_s.start(act)
            with act.Fori(0, nch) as i:
                for u, z, h in units + [(UNITS, 0, 0)]:
                    k = u % 2
                    if u < UNITS:
                        pe_s.wait(act, i, f"S{u}")
                        row = h + 32 * z
                        act_s.mark(act.activation(ktw[:, k], ps_s[k][:, MC:2 * MC], ACT.Copy,
                                                  scale=b.g_cols[:, bass.ds(i + n0, 1), COL_W, row]))
                        if need_out:
                            dve_s.wait(act, i, f"m{u}")
                            act_s.mark(act.activation(pw[:, k], pw[:, k], ACT.Exp))
                    if u and need_out:
                        k = (u - 1) % 2
                        pe_s.wait(act, i, f"N{u - 1}")
                        act_s.mark(act.activation(ab[:, k], ps_n[k][:, MC:2 * MC], ACT.Abs))

        @block.vector
        def _(v):
            dve_s.start(v)
            if not need_out:
                v.memset(b.mC[:], 0.0).then_inc(state_in, 1)
                v.wait_ge(state_in, 1)
            with v.Fori(0, nch) as i:
                for u, z, h in units + [(UNITS, 0, 0)]:
                    k = u % 2
                    if u < UNITS and need_out:
                        row = h + 32 * z
                        pe_s.wait(v, i, f"S{u}")
                        dve_s.mark(v.scalar_tensor_tensor(out=pw[:, k], in0=ps_b[k][:, 0:MC],
                                                          scalar=b.g_cols[:, bass.ds(i + n0, 1), COL_C, row],
                                                          in1=b.m_mask[:, z], op0=ALU.add, op1=ALU.min))
                        dve_s.mark(v.tensor_tensor(qa[:, k], ps_b[k][:, MC:2 * MC], qc[:, z, h // 2, :], ALU.mult))
                    if u:
                        w, zw, hw = units[u - 1]
                        kw = w % 2
                        pe_s.wait(v, i, f"N{w}")
                        end = MC + (MC - 1 if zw == 0 else 0)
                        if need_out:
                            act_s.wait(v, i, f"ab{w}")
                            dve_s.mark(v.tensor_tensor(ab[:, kw], ab[:, kw], ps_b[kw][:, 2 * MC:3 * MC], ALU.max))
                            dve_s.wait(v, i, f"mx{w}")
                            dve_s.mark(v.reciprocal(ab[:, kw], ab[:, kw]))
                            dve_s.wait(v, i, f"rc{w}")
                            dve_s.mark(v.tensor_tensor(b.mh[:, zw, hw, bass.ds(start_of(i, zw), MC)],
                                                       ps_n[kw][:, 0:MC], ab[:, kw], ALU.mult))
                        dve_s.mark(v.scalar_tensor_tensor(out=b.mC[:, w], in0=b.mC[:, w],
                                                          scalar=ps_b[kw][:, end:end + 1],
                                                          in1=ps_c[kw][:, 0:DV + 1], op0=ALU.mult, op1=ALU.add))
                    if u < UNITS and need_out:
                        act_s.wait(v, i, f"e{u}")
                        dve_s.mark(v.tensor_tensor(pw[:, k], ps_s[k][:, 0:MC], pw[:, k], ALU.mult))


def phase_mlstm_output(nc, a, b):
    with ExitStack() as ctx:
        sb = alloc(nc, ctx)

        def sem(name):
            return b.semaphore(nc, name)

        ng = sb("mlstm_g", [P, MH])
        sq = sb("mlo_sq", [P, 2, MH, TX])
        ps = [ctx.enter_context(nc.psum_tensor(f"ps_mo{k}", [P, TX], F32)) for k in range(8)]
        small_in, squared, mm, rooted, dve = sem("mlo_in"), sem("mlo_sq"), sem("mlo_mm"), sem("mlo_root"), sem("mlo_dve")
        block = ctx.enter_context(nc.Block())
        units = [(z, h) for z in range(2) for h in range(MH)]

        @block.sync
        def _(sp):
            sp.dma_start(ng[:], a["mlstm_g"]).then_inc(small_in, 16)

        @block.scalar
        def _(act):
            for z, h in units:
                act.activation(sq[:, z, h], b.mh[:, z, h], ACT.Square).then_inc(squared, 1)
            for n, (z, h) in enumerate(units):
                act.wait_ge(mm, n + 1)
                act.activation(sq[:, z, h], ps[n][:], ACT.Sqrt, bias=b.eps[:, 0:1], scale=1.0 / DV).then_inc(rooted, 1)

        @block.tensor
        def _(pe):
            for n, (z, h) in enumerate(units):
                pe.wait_ge(squared, n + 1)
                pe.matmul(ps[n][:], b.ones[:], sq[:, z, h], start=True, stop=True).then_inc(mm, 1)

        @block.vector
        def _(v):
            link = Count(v, dve)
            v.wait_ge(small_in, 16)
            v.wait_ge(rooted, 8)
            link(v.reciprocal(sq[:], sq[:]))
            link(v.tensor_tensor(sq[:], sq[:], b.mh[:], ALU.mult))
            link(v.tensor_tensor(sq[:, 0], sq[:, 0], sq[:, 1], ALU.add))
            for h in range(MH):
                v.tensor_scalar(b.yb[:, h, :].rearrange("p (r w) -> p w r", w=GRID_W),
                                sq[:, 0, h].rearrange("p (w r) -> p w r", r=ROWS), ng[:, h:h + 1], None,
                                ALU.mult).then_inc(dve, 1)


def phase_merge(nc, a, b, h_dram):
    with ExitStack() as ctx:
        sb = alloc(nc, ctx)

        def sem(name):
            return b.semaphore(nc, name)

        h = sb("mg_h", [P, KT, TX])
        x = sb("mg_x", [P, KT, TX])
        wo = sb("mg_wo", [P, MH, KT, P])
        ring = sb("mg_ring", [P, 2, 3, KT, P])
        wout = sb("mg_wout", [P, 2, KT, P])
        merged = sb("merged", [P, KT, TX])
        sg = sb("mg_sg", [P, 4, TX])
        sq = sb("mg_sq", [P, KT, TX])
        rs = sb("mg_rs", [P, TX])
        g2 = sb("mg_g2", [P, KT])
        gt = sb("mg_gt", [P, KT])
        ps = [ctx.enter_context(nc.psum_tensor(f"ps_mg{k}", [P, TX], F32)) for k in range(8)]
        h_in, x_in, g_in, o_in = sem("mg_h_in"), sem("mg_x_in"), sem("mg_g_in"), sem("mg_o_in")
        ring_in = [sem(f"mg_ring{k}") for k in range(2)]
        out_in = [sem(f"mg_out{k}") for k in range(2)]
        o_mm, o_tanh = sem("mg_o_mm"), sem("mg_o_tanh")
        m_mm = [sem(f"mg_m_mm{k}") for k in range(2)]
        m_tanh = [sem(f"mg_m_tanh{k}") for k in range(2)]
        m_used = [sem(f"mg_m_used{k}") for k in range(2)]
        w_mm = [sem(f"mg_w_mm{k}") for k in range(2)]
        x_done = [sem(f"mg_x_done{k}") for k in range(2)]
        squared, sum_mm, rooted, dve, pair = sem("mg_sq"), sem("mg_sum"), sem("mg_root"), sem("mg_dve"), sem("mg_pair")
        yb_done = sem("mg_yb")
        block = ctx.enter_context(nc.Block())
        half = KT // 2

        @block.sync
        def _(sp):
            sp.dma_start(h[:], h_dram).then_inc(h_in, 16)
            sp.dma_start(wo[:], a["w_o"]).then_inc(o_in, 16)
            for k in range(2):
                sp.dma_start(ring[:, k], a["w_merge"][k]).then_inc(ring_in[k], 16)
            sp.dma_start(g2[:], a["norm2_g"]).then_inc(g_in, 16)
            sp.dma_start(x[:], a["xT"]).then_inc(x_in, 16)
            with sp.Fori(1, half) as i:
                for k in range(2):
                    sp.wait_ge(m_mm[k], i)
                    sp.dma_start(ring[:, k], a["w_merge"][i * 2 + k]).then_inc(ring_in[k], 16)
            for k in range(2):
                sp.dma_start(wout[:, k], a["w_out"][k]).then_inc(out_in[k], 16)
            with sp.Fori(1, half) as i:
                for k in range(2):
                    sp.wait_ge(w_mm[k], i)
                    sp.dma_start(wout[:, k], a["w_out"][i * 2 + k]).then_inc(out_in[k], 16)

        @block.tensor
        def _(pe):
            pe.wait_ge(h_in, 16)
            pe.wait_ge(o_in, 16)
            for n in range(MH):
                for j in range(KT):
                    mm = pe.matmul(ps[n][:], wo[:, n, j, :], h[:, j, :], start=(j == 0), stop=(j == KT - 1))
                mm.then_inc(o_mm, 1)
            pe.wait_ge(yb_done, 1)
            with pe.Fori(0, half) as i:
                for k in range(2):
                    pe.wait_ge(ring_in[k], i * 16 + 16)
                    pe.wait_ge(m_used[k], i + 1)
                    for n in range(2):
                        for j in range(KT):
                            pe.matmul(ps[4 * k + n][:], ring[:, k, n, j, :], h[:, j, :],
                                      start=(j == 0), stop=(j == KT - 1))
                    for n, y in enumerate((b.ya, b.yb)):
                        for j in range(4):
                            mm = pe.matmul(ps[4 * k + 2 + n][:], ring[:, k, 2, 4 * n + j, :], y[:, j, :],
                                           start=(j == 0), stop=(j == 3))
                    mm.then_inc(m_mm[k], 1)
            for k in range(2):
                pe.wait_ge(m_used[k], half + 1)
            with pe.Fori(0, half) as i:
                for k in range(2):
                    pe.wait_ge(out_in[k], i * 16 + 16)
                    pe.wait_ge(x_done[k], i + 1)
                    for j in range(KT):
                        mm = pe.matmul(ps[4 * k][:], wout[:, k, j, :], merged[:, j, :], start=(j == 0), stop=(j == KT - 1))
                    mm.then_inc(w_mm[k], 1)
            for j in range(KT):
                pe.wait_ge(squared, j + 1)
                mm = pe.matmul(ps[1][:], b.ones[:], sq[:, j, :], start=(j == 0), stop=(j == KT - 1))
            mm.then_inc(sum_mm, 1)

        @block.scalar
        def _(act):
            for n in range(MH):
                act.wait_ge(o_mm, n + 1)
                act.activation(sg[:, n], ps[n][:], ACT.Tanh, scale=0.5).then_inc(o_tanh, 1)
            act.wait_ge(yb_done, 1)
            with act.Fori(0, half) as i:
                for k in range(2):
                    act.wait_ge(m_mm[k], i + 1)
                    act.wait_ge(m_used[k], i + 1)
                    for n in range(2):
                        m = act.activation(sg[:, 2 * k + n], ps[4 * k + n][:], ACT.Tanh, scale=0.5)
                    m.then_inc(m_tanh[k], 1)
            for j in range(KT):
                act.wait_ge(x_done[j % 2], j // 2 + 2)
                act.activation(sq[:, j], b.x1[:, j], ACT.Square).then_inc(squared, 1)
            act.wait_ge(sum_mm, 1)
            act.activation(rs[:], ps[1][:], ACT.Sqrt, bias=b.eps[:, 0:1], scale=1.0 / D).then_inc(rooted, 1)

        @block.vector
        def _(v):
            link = Count(v, dve)
            for k in range(2):
                v.sem_inc(m_used[k], 1)
                v.sem_inc(x_done[k], 1)
            for n in range(MH):
                v.wait_ge(o_tanh, n + 1)
                m = v.scalar_tensor_tensor(out=b.yb[:, n], in0=sg[:, n], scalar=1.0, in1=b.yb[:, n],
                                           op0=ALU.add, op1=ALU.mult)
            link(m)
            v.tensor_scalar(b.yb[:], b.yb[:], 0.5, None, ALU.mult).then_inc(yb_done, 1)
            v.wait_ge(yb_done, 1)
            link(v.tensor_scalar(gt[:], b.mod[:, 2 * KT:3 * KT, 0], 0.5, None, ALU.mult))
            with v.Fori(0, half) as i:
                for k in range(2):
                    v.wait_ge(m_tanh[k], i + 1)
                    for n in range(2):
                        m = v.scalar_tensor_tensor(out=sg[:, 2 * k + n], in0=sg[:, 2 * k + n], scalar=1.0,
                                                   in1=ps[4 * k + 2 + n][:], op0=ALU.add, op1=ALU.mult)
                    m.then_inc(pair, 1)
                    v.wait_ge(pair, i * 2 + k + 1)
                    v.tensor_tensor(merged[:, bass.ds(i * 2 + k, 1), :], sg[:, 2 * k:2 * k + 1], sg[:, 2 * k + 1:2 * k + 2],
                                    ALU.add).then_inc(m_used[k], 1)
            v.wait_ge(x_in, 16)
            with v.Fori(0, half) as i:
                for k in range(2):
                    v.wait_ge(w_mm[k], i + 1)
                    t = i * 2 + k
                    v.scalar_tensor_tensor(out=b.x1[:, bass.ds(t, 1), :], in0=ps[4 * k][:].unsqueeze(1),
                                           scalar=gt[:, bass.ds(t, 1)], in1=x[:, bass.ds(t, 1), :],
                                           op0=ALU.mult, op1=ALU.add).then_inc(x_done[k], 1)
            for k in range(2):
                v.wait_ge(x_done[k], half + 1)
            v.wait_ge(g_in, 16)
            link(v.scalar_tensor_tensor(out=g2[:], in0=b.mod[:, 4 * KT:5 * KT, 0], scalar=1.0, in1=g2[:],
                                        op0=ALU.add, op1=ALU.mult))
            v.wait_ge(rooted, 1)
            link(v.reciprocal(rs[:], rs[:]))
            for j in range(KT):
                link(v.scalar_tensor_tensor(out=b.h2[:, j], in0=b.x1[:, j], scalar=g2[:, j:j + 1], in1=rs[:],
                                            op0=ALU.mult, op1=ALU.mult))
                link(v.tensor_scalar(b.h2[:, j], b.h2[:, j], b.mod[:, 3 * KT + j, 0:1], None, ALU.add))


TT = TX // P
LOW = -3.0e38


def phase_route(nc, a, b):
    with ExitStack() as ctx:
        sb = alloc(nc, ctx)

        def sem(name):
            return b.semaphore(nc, name)

        keys = sb("keys", [P, 2 * PH, NK])
        ring = sb("wq_ring", [P, 2, KT, P])
        qT = sb("q_T", [P, 2, TX])
        S = sb("scores", [P, 2, 2, TT, NK])
        left = sb("scores_left", [P, TT, 2, NK])
        top = sb("top", [P, TT, 2, TOPK])
        ix = sb("top_ix", [P, TT, 2, TOPK], U32)
        cand = sb("cand", [P, TT, TOPK, TOPK])
        cleft = sb("cand_left", [P, TT, TOPK * TOPK])
        ctop = sb("cand_top", [P, TT, TOPK])
        cix = sb("cand_top_ix", [P, TT, TOPK], U32)
        ps_q = [ctx.enter_context(nc.psum_tensor(f"ps_q{k}", [P, TX], F32)) for k in range(2)]
        ps_s = [ctx.enter_context(nc.psum_tensor(f"ps_sc{k}", [P, TT, NK], F32)) for k in range(2)]
        keys_in = sem("rt_keys")
        ring_in = [sem(f"rt_ring{k}") for k in range(2)]
        q_mm = [sem(f"rt_q_mm{k}") for k in range(2)]
        q_out = [sem(f"rt_q_out{k}") for k in range(2)]
        s_mm = [sem(f"rt_s_mm{k}") for k in range(2)]
        s_out = [sem(f"rt_s_out{k}") for k in range(2)]
        s_free = [sem(f"rt_s_free{k}") for k in range(2)]
        groups = ("max1", "ix1", "left", "max2", "ix2", "cand", "cmax1", "cix1", "cleft", "cmax2", "cix2", "keep")
        dve_s = Steps(sem("rt_dve"), [f"{x}{hh}" for hh in range(2) for x in groups])
        turn = sem("rt_turn")
        block = ctx.enter_context(nc.Block())

        @block.sync
        def _(sp):
            for k in range(2):
                sp.dma_start(ring[:, k], a["w_q"][k]).then_inc(ring_in[k], 16)
            sp.dma_start(keys[:], a["keys"]).then_inc(keys_in, 16)
            with sp.Fori(1, PH) as i:
                for k in range(2):
                    sp.wait_ge(q_mm[k], i)
                    sp.dma_start(ring[:, k], a["w_q"][i * 2 + k]).then_inc(ring_in[k], 16)

        @block.tensor
        def _(pe):
            pe.wait_ge(keys_in, 16)
            with pe.Fori(0, PH) as i:
                for k in range(2):
                    pe.wait_ge(ring_in[k], i * 16 + 16)
                    pe.wait_ge(q_out[k], i + 1)
                    for j in range(KT):
                        mm = pe.matmul(ps_q[k][:], ring[:, k, j, :], b.h2[:, j, :], start=(j == 0), stop=(j == KT - 1))
                    mm.then_inc(q_mm[k], 1)
                for k in range(2):
                    pe.wait_ge(q_out[k], i + 2)
                    pe.wait_ge(s_out[k], i + 1)
                    for t in range(TT):
                        mm = pe.matmul(ps_s[k][:, t, :], qT[:, k, t * P:(t + 1) * P],
                                       keys[:, bass.ds(i * 2 + k, 1), :].rearrange("p o n -> p (o n)"),
                                       start=True, stop=True)
                    mm.then_inc(s_mm[k], 1)

        @block.scalar
        def _(act):
            for k in range(2):
                act.sem_inc(q_out[k], 1)
                act.sem_inc(s_out[k], 1)
            with act.Fori(0, PH // 2) as i:
                for hh in range(2):
                    for k in range(2):
                        act.wait_ge(q_mm[k], i * 2 + (hh + 1))
                        act.activation(qT[:, k], ps_q[k][:], ACT.Copy).then_inc(q_out[k], 1)
                    act.wait_ge(s_free[hh], i + 1)
                    for k in range(2):
                        act.wait_ge(s_mm[k], i * 2 + (hh + 1))
                        act.activation(S[:, hh, k], ps_s[k][:], ACT.Copy).then_inc(s_out[k], 1)

        @block.vector
        def _(v):
            dve_s.start(v)
            for hh in range(2):
                v.sem_inc(s_free[hh], 1)
            both = [(t, p) for t in range(TT) for p in range(2)]

            def when(i, name, gate=None):
                dve_s.wait(v, i, name)
                v.sem_inc(turn if gate is None else gate, 1)

            with v.Fori(0, PH // 2) as i:
                for hh in range(2):
                    s = S[:, hh]
                    for k in range(2):
                        v.wait_ge(s_out[k], i * 2 + (hh + 2))
                        v.sem_inc(turn, 1)
                    for t, p in both:
                        m = v.max(top[:, t, p, 0:8], s[:, p, t, :])
                    dve_s.mark(m)
                    when(i, f"max1{hh}")
                    for t, p in both:
                        m = v.max_index(ix[:, t, p, 0:8], top[:, t, p, 0:8], s[:, p, t, :])
                    dve_s.mark(m)
                    for t, p in both:
                        m = v.match_replace(left[:, t, p], top[:, t, p, 0:8], s[:, p, t, :], LOW)
                    dve_s.mark(m)
                    when(i, f"left{hh}", s_free[hh])
                    for t, p in both:
                        m = v.max(top[:, t, p, 8:16], left[:, t, p])
                    dve_s.mark(m)
                    when(i, f"max2{hh}")
                    for t, p in both:
                        m = v.max_index(ix[:, t, p, 8:16], top[:, t, p, 8:16], left[:, t, p])
                    dve_s.mark(m)
                    for t in range(TT):
                        m = v.tensor_tensor(cand[:, t], top[:, t, 0, :].unsqueeze(2).to_broadcast([P, TOPK, TOPK]),
                                            top[:, t, 1, :].unsqueeze(1).to_broadcast([P, TOPK, TOPK]), ALU.add)
                    dve_s.mark(m)
                    when(i, f"cand{hh}")
                    flat = [cand[:, t].rearrange("p a c -> p (a c)") for t in range(TT)]
                    for t in range(TT):
                        m = v.max(ctop[:, t, 0:8], flat[t])
                    dve_s.mark(m)
                    when(i, f"cmax1{hh}")
                    for t in range(TT):
                        m = v.max_index(cix[:, t, 0:8], ctop[:, t, 0:8], flat[t])
                    dve_s.mark(m)
                    for t in range(TT):
                        m = v.match_replace(cleft[:, t], ctop[:, t, 0:8], flat[t], LOW)
                    dve_s.mark(m)
                    when(i, f"cleft{hh}")
                    for t in range(TT):
                        m = v.max(ctop[:, t, 8:16], cleft[:, t])
                    dve_s.mark(m)
                    when(i, f"cmax2{hh}")
                    for t in range(TT):
                        m = v.max_index(cix[:, t, 8:16], ctop[:, t, 8:16], cleft[:, t])
                    dve_s.mark(m)
                    when(i, f"cix2{hh}")
                    head = bass.ds(i * 2 + hh, 1)
                    for p in range(2):
                        v.tensor_copy(b.IX[:, p, :, head, :].rearrange("p t o k -> p t (o k)"), ix[:, :, p, :])
                    v.tensor_copy(b.CI[:, :, head, :].rearrange("p t o k -> p t (o k)"), cix[:])
                    dve_s.mark(v.tensor_copy(b.SC[:, :, head, :].rearrange("p t o k -> p t (o k)"), ctop[:]))


def phase_slots(nc, a, b):
    N = TT * PH
    with ExitStack() as ctx:
        sb = alloc(nc, ctx)

        def sem(name):
            return b.semaphore(nc, name)

        half_ix = sb("cand_half", [P, 2, N, TOPK], U32)
        half_f = sb("cand_half_f", [P, 2, N, TOPK])
        eq = sb("pick", [P, N, TOPK, TOPK])
        idx = sb("slot_src", [P, 3, TT, PH * TOPK])
        total = sb("soft_total", [P, N])
        iota = sb("iota16", [P, TOPK])
        ps = [ctx.enter_context(nc.psum_tensor(f"ps_sl{k}", [P, TX], F32)) for k in range(3)]
        small_in, sub_done, exp_done, dve, src_done, turned, out = (
            sem(f"sl_{n}") for n in ("in", "sub", "exp", "dve", "src", "turned", "out"))
        block = ctx.enter_context(nc.Block())
        sc = b.SC[:].rearrange("p t h k -> p (t h) k")
        w = idx[:, 2].rearrange("p t (h k) -> p (t h) k", k=TOPK)

        @block.sync
        def _(sp):
            sp.dma_start(iota[:], a["iota"][:, 0:TOPK]).then_inc(small_in, 16)

        @block.scalar
        def _(act):
            act.wait_ge(sub_done, 1)
            act.activation(w, w, ACT.Exp).then_inc(exp_done, 1)

        @block.vector
        def _(v):
            link = Count(v, dve)
            v.tensor_tensor(w, sc, sc[:, :, 0:1].to_broadcast([P, N, TOPK]), ALU.subtract).then_inc(sub_done, 1)
            ci = b.CI[:].rearrange("p t h k -> p (t h) k")
            link(v.tensor_scalar(half_ix[:, 0], ci, 4, None, ALU.logical_shift_right))
            link(v.tensor_scalar(half_ix[:, 1], ci, TOPK - 1, None, ALU.bitwise_and))
            link(v.tensor_copy(half_f[:], half_ix[:]))
            v.wait_ge(small_in, 16)
            for side in range(2):
                link(v.tensor_tensor(eq[:], half_f[:, side].unsqueeze(3).to_broadcast([P, N, TOPK, TOPK]),
                                     iota[:].unsqueeze(1).unsqueeze(1).to_broadcast([P, N, TOPK, TOPK]), ALU.is_equal))
                link(v.tensor_tensor(eq[:], eq[:], b.IX[:, side].rearrange("p t h k -> p (t h) k").unsqueeze(2)
                                     .to_broadcast([P, N, TOPK, TOPK]), ALU.mult))
                link(v.tensor_reduce(idx[:, side].rearrange("p t s -> p (t s)"),
                                     eq[:].rearrange("p n k m -> p (n k) m"), AX.X, ALU.add))
            v.wait_ge(exp_done, 1)
            link(v.tensor_reduce(total[:], w, AX.X, ALU.add))
            link(v.reciprocal(total[:], total[:]))
            v.tensor_tensor(w, w, total[:].unsqueeze(2).to_broadcast([P, N, TOPK]), ALU.mult).then_inc(src_done, 1)
            v.wait_ge(turned, 3)
            for k in range(3):
                v.tensor_copy(b.slots[:, k], ps[k][:]).then_inc(out, 1)

        @block.tensor
        def _(pe):
            pe.wait_ge(src_done, 1)
            for k in range(3):
                for t in range(TT):
                    m = pe.transpose(ps[k][:, t * P:(t + 1) * P], idx[:, k, t, :], b.ident[:])
                m.then_inc(turned, 1)


def phase_weights(nc, a, b, w_dram):
    SUB = 4
    HALF = 64
    LOOPS = HALF // (2 * SUB)
    with ExitStack() as ctx:
        sb = alloc(nc, ctx)

        def sem(name):
            return b.semaphore(nc, name)

        iota = sb("iota128", [P, NK])
        oi = sb("onehot_i", [P, 2, SUB, NK])
        oj = sb("onehot_j", [P, 2, SUB, NK])
        wb = sb("w_block", [P, 2, NK, HALF])
        ps = [ctx.enter_context(nc.psum_tensor(f"ps_w{k}", [P, SUB, NK], F32)) for k in range(2)]
        small_in = sem("w_in")
        built, mm, evac = ([sem(f"w_{n}{k}") for k in range(2)] for n in ("built", "mm", "evac"))
        stored = [sem(f"w_stored{k}") for k in range(2)]
        block = ctx.enter_context(nc.Block())
        dst = w_dram.rearrange("j i (n t) -> n i j t", t=HALF)
        n_outer = TX // (2 * HALF)

        @block.sync
        def _(sp):
            sp.dma_start(iota[:], a["iota"]).then_inc(small_in, 16)
            for half in range(2):
                sp.sem_inc(stored[half], 16)
            with sp.Fori(0, n_outer) as o:
                for half in range(2):
                    for s in range(2):
                        sp.wait_ge(evac[s], o * (2 * LOOPS) + ((half + 1) * LOOPS + 1))
                    sp.dma_start(dst[o * 2 + half], wb[:, half]).then_inc(stored[half], 16)
            for half in range(2):
                sp.wait_ge(stored[half], 16 * (n_outer + 1))

        def tokens(eng, body):
            with eng.Fori(0, n_outer) as o:
                for half in range(2):
                    with eng.Fori(0, LOOPS) as g:
                        for s in range(2):
                            body(o, half, g, s, o * (2 * LOOPS) + g + half * LOOPS)

        @block.vector
        def _(v):
            for s in range(2):
                v.sem_inc(built[s], 1)
            v.wait_ge(small_in, 16)

            def body(o, half, g, s, n):
                v.wait_ge(mm[s], n + 1)
                for k in range(SUB):
                    t = o * (2 * HALF) + g * (2 * SUB) + (half * HALF + s * SUB + k)
                    v.tensor_scalar(oi[:, s, k], iota[:], b.slots[:, 0, bass.ds(t, 1)],
                                    b.slots[:, 2, bass.ds(t, 1)], ALU.is_equal, ALU.mult)
                    m = v.tensor_scalar(oj[:, s, k], iota[:], b.slots[:, 1, bass.ds(t, 1)], None, ALU.is_equal)
                m.then_inc(built[s], 1)

            tokens(v, body)

        @block.tensor
        def _(pe):
            for s in range(2):
                pe.sem_inc(mm[s], 1)

            def body(o, half, g, s, n):
                pe.wait_ge(built[s], n + 2)
                pe.wait_ge(evac[s], n + 1)
                for k in range(SUB):
                    m = pe.matmul(ps[s][:, k, :], oi[:, s, k], oj[:, s, k], start=True, stop=True)
                m.then_inc(mm[s], 1)

            tokens(pe, body)

        @block.scalar
        def _(act):
            for s in range(2):
                act.sem_inc(evac[s], 1)

            def body(o, half, g, s, n):
                act.wait_ge(mm[s], n + 2)
                act.wait_ge(stored[half], o * 16 + 16)
                act.activation(wb[:, half, :, bass.ds(g * (2 * SUB) + s * SUB, SUB)].rearrange("p j t -> p t j"),
                               ps[s][:], ACT.Copy).then_inc(evac[s], 1)

            tokens(act, body)


def phase_experts(nc, a, b, w_dram):
    G = 4
    rounds = NK // G
    with ExitStack() as ctx:
        sb = alloc(nc, ctx)

        def sem(name):
            return b.semaphore(nc, name)

        ur = sb("u_ring", [P, G, KT, P])
        vr = sb("v_ring", [P, G, D])
        wr = sb("w_ring", [P, G, TX])
        ga = sb("act", [P, G, TX])
        ps_a = [ctx.enter_context(nc.psum_tensor(f"ps_a{g}", [P, TX], F32)) for g in range(G)]
        ps_y = [ctx.enter_context(nc.psum_tensor(f"ps_y{k}", [P, TX], F32)) for k in range(2)]
        u_in, v_in, w_in, a_mm, gelu, gated = ([sem(f"ex_{n}{g}") for g in range(G)]
                                               for n in ("u_in", "v_in", "w_in", "a_mm", "gelu", "gated"))
        y_mm = [sem(f"ex_y_mm{k}") for k in range(2)]
        y_add = [sem(f"ex_y_add{k}") for k in range(2)]
        half = KT // 2
        block = ctx.enter_context(nc.Block())

        @block.sync
        def _(sp):
            for g in range(G):
                sp.dma_start(ur[:, g], a["uT"][g]).then_inc(u_in[g], 16)
                sp.dma_start(wr[:, g], w_dram[g]).then_inc(w_in[g], 16)
            for g in range(G):
                sp.dma_start(vr[:, g], a["v"][g]).then_inc(v_in[g], 16)
            with sp.Fori(1, rounds) as i:
                for g in range(G):
                    sp.wait_ge(a_mm[g], i)
                    sp.dma_start(ur[:, g], a["uT"][i * G + g]).then_inc(u_in[g], 16)
                    sp.wait_ge(gated[g], i)
                    sp.dma_start(wr[:, g], w_dram[i * G + g]).then_inc(w_in[g], 16)
                sp.wait_ge(y_mm[1], i * half)
                for g in range(G):
                    sp.dma_start(vr[:, g], a["v"][i * G + g]).then_inc(v_in[g], 16)

        @block.tensor
        def _(pe):
            with pe.Fori(0, rounds) as i:
                for g in range(G):
                    pe.wait_ge(u_in[g], i * 16 + 16)
                    pe.wait_ge(gelu[g], i + 1)
                    for j in range(KT):
                        mm = pe.matmul(ps_a[g][:], ur[:, g, j, :], b.h2[:, j, :], start=(j == 0), stop=(j == KT - 1))
                    mm.then_inc(a_mm[g], 1)
                for m in range(KT):
                    pe.wait_ge(y_add[m % 2], i * half + (m // 2 + 1))
                    for g in range(G):
                        if m == 0:
                            pe.wait_ge(v_in[g], i * 16 + 16)
                            pe.wait_ge(gated[g], i + 1)
                        mm = pe.matmul(ps_y[m % 2][:], vr[:, g, m * P:(m + 1) * P], ga[:, g, :],
                                       start=(g == 0), stop=(g == G - 1))
                    mm.then_inc(y_mm[m % 2], 1)

        @block.scalar
        def _(act):
            for g in range(G):
                act.sem_inc(gelu[g], 1)
            with act.Fori(0, rounds) as i:
                for g in range(G):
                    act.wait_ge(a_mm[g], i + 1)
                    act.activation(ga[:, g], ps_a[g][:], ACT.Gelu).then_inc(gelu[g], 1)

        @block.vector
        def _(v):
            for k in range(2):
                v.memset(b.acc[:, k::2], 0.0).then_inc(y_add[k], 1)
            with v.Fori(0, rounds) as i:
                for g in range(G):
                    v.wait_ge(w_in[g], i * 16 + 16)
                    v.wait_ge(gelu[g], i + 2)
                    v.tensor_tensor(ga[:, g], ga[:, g], wr[:, g], ALU.mult).then_inc(gated[g], 1)
                for m in range(KT):
                    v.wait_ge(y_mm[m % 2], i * half + (m // 2 + 1))
                    v.wait_ge(y_add[m % 2], i * half + (m // 2 + 1))
                    v.tensor_tensor(b.acc[:, m], b.acc[:, m], ps_y[m % 2][:], ALU.add).then_inc(y_add[m % 2], 1)


def phase_final(nc, a, b, out):
    with ExitStack() as ctx:
        sb = alloc(nc, ctx)

        def sem(name):
            return b.semaphore(nc, name)

        fg = sb("final_g", [P, KT])
        sq = sb("fin_sq", [P, KT, TX])
        rs = sb("fin_rs", [P, TX])
        ps = ctx.enter_context(nc.psum_tensor("ps_fin", [P, TX], F32))
        small_in, x_done, squared, summed, rooted, dve, y_done, stored = (
            sem(f"fin_{n}") for n in ("in", "x", "sq", "sum", "root", "dve", "y", "stored"))
        block = ctx.enter_context(nc.Block())

        @block.sync
        def _(sp):
            sp.dma_start(fg[:], a["final_g"]).then_inc(small_in, 16)
            for j in range(KT):
                sp.wait_ge(y_done, j + 1)
                sp.dma_start(out[:, j, :], b.acc[:, j]).then_inc(stored, 16)
            sp.wait_ge(stored, 16 * KT)

        @block.vector
        def _(v):
            link = Count(v, dve)
            for j in range(KT):
                v.scalar_tensor_tensor(out=b.x1[:, j], in0=b.acc[:, j], scalar=b.mod[:, 5 * KT + j, 0:1],
                                       in1=b.x1[:, j], op0=ALU.mult, op1=ALU.add).then_inc(x_done, 1)
            v.wait_ge(small_in, 16)
            v.wait_ge(rooted, 1)
            link(v.reciprocal(rs[:], rs[:]))
            v.wait_ge(x_done, KT)
            for j in range(KT):
                v.scalar_tensor_tensor(out=b.acc[:, j], in0=b.x1[:, j], scalar=fg[:, j:j + 1], in1=rs[:],
                                       op0=ALU.mult, op1=ALU.mult).then_inc(y_done, 1)

        @block.scalar
        def _(act):
            for j in range(KT):
                act.wait_ge(x_done, j + 1)
                act.activation(sq[:, j], b.x1[:, j], ACT.Square).then_inc(squared, 1)
            act.wait_ge(summed, 1)
            act.activation(rs[:], ps[:], ACT.Sqrt, bias=b.eps[:, 0:1], scale=1.0 / D).then_inc(rooted, 1)

        @block.tensor
        def _(pe):
            for j in range(KT):
                pe.wait_ge(squared, j + 1)
                mm = pe.matmul(ps[:], b.ones[:], sq[:, j], start=(j == 0), stop=(j == KT - 1))
            mm.then_inc(summed, 1)


def build_program(nc, a, out):
    with ExitStack() as ctx:
        sb = alloc(nc, ctx)
        b = Buffers()
        b.ones = sb("ones", [P, P])
        b.eps = sb("eps", [P, 4])
        b.masks = sb("rwkv_masks", [P, 2, N_MASKS, C])
        b.unit = sb("unit", [P, C])
        b.block_ones = sb("block_ones", [P, P])
        b.ident = sb("ident", [P, P])
        b.mod = sb("mod", [P, N_MOD * KT, 2])
        b.ya = sb("ya", [P, PAIRS, TX])
        b.yb = sb("yb", [P, MH, TX])
        const = ctx.enter_context(nc.semaphore("const_done"))
        const_in = ctx.enter_context(nc.semaphore("const_in"))
        with nc.Block() as block:
            @block.gpsimd
            def _(g):
                g.memset(b.ones[:], 1.0).then_inc(const, 1)
                g.memset(b.eps[:, 0:1], NORM_EPS).then_inc(const, 1)
                g.memset(b.eps[:, 1:2], GN_EPS).then_inc(const, 1)
                g.memset(b.eps[:, 2:3], -HALF_DECAY).then_inc(const, 1)
                g.wait_ge(const, 4)

            @block.sync
            def _(sp):
                sp.dma_start(b.masks[:], a["rwkv_masks"]).then_inc(const_in, 16)
                sp.dma_start(b.unit[:], a["unit"]).then_inc(const_in, 16)
                sp.dma_start(b.block_ones[:], a["block_ones"]).then_inc(const_in, 16)
                sp.dma_start(b.ident[:], a["ident"]).then_inc(const_in, 16)
                sp.wait_ge(const_in, 64)
        h_dram = nc.dram_tensor("h_scratch", [P, KT, TX], F32, kind="Internal").ap()
        with ExitStack() as mixers:
            sm = alloc(nc, mixers)
            b.fX = sm("fX", [P, RW_TILES, TX])
            b.fC = sm("fC", [P, RW_TILES, TC])
            with ExitStack() as ml:
                sl = alloc(nc, ml)
                b.qX = sl("qX", [P, QK_TILES, TX])
                b.qC = sl("qC", [P, QK_TILES, TC])
                b.vM = sl("vM", [P, (TX + TC) // MC, MH, DV + 1])
                b.gates = sl("gates", [GROWS, 2, TX + TC])
                with ExitStack() as norm:
                    b.hT = alloc(nc, norm)("hT_sb", [P, KT, TX + TC])
                    phase_modulation(nc, a, b)
                    phase_projection(nc, a, b, h_dram)
                b.g_rows = sl("g_rows", [GROWS, 3, TX + TC])
                b.g_turn = sl("g_turn", [GROWS, 2, TX + TC])
                b.g_cols = sl("g_cols", [P, (TX + TC) // MC, 2, GROWS])
                b.select = sl("select", [GROWS, UNITS, P])
                b.m_mask = sl("m_mask", [P, 2, MC])
                b.mC = sl("mC", [P, UNITS, DV + 1])
                b.mh = sl("mh", [P, 2, MH, TX])
                phase_mlstm_gates(nc, a, b)
                phase_mlstm(nc, a, b, b.qC, TC, TX // MC, 0, "_c", False)
                phase_mlstm(nc, a, b, b.qX, TX, 0, TC // MC, "_x", True)
                phase_mlstm_output(nc, a, b)
            with ExitStack() as rw:
                sr = alloc(nc, rw)
                b.kk = sr("kk", [P, PAIRS, TX])
                b.ke = sr("ke", [P, 2, PAIRS, TX])
                b.qa = sr("qa", [P, 2, PAIRS, TX])
                b.G = sr("G", [P, 2, PAIRS, TX // C * (C + 1)])
                b.state = sr("rw_state", [P, 2, PAIRS, C])
                phase_rwkv_features(nc, a, b, b.fC, TC, "_c")
                phase_rwkv_scan(nc, a, b, b.fC, TC, "_c", False)
                phase_rwkv_features(nc, a, b, b.fX, TX, "_x")
                b.rwo = sr("rwo", [P, 2, PAIRS, TX])
                phase_rwkv_scan(nc, a, b, b.fX, TX, "_x", True)
                phase_rwkv_output(nc, a, b)
        w_dram = nc.dram_tensor("w_scratch", [NK, P, TX], F32, kind="Internal").ap()
        b.x1 = sb("x1", [P, KT, TX])
        b.h2 = sb("h2", [P, KT, TX])
        b.clear_semaphores(nc)
        phase_merge(nc, a, b, h_dram)
        with ExitStack() as route:
            st = alloc(nc, route)
            b.slots = st("slots", [P, 3, TX])
            b.IX = st("IX", [P, 2, TT, PH, TOPK])
            b.CI = st("CI", [P, TT, PH, TOPK], U32)
            b.SC = st("SC", [P, TT, PH, TOPK])
            phase_route(nc, a, b)
            phase_slots(nc, a, b)
            phase_weights(nc, a, b, w_dram)
        b.clear_semaphores(nc)
        b.acc = sb("acc", [P, KT, TX])
        phase_experts(nc, a, b, w_dram)
        phase_final(nc, a, b, out)


def column(v):
    return v.reshape(-1, P).T


def weight_tiles(w):
    k, n = w.shape
    return w.reshape(k // P, P, n // P, P).transpose(2, 1, 0, 3)


def turned(x):
    return x.T.reshape(-1, P, x.shape[0]).transpose(1, 0, 2)


def laid_out(x, c, ctx, c_ctx, ada_w, ada_b, norm1_g, w_in, rwkv_conv, rwkv_w0, rwkv_w_up, rwkv_a0,
             rwkv_a_up, rwkv_g_up, rwkv_k_k, rwkv_k_a, rwkv_r_k, rwkv_ln_w, rwkv_ln_b, mlstm_conv,
             mlstm_i_b, mlstm_f_b, mlstm_norm_g, w_branch_a, w_branch_b, w_out, norm2_g, peer_wq,
             peer_keys, peer_u, peer_v, final_g):
    rw_cols = RW_TILES * P
    ends = np.cumsum([rw_cols, 2 * MH * DQK, MH * DV, 2 * MH, 2 * MH, MH * DV, D, D])
    w_rw, w_qk, w_mv, w_i, w_f, w_o, w_ga, w_gb = np.split(w_in[0], ends[:-1], axis=1)
    gates = np.zeros((D, 2, GROWS), w_in.dtype)
    gate_bias = np.zeros((GROWS, 2), w_in.dtype)
    for k, (w, bias) in enumerate(((w_i, mlstm_i_b[0]), (w_f, mlstm_f_b[0]))):
        for z in range(2):
            gates[:, k, 32 * z:32 * z + MH] = w[:, z * MH:(z + 1) * MH]
            gate_bias[32 * z:32 * z + MH, k] = bias[z]
    w_ab = np.concatenate([w_branch_a[0], w_branch_b[0]], 0)
    merge = np.stack([weight_tiles(w_ga), weight_tiles(w_gb), weight_tiles(w_ab)], 2)
    r = np.arange(P)
    mask = np.zeros((P, 2, MC), np.float32)
    mask[:, 0] = np.where(r[:, None] <= r[None, :], 0.0, NEG)
    mask[:, 1] = np.where(r[:, None] >= r[None, :], 0.0, NEG)
    resets = np.zeros((GROWS, 2, (TX + TC) // MC, MC), np.float32)
    resets[:, 0, :, 1:] = 1.0
    resets[:, 1, :, 0] = NEG
    select = np.zeros((GROWS, UNITS, P), np.float32)
    for u in range(UNITS):
        select[u % MH + 32 * (u // MH), u] = 1.0
    return {
        "xT": turned(x[0]), "ctxT": turned(ctx[0]),
        "cc": np.stack([c[0], c_ctx], -1).reshape(KT, P, 2).transpose(1, 0, 2),
        "ada_w": weight_tiles(ada_w[0]), "ada_b": column(ada_b[0]), "norm1_g": column(norm1_g[0]),
        "w_rw": weight_tiles(np.concatenate([w_rw, w_qk], 1)),
        "w_mv": w_mv.reshape(KT, P, MH * DV).transpose(1, 0, 2),
        "w_gates": gates.reshape(KT, P, 2, GROWS).transpose(1, 0, 2, 3),
        "rwkv_conv": rwkv_conv[0].reshape(3, RW_TILES, P).transpose(2, 1, 0),
        "mlstm_conv": mlstm_conv[0].reshape(3, QK_TILES, P).transpose(2, 1, 0),
        "wa_up": np.concatenate([rwkv_w_up[0], rwkv_a_up[0]], 1).transpose(1, 0, 2),
        "rw_vecs": np.stack([column(v) for v in (rwkv_w0[0, 0], rwkv_w0[0, 1], rwkv_a0[0, 0], rwkv_a0[0, 1],
                                                 rwkv_k_k[0], rwkv_k_a[0])], 1),
        "g_up": rwkv_g_up[0],
        "rwo_vecs": np.stack([column(v[0]) for v in (rwkv_r_k, rwkv_ln_w, rwkv_ln_b)], 1),
        "gate_bias": gate_bias, "mlstm_g": column(mlstm_norm_g[0]),
        "w_o": weight_tiles(w_o).transpose(1, 0, 2, 3), "w_merge": merge, "w_out": weight_tiles(w_out[0]),
        "norm2_g": column(norm2_g[0]),
        "w_q": weight_tiles(peer_wq[0]),
        "keys": peer_keys[0].transpose(3, 0, 1, 2).reshape(P, 2 * PH, NK),
        "uT": peer_u[0].reshape(NK, NK, KT, P).transpose(1, 3, 2, 0),
        "v": peer_v[0].reshape(NK, NK, D).transpose(1, 0, 2),
        "final_g": column(final_g),
        "rwkv_masks": rwkv_masks(), "unit": np.tile(np.eye(C, dtype=np.float32), (2, 1)),
        "block_ones": np.kron(np.eye(2, dtype=np.float32), np.ones((C, C), np.float32)),
        "ident": np.eye(P, dtype=np.float32), "gate_resets": resets, "select": select, "m_mask": mask,
        "iota": np.tile(np.arange(NK, dtype=np.float32), (P, 1)),
    }


def kernel(**inputs):
    import concourse.bacc as _bacc
    from concourse.bass_utils import run_bass_kernel_spmd as _run

    nc = _bacc.Bacc("TRN2", target_bir_lowering=False, num_devices=1)
    arrays, args = {}, {}
    for name, v in laid_out(**inputs).items():
        v = np.ascontiguousarray(v)
        arrays[f"in_{name}"] = v
        args[name] = nc.dram_tensor(f"in_{name}", v.shape, mybir.dt.from_np(v.dtype), kind="ExternalInput").ap()
    out = nc.dram_tensor("out_y", (P, KT, TX), F32, kind="ExternalOutput").ap()
    build_program(nc, args, out)
    y = _run(nc, [arrays], core_ids=[0]).results[0]["out_y"]
    return y.transpose(1, 0, 2).reshape(D, TX).T[None]
```

```python
from contextlib import ExitStack

import numpy as np

import concourse.bass as bass
from concourse import mybir

F32 = mybir.dt.float32
F32R = mybir.dt.float32r
U32 = mybir.dt.uint32
ALU = mybir.AluOpType
ACT = mybir.ActivationFunctionType
AX = mybir.AxisListType

P = 128
D = 1024
KT = D // P
TX, TC = 512, 256
GRID_W = 64
ROWS = TX // GRID_W
N_MOD = 6
NORM_EPS = 1e-6
NEG = -1e30

D_RWKV = 512
RW_TILES = 14
PAIRS = 4
C = 64
GN_EPS = 64e-5
DECAY = float(np.exp(-0.5))

MH = 4
DQK, DV = 64, 128
MC = 128
GROWS = 36
QK_TILES = 4

PH, NK, TOPK = 8, 128, 16


class Count:

    def __init__(self, eng, sem):
        self.eng, self.sem, self.n = eng, sem, 0

    def __call__(self, ins):
        ins.then_inc(self.sem, 1)
        self.n += 1
        self.eng.wait_ge(self.sem, self.n)


class Steps:

    def __init__(self, sem, names):
        self.sem, self.names = sem, list(names)

    def start(self, eng):
        eng.sem_inc(self.sem, 1)

    def wait(self, eng, i, name):
        eng.wait_ge(self.sem, i * len(self.names) + (self.names.index(name) + 2))

    def wait_last(self, eng, i):
        eng.wait_ge(self.sem, i * len(self.names) + 1)

    def mark(self, ins):
        ins.then_inc(self.sem, 1)


def product(pe, out, wh, wl, xh, xl, first, last):
    pe.matmul(out, wh, xh, start=first, stop=False)
    pe.matmul(out, wl, xh, start=False, stop=False)
    return pe.matmul(out, wh, xl, start=False, stop=last)


class Buffers:

    def __init__(self):
        self.used = []

    def semaphore(self, nc, name):
        s = nc.alloc_semaphore(name)
        self.used.append(s)
        return s

    def clear_semaphores(self, nc):
        nc.clear_and_free_semaphores(self.used)
        self.used = []
        nc.all_engine_barrier()


def alloc(nc, ctx):
    def sb(name, shape, dt=F32):
        return ctx.enter_context(nc.sbuf_tensor(name, shape, dt))
    return sb


MOD_W = 512
MOD_TILES = N_MOD * D // MOD_W
MOD_FIRST = 2 * D // MOD_W
PER = MOD_W // P


class Modulation:

    def __init__(self, nc, ctx, a, b, tag, lo, hi, row):
        self.a, self.b, self.lo, self.hi = a, b, lo, hi
        self.ring = ctx.enter_context(nc.sbuf_tensor("ada_ring" + tag, [P, 2, KT, MOD_W], F32))
        self.bias = ctx.enter_context(nc.sbuf_tensor("ada_bias" + tag, [P, N_MOD * KT], F32))
        self.row = row
        self.ps_row = [ctx.enter_context(nc.psum_tensor(f"ps_row{k}" + tag, [P, MOD_W], F32)) for k in range(2)]
        self.ps_mod = ctx.enter_context(nc.psum_tensor("ps_mod" + tag, [P, 512], F32))
        self.ring_in = [b.semaphore(nc, f"ada_in{k}" + tag) for k in range(2)]
        self.bias_in, self.mm, self.out, self.turned, self.done = (
            b.semaphore(nc, f"mod_{n}" + tag) for n in ("bias_in", "mm", "row_out", "turned", "done"))

    def load(self, sp, n):
        if n >= 2:
            sp.wait_ge(self.mm, n - 1)
        sp.dma_start(self.ring[:, n % 2], self.a["ada_w"][self.lo + n]).then_inc(self.ring_in[n % 2], 16)

    def load_bias(self, sp):
        sp.dma_start(self.bias[:], self.a["ada_b"]).then_inc(self.bias_in, 16)

    def multiply(self, pe, n):
        pe.wait_ge(self.ring_in[n % 2], (n // 2 + 1) * 16)
        if n >= 2:
            pe.wait_ge(self.out, n - 1)
        for k in range(KT):
            mm = pe.matmul(self.ps_row[n % 2][0:2, :], self.b.silu_c[:, k, :], self.ring[:, n % 2, k, :],
                           start=(k == 0), stop=(k == KT - 1))
        mm.then_inc(self.mm, 1)

    def copy_row(self, act, n):
        act.wait_ge(self.mm, n + 1)
        act.activation(self.row[:, n, :], self.ps_row[n % 2][0:2, :], ACT.Copy).then_inc(self.out, 1)

    def turn(self, pe):
        pe.wait_ge(self.out, self.hi - self.lo)
        for n in range(self.hi - self.lo):
            for q in range(PER):
                o = 2 * (n * PER + q)
                mm = pe.matmul(self.ps_mod[:, o:o + 2], self.row[:, n, q * P:(q + 1) * P], self.b.ident[0:2, 0:2],
                               start=True, stop=True)
        mm.then_inc(self.turned, 1)

    def add_bias(self, v):
        lo, hi = self.lo * PER, self.hi * PER
        v.wait_ge(self.bias_in, 16)
        v.wait_ge(self.turned, 1)
        v.tensor_tensor(self.b.mod[:, lo:hi, :], self.ps_mod[:, 0:2 * (hi - lo)].rearrange("p (g s) -> p g s", s=2),
                        self.bias[:, lo:hi].unsqueeze(2).to_broadcast([P, hi - lo, 2]), ALU.add).then_inc(self.done, 1)
        v.wait_ge(self.done, 1)


def phase_modulation(nc, a, b, h_dram):
    with ExitStack() as ctx:
        sb = alloc(nc, ctx)

        def sem(name):
            return b.semaphore(nc, name)

        cc = sb("cc", [P, KT, 2])
        th = sb("cc_th", [P, KT, 2])
        g1 = sb("g1", [P, KT])
        h = sb("h_f32", [P, KT, TX + TC])
        xx, xc = b.acc, b.fC[:, 0:KT, :]
        rs = sb("rs", [P, TX + TC])
        scale = sb("scale1", [P, 2, KT])
        ps_sx = ctx.enter_context(nc.psum_tensor("ps_sx", [P, TX], F32))
        ps_sc = ctx.enter_context(nc.psum_tensor("ps_sc", [P, 512], F32))
        small_in, x_in, h_out = sem("mod_small_in"), sem("mod_x_in"), sem("mod_h_out")
        tanh_done, silu_done = sem("mod_tanh"), sem("mod_silu")
        sq_done, sum_done, sqrt_done = sem("sq_done"), sem("sum_done"), sem("sqrt_done")
        scaled, shifted, rounded, rest = sem("h_scaled"), sem("h_shifted"), sem("h_rounded"), sem("h_rest")
        dve = sem("mod_dve")
        mod = Modulation(nc, ctx, a, b, "_1", 0, MOD_FIRST, b.qX[0:2, :, :])
        block = ctx.enter_context(nc.Block())

        @block.sync
        def _(sp):
            sp.dma_start(cc[:], a["cc"]).then_inc(small_in, 16)
            sp.dma_start(g1[:], a["norm1_g"]).then_inc(small_in, 16)
            mod.load_bias(sp)
            sp.dma_start(xx[:], a["xT"]).then_inc(x_in, 16)
            sp.dma_start(xc, a["ctxT"]).then_inc(x_in, 16)
            for n in range(MOD_FIRST):
                mod.load(sp, n)
            sp.wait_ge(shifted, KT)
            sp.dma_start(h_dram, h[:, :, 0:TX]).then_inc(h_out, 16)
            sp.wait_ge(h_out, 16)

        @block.scalar
        def _(act):
            act.wait_ge(small_in, 32)
            act.activation(th[:], cc[:], ACT.Tanh, scale=0.5).then_inc(tanh_done, 1)
            act.wait_ge(x_in, 32)
            act.activation(h[:, :, 0:TX], xx[:], ACT.Square).then_inc(sq_done, 1)
            act.activation(h[:, :, TX:], xc, ACT.Square).then_inc(sq_done, 1)
            act.wait_ge(sum_done, 1)
            act.activation(rs[:, 0:TX], ps_sx[:], ACT.Sqrt, bias=b.eps[:, 0:1], scale=1.0 / D).then_inc(sqrt_done, 1)
            act.activation(rs[:, TX:], ps_sc[:, 0:TC], ACT.Sqrt, bias=b.eps[:, 0:1], scale=1.0 / D).then_inc(sqrt_done, 1)
            for n in range(MOD_FIRST):
                mod.copy_row(act, n)
            for j in range(KT):
                act.wait_ge(scaled, 2 * j + 2)
                for s, (lo, hi) in enumerate(((0, TX), (TX, TX + TC))):
                    m = act.activation(h[:, j, lo:hi], h[:, j, lo:hi], ACT.Identity, bias=b.mod[:, j, s:s + 1])
                m.then_inc(shifted, 1)
                act.wait_ge(shifted, j + 1)
                act.activation(b.hh[:, j], h[:, j], ACT.Copy).then_inc(rounded, 1)

        @block.gpsimd
        def _(g):
            for j in range(KT):
                g.wait_ge(rounded, j + 1)
                g.tensor_tensor(b.hl[:, j], h[:, j], b.hh[:, j], ALU.subtract).then_inc(rest, 1)

        @block.tensor
        def _(pe):
            pe.wait_ge(sq_done, 2)
            for k in range(KT):
                pe.matmul(ps_sx[:], b.ones[:], h[:, k, 0:TX], start=(k == 0), stop=(k == KT - 1))
            for k in range(KT):
                mm = pe.matmul(ps_sc[:, 0:TC], b.ones[:], h[:, k, TX:], start=(k == 0), stop=(k == KT - 1))
            mm.then_inc(sum_done, 1)
            pe.wait_ge(silu_done, 1)
            for n in range(MOD_FIRST):
                mod.multiply(pe, n)
            mod.turn(pe)

        @block.vector
        def _(v):
            link = Count(v, dve)
            v.wait_ge(small_in, 32)
            v.wait_ge(tanh_done, 1)
            link(v.scalar_tensor_tensor(out=b.silu_c[:], in0=th[:], scalar=1.0, in1=cc[:], op0=ALU.add, op1=ALU.mult))
            v.tensor_scalar(b.silu_c[:], b.silu_c[:], 0.5, None, ALU.mult).then_inc(silu_done, 1)
            v.wait_ge(sqrt_done, 2)
            link(v.reciprocal(rs[:], rs[:]))
            mod.add_bias(v)
            for s in range(2):
                link(v.scalar_tensor_tensor(out=scale[:, s], in0=b.mod[:, KT:2 * KT, s], scalar=1.0, in1=g1[:],
                                            op0=ALU.add, op1=ALU.mult))
            for k in range(KT):
                for s, (src, lo, hi) in enumerate(((xx, 0, TX), (xc, TX, TX + TC))):
                    v.scalar_tensor_tensor(out=h[:, k, lo:hi], in0=src[:, k, :], scalar=scale[:, s, k:k + 1],
                                           in1=rs[:, lo:hi], op0=ALU.mult, op1=ALU.mult).then_inc(scaled, 1)


def phase_projection(nc, a, b):
    with ExitStack() as ctx:
        sb = alloc(nc, ctx)

        def sem(name):
            return b.semaphore(nc, name)

        ring = sb("win_ring", [P, 2, KT, P])
        wh, wl = sb("win_hi", [P, 2, KT, P], F32R), sb("win_lo", [P, 2, KT, P], F32R)
        cw = sb("conv_r", [P, RW_TILES, 3])
        cq = sb("conv_q", [P, QK_TILES, 3])
        ps_x = [ctx.enter_context(nc.psum_tensor(f"ps_px{k}", [P, TX], F32)) for k in range(2)]
        ps_c = [ctx.enter_context(nc.psum_tensor(f"ps_pc{k}", [P, 512], F32)) for k in range(2)]
        small_in = sem("proj_small_in")
        ring_in = [sem(f"proj_in{k}") for k in range(2)]
        mm_done = [sem(f"proj_mm{k}") for k in range(2)]
        centre = [sem(f"proj_centre{k}") for k in range(2)]
        taps = [sem(f"proj_taps{k}") for k in range(2)]
        w_hi = [sem(f"proj_w_hi{k}") for k in range(2)]
        w_lo = [sem(f"proj_w_lo{k}") for k in range(2)]
        one, col_done = sem("proj_vec"), sem("proj_col")
        n_r, n_q = RW_TILES // 2, QK_TILES // 2
        block = ctx.enter_context(nc.Block())

        @block.gpsimd
        def _(g):
            def rest(i, k):
                g.wait_ge(w_hi[k], i + 1)
                g.tensor_tensor(wl[:, k], ring[:, k], wh[:, k], ALU.subtract).then_inc(w_lo[k], 1)

            with g.Fori(0, n_r + n_q) as i:
                for k in range(2):
                    rest(i, k)
            for j in range(KT):
                g.tensor_tensor(b.hf[:, j, 0:TX].rearrange("p (w r) -> p w r", r=ROWS),
                                b.hh[:, j, 0:TX].rearrange("p (r w) -> p w r", w=GRID_W),
                                b.hl[:, j, 0:TX].rearrange("p (r w) -> p w r", w=GRID_W), ALU.add).then_inc(col_done, 1)
                g.tensor_tensor(b.hf[:, j, TX:], b.hh[:, j, TX:], b.hl[:, j, TX:], ALU.add).then_inc(col_done, 1)

        @block.sync
        def _(sp):
            for k in range(2):
                sp.dma_start(ring[:, k], a["w_rw"][k]).then_inc(ring_in[k], 16)
            sp.dma_start(cw[:], a["rwkv_conv"]).then_inc(small_in, 16)
            sp.dma_start(cq[:], a["mlstm_conv"]).then_inc(small_in, 16)
            with sp.Fori(1, n_r + n_q) as i:
                for k in range(2):
                    sp.wait_ge(w_lo[k], i)
                    sp.dma_start(ring[:, k], a["w_rw"][i * 2 + k]).then_inc(ring_in[k], 16)

        @block.tensor
        def _(pe):
            with pe.Fori(0, n_r + n_q) as i:
                for k in range(2):
                    pe.wait_ge(w_lo[k], i + 1)
                    pe.wait_ge(taps[k], i + 1)
                    for out, lo, hi in ((ps_x[k][:], 0, TX), (ps_c[k][:, 0:TC], TX, TX + TC)):
                        for j in range(KT):
                            mm = product(pe, out, wh[:, k, j, :], wl[:, k, j, :], b.hh[:, j, lo:hi], b.hl[:, j, lo:hi],
                                         j == 0, j == KT - 1)
                    mm.then_inc(mm_done[k], 1)

        @block.scalar
        def _(act):
            act.wait_ge(small_in, 32)
            for k in range(2):
                act.sem_inc(taps[k], 1)

            def round_weights(i, k):
                act.wait_ge(ring_in[k], i * 16 + 16)
                act.activation(wh[:, k], ring[:, k], ACT.Copy).then_inc(w_hi[k], 1)

            for k in range(2):
                round_weights(0, k)
            with act.Fori(0, n_r) as i:
                for k in range(2):
                    act.wait_ge(mm_done[k], i + 1)
                    t = i * 2 + k
                    act.activation(b.fX[:, bass.ds(t, 1), :], ps_x[k][:].unsqueeze(1), ACT.Copy,
                                   scale=cw[:, bass.ds(t, 1), 1]).then_inc(centre[k], 1)
                    act.activation(b.fC[:, bass.ds(t, 1), :], ps_c[k][:, 0:TC].unsqueeze(1), ACT.Copy,
                                   scale=cw[:, bass.ds(t, 1), 1]).then_inc(centre[k], 1)
                    round_weights(i + 1, k)
            for i in range(n_q):
                for k in range(2):
                    act.wait_ge(mm_done[k], n_r + i + 1)
                    t = 2 * i + k
                    act.activation(b.qX[:, t, :].rearrange("p (w r) -> p r w", r=ROWS),
                                   ps_x[k][:].rearrange("p (r w) -> p r w", w=GRID_W), ACT.Copy,
                                   scale=cq[:, t, 1:2]).then_inc(centre[k], 1)
                    act.activation(b.qC[:, t, :], ps_c[k][:, 0:TC], ACT.Copy, scale=cq[:, t, 1:2]).then_inc(centre[k], 1)
                    if i < n_q - 1:
                        round_weights(n_r + i + 1, k)

        @block.vector
        def _(v):
            with v.Fori(0, n_r) as i:
                for k in range(2):
                    v.wait_ge(centre[k], i * 2 + 2)
                    t = i * 2 + k
                    z = ps_x[k][:].rearrange("p (r w) -> p r w", w=GRID_W)
                    o = b.fX[:, bass.ds(t, 1), :].rearrange("p o (r w) -> p (o r) w", w=GRID_W)
                    zc, oc = ps_c[k][:, 0:TC], b.fC[:, bass.ds(t, 1), :].rearrange("p o w -> p (o w)")
                    v.scalar_tensor_tensor(out=o[:, :, 1:], in0=z[:, :, :-1], scalar=cw[:, bass.ds(t, 1), 0],
                                           in1=o[:, :, 1:], op0=ALU.mult, op1=ALU.add)
                    v.scalar_tensor_tensor(out=oc[:, 1:], in0=zc[:, :-1], scalar=cw[:, bass.ds(t, 1), 0],
                                           in1=oc[:, 1:], op0=ALU.mult, op1=ALU.add).then_inc(one, 1)
                    v.wait_ge(one, i * 2 + k + 1)
                    v.scalar_tensor_tensor(out=o[:, :, :-1], in0=z[:, :, 1:], scalar=cw[:, bass.ds(t, 1), 2],
                                           in1=o[:, :, :-1], op0=ALU.mult, op1=ALU.add)
                    v.scalar_tensor_tensor(out=oc[:, :-1], in0=zc[:, 1:], scalar=cw[:, bass.ds(t, 1), 2],
                                           in1=oc[:, :-1], op0=ALU.mult, op1=ALU.add).then_inc(taps[k], 1)
            for i in range(n_q):
                for k in range(2):
                    v.wait_ge(centre[k], 2 * (n_r + i) + 2)
                    t = 2 * i + k
                    z = ps_x[k][:].rearrange("p (r w) -> p r w", w=GRID_W)
                    o = b.qX[:, t, :].rearrange("p (w r) -> p r w", r=ROWS)
                    zc, oc = ps_c[k][:, 0:TC], b.qC[:, t, :]
                    v.scalar_tensor_tensor(out=o[:, 1:, :], in0=z[:, :-1, :], scalar=cq[:, t, 0:1],
                                           in1=o[:, 1:, :], op0=ALU.mult, op1=ALU.add)
                    v.scalar_tensor_tensor(out=oc[:, 1:], in0=zc[:, :-1], scalar=cq[:, t, 0:1],
                                           in1=oc[:, 1:], op0=ALU.mult, op1=ALU.add).then_inc(one, 1)
                    v.wait_ge(one, RW_TILES + t + 1)
                    v.scalar_tensor_tensor(out=o[:, :-1, :], in0=z[:, 1:, :], scalar=cq[:, t, 2:3],
                                           in1=o[:, :-1, :], op0=ALU.mult, op1=ALU.add)
                    v.scalar_tensor_tensor(out=oc[:, :-1], in0=zc[:, 1:], scalar=cq[:, t, 2:3],
                                           in1=oc[:, :-1], op0=ALU.mult, op1=ALU.add).then_inc(taps[k], 1)


def phase_values(nc, a, b):
    with ExitStack() as ctx:
        sb = alloc(nc, ctx)

        def sem(name):
            return b.semaphore(nc, name)

        wv = sb("win_v", [P, KT, MH * DV])
        wg = sb("win_gates", [P, KT, 2, GROWS])
        th = sb("qk_tanh", [P, QK_TILES, TX])
        ps_v = [ctx.enter_context(nc.psum_tensor(f"ps_pv{k}", [P, 512], F32)) for k in range(2)]
        ps_x = [ctx.enter_context(nc.psum_tensor(f"ps_gx{k}", [P, TX], F32)) for k in range(2)]
        ps_c = [ctx.enter_context(nc.psum_tensor(f"ps_gc{k}", [P, 512], F32)) for k in range(2)]
        v_in = sem("val_in")
        v_mm, v_out = sem("val_mm"), sem("val_out")
        g_mm, g_out = sem("val_g_mm"), sem("val_g_out")
        tanh_done, dve, ones_col = sem("val_tanh"), sem("val_dve"), sem("ones_column")
        block = ctx.enter_context(nc.Block())

        @block.sync
        def _(sp):
            sp.dma_start(wv[:], a["w_mv"]).then_inc(v_in, 16)
            sp.dma_start(wg[:], a["w_gates"]).then_inc(v_in, 16)

        @block.tensor
        def _(pe):
            pe.wait_ge(v_in, 32)
            for t in range((TX + TC) // MC):
                if t >= 2:
                    pe.wait_ge(v_out, t - 1)
                for j in range(KT):
                    mm = pe.matmul(ps_v[t % 2][:], b.hf[:, j, t * MC:(t + 1) * MC], wv[:, j, :],
                                   start=(j == 0), stop=(j == KT - 1))
                mm.then_inc(v_mm, 1)
            for gt in range(2):
                for lo, hi, bank in ((0, TX, ps_x[gt]), (TX, TX + TC, ps_c[gt])):
                    for j in range(KT):
                        mm = pe.matmul(bank[0:GROWS, 0:hi - lo], wg[:, j, gt, :], b.hf[:, j, lo:hi],
                                       start=(j == 0), stop=(j == KT - 1))
            mm.then_inc(g_mm, 1)

        @block.scalar
        def _(act):
            act.activation(th[:], b.qX[:], ACT.Tanh, scale=0.5).then_inc(tanh_done, 1)
            for t in range((TX + TC) // MC):
                act.wait_ge(v_mm, t + 1)
                act.activation(b.vM[:, t, :, 0:DV], ps_v[t % 2][:].rearrange("p (h v) -> p h v", v=DV),
                               ACT.Copy).then_inc(v_out, 1)
            act.wait_ge(dve, 1)
            act.activation(th[:, :, 0:TC], b.qC[:], ACT.Tanh, scale=0.5).then_inc(tanh_done, 1)
            act.wait_ge(g_mm, 1)
            for gt in range(2):
                act.activation(b.gates[:, gt, 0:TX], ps_x[gt][0:GROWS], ACT.Copy).then_inc(g_out, 1)
                act.activation(b.gates[:, gt, TX:], ps_c[gt][0:GROWS, 0:TC], ACT.Copy).then_inc(g_out, 1)

        @block.vector
        def _(v):
            v.memset(b.vM[:, :, :, DV:], 1.0).then_inc(ones_col, 1)
            link = Count(v, dve)
            for s, (z, n) in enumerate(((b.qX, TX), (b.qC, TC))):
                v.wait_ge(tanh_done, s + 1)
                zf, tf = z[:], th[:, :, 0:n]
                link(v.scalar_tensor_tensor(out=zf, in0=tf, scalar=1.0, in1=zf, op0=ALU.add, op1=ALU.mult))
                half = QK_TILES // 2
                link(v.tensor_scalar(z[:, 0:half], z[:, 0:half], 0.5, None, ALU.mult))
                link(v.tensor_scalar(z[:, half:], z[:, half:], 0.5 * DQK ** -0.5, None, ALU.mult))


HALF_DECAY = 0.5 * DECAY
LEVELS = [2, 4, 8, 16, 32]
M_NEG1_TS, M_NEG1_ST, M_STRICT, M_NEG_INCL, M_INCL, M_OFF = 0, 1, 2, 3, 4, 5
N_MASKS = 5 + len(LEVELS)


def rwkv_masks():
    r = np.arange(C)
    out = np.zeros((C, 2, N_MASKS, C), np.float32)
    for z in range(2):
        first = (lambda s, t: s < t) if z == 0 else (lambda s, t: s > t)
        s_t = first(r[:, None], r[None, :])
        t_s = s_t.T

        def off(size):
            same = (r[:, None] // (2 * size)) == (r[None, :] // (2 * size))
            return same & ((r[:, None] // size) != (r[None, :] // size))

        out[:, z, M_NEG1_TS] = -(off(1) & t_s).astype(np.float32)
        out[:, z, M_NEG1_ST] = -(off(1) & s_t).astype(np.float32)
        out[:, z, M_STRICT] = s_t
        out[:, z, M_NEG_INCL] = -(s_t | np.eye(C, dtype=bool)).astype(np.float32)
        out[:, z, M_INCL] = s_t | np.eye(C, dtype=bool)
        for n, size in enumerate(LEVELS):
            out[:, z, M_OFF + n] = off(size) & t_s
    return np.concatenate([out, out], 0)


def phase_rwkv_features(nc, a, b, f, T, tag):
    nch = T // C
    with ExitStack() as ctx:
        sb = alloc(nc, ctx)

        def sem(name):
            return b.semaphore(nc, name + tag)

        wa_up = sb("wa_up" + tag, [P, 2, D_RWKV])
        vecs = sb("rw_vecs" + tag, [P, 6, PAIRS])
        half = sb("rw_half" + tag, [P, 4, PAIRS])
        one_ka = sb("rw_1ka" + tag, [P, PAIRS])
        w65 = sb("w65" + tag, [P, PAIRS, nch, C + 1])
        first = sb("w65_first" + tag, [P, nch, C + 1])
        tmp = sb("rw_tmp" + tag, [P, PAIRS, T])
        th = sb("rw_th" + tag, [P, 2, T])
        ps = [ctx.enter_context(nc.psum_tensor(f"ps_rf{k}" + tag, [P, 512], F32)) for k in range(8)]
        vec_in = sem("rwf_in")
        tanh_wd, half_done, proj = sem("rwf_tanh"), sem("rwf_half"), sem("rwf_proj")
        th_done, dec_done, a_done = sem("rwf_th"), sem("rwf_decay"), sem("rwf_a")
        sq_in, sq_done, norm_mm, norm_max, norm_sqrt = (sem("rwf_kk"), sem("rwf_sq"), sem("rwf_norm"),
                                                        sem("rwf_max"), sem("rwf_sqrt"))
        dve, a_used, scanned = sem("rwf_dve"), sem("rwf_a_used"), sem("rwf_scanned")
        block = ctx.enter_context(nc.Block())

        @block.sync
        def _(sp):
            sp.dma_start(wa_up[:], a["wa_up"]).then_inc(vec_in, 16)
            sp.dma_start(vecs[:], a["rw_vecs"]).then_inc(vec_in, 16)

        @block.scalar
        def _(act):
            act.activation(f[0:64, 12, :], f[0:64, 12, :], ACT.Tanh).then_inc(tanh_wd, 1)
            act.wait_ge(half_done, 1)
            act.wait_ge(sq_in, 1)
            act.activation(tmp[:], b.kk[:, :, 0:T], ACT.Square).then_inc(sq_done, 1)
            for z in range(2):
                for c in range(PAIRS):
                    n = z * PAIRS + c
                    act.wait_ge(proj, n + 1)
                    act.activation(th[:, n % 2], ps[2 * (n % 2)][:, 0:T], ACT.Tanh, bias=half[:, z, c:c + 1],
                                   scale=0.5).then_inc(th_done, 1)
                    act.wait_ge(th_done, n + 1)
                    if z == 1:
                        act.wait_ge(scanned, c + 1)
                    act.activation(w65[:, c, :, 1:] if z == 0 else w65[:, c, :, 0:C],
                                   th[:, n % 2].rearrange("p (n t) -> p n t", t=C), ACT.Exp,
                                   bias=b.eps[:, 2:3], scale=-HALF_DECAY).then_inc(dec_done, 1)
                    act.activation(b.qa[:, z, c, 0:T], ps[2 * (n % 2) + 1][:, 0:T], ACT.Tanh,
                                   bias=half[:, 2 + z, c:c + 1], scale=0.5).then_inc(a_done, 1)
            act.wait_ge(norm_max, 1)
            act.activation(tmp[:], tmp[:], ACT.Sqrt).then_inc(norm_sqrt, 1)

        @block.tensor
        def _(pe):
            pe.wait_ge(vec_in, 32)
            pe.wait_ge(tanh_wd, 1)
            for n in range(2 * PAIRS):
                z, c = n // PAIRS, n % PAIRS
                if n >= 2:
                    pe.wait_ge(a_done, n - 1)
                pe.matmul(ps[2 * (n % 2)][:, 0:T], wa_up[0:64, z, c * P:(c + 1) * P], f[0:64, 12, :],
                          start=True, stop=True)
                pe.matmul(ps[2 * (n % 2) + 1][:, 0:T], wa_up[64:P, z, c * P:(c + 1) * P], f[64:P, 12, :],
                          start=True, stop=True).then_inc(proj, 1)
            pe.wait_ge(sq_done, 1)
            for c in range(PAIRS):
                mm = pe.matmul(ps[4 + c][:, 0:T], b.block_ones[:], tmp[:, c, :], start=True, stop=True)
            mm.then_inc(norm_mm, 1)

        @block.vector
        def _(v):
            link = Count(v, dve)
            v.wait_ge(vec_in, 32)
            link(v.tensor_scalar(half[:], vecs[:, 0:4, :], 0.5, None, ALU.mult))
            v.tensor_scalar(one_ka[:], vecs[:, 5, :], -1.0, 1.0, ALU.mult, ALU.add).then_inc(half_done, 1)
            v.wait_ge(half_done, 1)
            for c in range(PAIRS):
                m = v.tensor_scalar(b.kk[:, c, 0:T], f[:, 4 + c, :], vecs[:, 4, c:c + 1], None, ALU.mult)
            m.then_inc(sq_in, 1)
            link(v.memset(first[:], 0.0))
            link(v.memset(first[:, :, 0:1], 1.0))
            for z in range(2):
                slot = 0 if z == 0 else C
                if z == 1:
                    v.wait_ge(scanned, PAIRS)
                    v.wait_ge(dec_done, 2 * PAIRS)
                link(v.memset(w65[:, :, :, slot:slot + 1], 0.0))
                for c in range(PAIRS):
                    v.wait_ge(dec_done, z * PAIRS + c + 1)
                    w = w65[:, c].rearrange("p n t -> p (n t)")
                    g = b.G[:, z, c, 0:nch * (C + 1)]
                    if z:
                        w, g = w[:, ::-1], g[:, ::-1]
                    v.tensor_tensor_scan(out=g, data0=w, data1=first[:].rearrange("p n t -> p (n t)"), initial=0.0,
                                         op0=ALU.mult, op1=ALU.add).then_inc(scanned, 1)
            v.wait_ge(norm_mm, 1)
            v.wait_ge(sq_done, 1)
            for c in range(PAIRS):
                m = v.tensor_scalar(tmp[:, c, :], ps[4 + c][:, 0:T], 1e-24, None, ALU.max)
            m.then_inc(norm_max, 1)
            v.wait_ge(norm_sqrt, 1)
            link(v.reciprocal(tmp[:], tmp[:]))
            link(v.tensor_tensor(b.kk[:, :, 0:T], b.kk[:, :, 0:T], tmp[:], ALU.mult))
            for z in range(2):
                v.wait_ge(a_done, (z + 1) * PAIRS)
                qa, ke = b.qa[:, z, :, 0:T], b.ke[:, z, :, 0:T]
                link(v.tensor_scalar(qa, qa, 0.5, 0.5, ALU.mult, ALU.add))
                for c in range(PAIRS):
                    m = v.tensor_scalar(ke[:, c], qa[:, c], vecs[:, 5, c:c + 1], one_ka[:, c:c + 1], ALU.mult, ALU.add)
                link(m)
                link(v.tensor_tensor(ke, ke, f[:, 4:8, :], ALU.mult))
                link(v.tensor_tensor(qa, qa, b.kk[:, :, 0:T], ALU.mult))


def phase_rwkv_scan(nc, a, b, f, T, tag, need_out):
    nch = T // C
    with ExitStack() as ctx:
        sb = alloc(nc, ctx)

        def sem(name):
            return b.semaphore(nc, name + tag)

        def each(name, shape):
            return [sb(f"{name}{g}" + tag, shape) for g in range(2)]

        RW = 3 * C
        pr, qs, ks, vs = (each(n, [P, PAIRS, w]) for n, w in (("pr", RW), ("qs", C), ("ks", C), ("vs", C)))
        ginv = each("ginv", [P, PAIRS, C])
        lt, mt, at, bt, qt, kt, vv = (each(n, [P, PAIRS, C]) for n in ("lt", "mt", "at", "bt", "qt", "kt", "vv"))
        xx, rr, uu, st = (each(n, [P, PAIRS, C]) for n in ("xx", "rr", "uu", "st"))
        tt = each("tt", [P, PAIRS, 2, C])
        tm = each("tm", [P, PAIRS, C])
        psw = [[ctx.enter_context(nc.psum_tensor(f"ps_rs{g}{k}" + tag, [P, 2, 512], F32)) for k in range(2)]
               for g in range(2)]
        pe_names = ["Q", "K", "LV"] + [x + str(s) for s in LEVELS for x in "XY"] + ["R", "U"] + ["O"] * need_out + ["S"]
        dve_names = (["gi", "p", "q", "k"] + ["rho"] * need_out + ["tt_m", "tt"] + ["bt"] * need_out + ["mt"]
                     + ["at"] * need_out + ["t_m", "t"] + [x + str(s) for s in LEVELS for x in "xy"] + ["s1", "s2"])
        act_names = ["vs", "lt", "qt", "kt", "v", "r", "u"] + ["out"] * need_out
        pe_s = [Steps(sem(f"rws_pe{g}"), pe_names) for g in range(2)]
        dve_s = [Steps(sem(f"rws_dve{g}"), dve_names) for g in range(2)]
        act_s = [Steps(sem(f"rws_act{g}"), act_names) for g in range(2)]
        unit, state_in = sem("rws_unit"), sem("rws_state")
        turn = sem("rws_turn")
        block = ctx.enter_context(nc.Block())

        def start_of(i, g, stride, base=0):
            return i * stride + base if g == 0 else i * (-stride) + ((nch - 1) * stride + base)

        def mask(g, m, shape):
            ap = b.masks[:, g, m, :]
            for _ in shape[1:-1]:
                ap = ap.unsqueeze(1)
            return ap.to_broadcast(shape)

        def wide(g, k, lo):
            return psw[g][k][:, :, 0:2 * RW].rearrange("p b (m x) -> p b m x", x=RW)[:, :, :, lo:lo + C]

        def quad(t):
            return t[:].rearrange("p (b m) x -> p b m x", b=2)

        @block.scalar
        def _(act):
            for g in range(2):
                act_s[g].start(act)
                act.activation(pr[g][:, :, 2 * C:], b.unit[:].unsqueeze(1).to_broadcast([P, PAIRS, C]),
                               ACT.Copy).then_inc(unit, 1)
            with act.Fori(0, nch) as i:
                for g in range(2):
                    pe_s[g].wait_last(act, i)
                    act_s[g].mark(act.activation(vs[g][:], f[:, 8:12, bass.ds(start_of(i, g, C), C)], ACT.Copy))
                for g in range(2):
                    pe_s[g].wait(act, i, "Q")
                    dve_s[g].wait(act, i, "bt" if need_out else "tt_m")
                    act_s[g].mark(act.activation(quad(lt[g]), wide(g, 0, 0), ACT.Copy))
                    act_s[g].mark(act.activation(quad(qt[g]), wide(g, 0, 2 * C), ACT.Copy, scale=-1.0))
                for g in range(2):
                    pe_s[g].wait(act, i, "K")
                    dve_s[g].wait(act, i, "at" if need_out else "mt")
                    act_s[g].mark(act.activation(quad(kt[g]), wide(g, 1, 2 * C), ACT.Copy))
                for g in range(2):
                    pe_s[g].wait(act, i, "LV")
                    dve_s[g].wait(act, i, "t_m")
                    act_s[g].mark(act.activation(vv[g][:], psw[g][0][:, 0, :].rearrange(
                        "p (m x) -> p m x", m=PAIRS)[:, :, C:], ACT.Copy))
                for g in range(2):
                    pe_s[g].wait(act, i, "R")
                    act_s[g].mark(act.activation(rr[g][:], psw[g][0][:, 0, 0:PAIRS * C].rearrange(
                        "p (m x) -> p m x", m=PAIRS), ACT.Copy))
                for g in range(2):
                    pe_s[g].wait(act, i, "U")
                    act_s[g].mark(act.activation(uu[g][:], psw[g][1][:, 1, 0:PAIRS * C].rearrange(
                        "p (m x) -> p m x", m=PAIRS), ACT.Copy))
                if need_out:
                    for g in range(2):
                        pe_s[g].wait(act, i, "O")
                        act_s[g].mark(act.activation(b.rwo[:, g, :, bass.ds(start_of(i, g, C), C)],
                                                     psw[g][0][:, 0, 0:PAIRS * C].rearrange("p (m x) -> p m x", m=PAIRS),
                                                     ACT.Copy))

        @block.tensor
        def _(pe):
            for g in range(2):
                pe_s[g].start(pe)

            def heads():
                return ((m, h * C) for m in range(PAIRS) for h in range(2))

            pe.wait_ge(unit, 2)
            with pe.Fori(0, nch) as i:
                for k, (name, step, buf) in enumerate((("Q", "q", qs), ("K", "k", ks))):
                    for g in range(2):
                        if k == 0:
                            dve_s[g].wait(pe, i, "rho" if need_out else "k")
                            act_s[g].wait_last(pe, i)
                        pe.sem_inc(turn, 1)
                        for m, h in heads():
                            mm = pe.matmul(psw[g][k][h:h + C, m // 2, (m % 2) * RW:(m % 2 + 1) * RW],
                                           buf[g][h:h + C, m, :], pr[g][h:h + C, m, :], start=True, stop=True)
                        pe_s[g].mark(mm)
                for g in range(2):
                    dve_s[g].wait(pe, i, "bt" if need_out else "tt")
                    act_s[g].wait(pe, i, "qt")
                    pe.sem_inc(turn, 1)
                    for m, h in heads():
                        pe.matmul(psw[g][0][h:h + C, 0, m * 2 * C:m * 2 * C + C], pr[g][h:h + C, m, 0:C],
                                  qs[g][h:h + C, m, :], start=True, stop=True)
                        mm = pe.matmul(psw[g][0][h:h + C, 0, m * 2 * C + C:(m + 1) * 2 * C], vs[g][h:h + C, m, :],
                                       b.unit[h:h + C, :], start=True, stop=True)
                    pe_s[g].mark(mm)
                last = "t"
                for s in LEVELS:
                    for g in range(2):
                        dve_s[g].wait(pe, i, last)
                        pe.sem_inc(turn, 1)
                        for m, h in heads():
                            mm = pe.matmul(psw[g][0][h:h + C, 1, m * C:(m + 1) * C], lt[g][h:h + C, m, :],
                                           tt[g][h:h + C, m, 0, :], start=True, stop=True)
                        pe_s[g].mark(mm)
                    for g in range(2):
                        dve_s[g].wait(pe, i, f"x{s}")
                        if s == LEVELS[0]:
                            act_s[g].wait(pe, i, "kt")
                        pe.sem_inc(turn, 1)
                        for m, h in heads():
                            pe.matmul(psw[g][1][h:h + C, 0, m * 2 * C:m * 2 * C + C], tt[g][h:h + C, m, 1, :],
                                      xx[g][h:h + C, m, :], start=True, stop=True)
                            mm = pe.matmul(psw[g][1][h:h + C, 0, m * 2 * C + C:(m + 1) * 2 * C], xx[g][h:h + C, m, :],
                                           tt[g][h:h + C, m, 1, :], start=True, stop=True)
                        pe_s[g].mark(mm)
                    last = f"y{s}"
                for g in range(2):
                    act_s[g].wait(pe, i, "v")
                    pe.sem_inc(turn, 1)
                    for m, h in heads():
                        o = psw[g][0][h:h + C, 0, m * C:(m + 1) * C]
                        pe.matmul(o, pr[g][h:h + C, m, 0:C], st[g][h:h + C, m, :], start=True, stop=False)
                        mm = pe.matmul(o, mt[g][h:h + C, m, :], vv[g][h:h + C, m, :], start=False, stop=True)
                    pe_s[g].mark(mm)
                for g in range(2):
                    dve_s[g].wait(pe, i, last)
                    act_s[g].wait(pe, i, "r")
                    pe.sem_inc(turn, 1)
                    for m, h in heads():
                        mm = pe.matmul(psw[g][1][h:h + C, 1, m * C:(m + 1) * C], tt[g][h:h + C, m, 1, :],
                                       rr[g][h:h + C, m, :], start=True, stop=True)
                    pe_s[g].mark(mm)
                for g in range(2):
                    act_s[g].wait(pe, i, "u")
                    pe.sem_inc(turn, 1)
                    if need_out:
                        for m, h in heads():
                            o = psw[g][0][h:h + C, 0, m * C:(m + 1) * C]
                            pe.matmul(o, st[g][h:h + C, m, :], pr[g][h:h + C, m, C:2 * C], start=True, stop=False)
                            pe.matmul(o, vv[g][h:h + C, m, :], at[g][h:h + C, m, :], start=False, stop=False)
                            mm = pe.matmul(o, uu[g][h:h + C, m, :], bt[g][h:h + C, m, :], start=False, stop=True)
                        pe_s[g].mark(mm)
                    for m, h in heads():
                        o = psw[g][1][h:h + C, 1, m * C:(m + 1) * C]
                        pe.matmul(o, kt[g][h:h + C, m, :], vv[g][h:h + C, m, :], start=True, stop=False)
                        mm = pe.matmul(o, qt[g][h:h + C, m, :], uu[g][h:h + C, m, :], start=False, stop=True)
                    pe_s[g].mark(mm)

        @block.vector
        def _(v):
            for g in range(2):
                dve_s[g].start(v)
                if not need_out:
                    v.memset(pr[g][:, :, C:2 * C], 0.0).then_inc(state_in, 1)
                    v.memset(st[g][:], 0.0).then_inc(state_in, 1)
                else:
                    v.tensor_copy(st[g][:], b.state[:, g]).then_inc(state_in, 1)
            v.wait_ge(state_in, 2 if need_out else 4)
            small = [P, PAIRS, C]
            four = [P, 2, 2, C]
            with v.Fori(0, nch) as i:
                for g in range(2):
                    t0, g0 = start_of(i, g, C), start_of(i, g, C + 1)
                    cur = b.G[:, g, :, bass.ds(start_of(i, g, C + 1, 1 - g), C)]
                    prev = b.G[:, g, :, bass.ds(start_of(i, g, C + 1, g), C)]
                    if True:
                        pe_s[g].wait_last(v, i)
                        dve_s[g].wait_last(v, i)
                    dve_s[g].mark(v.reciprocal(ginv[g][:], cur))
                    dve_s[g].mark(v.tensor_tensor(pr[g][:, :, 0:C], b.kk[:, :, bass.ds(t0, C)], prev, ALU.mult))
                    dve_s[g].wait(v, i, "gi")
                    dve_s[g].mark(v.tensor_tensor(qs[g][:], b.qa[:, g, :, bass.ds(t0, C)], ginv[g][:], ALU.mult))
                    dve_s[g].mark(v.tensor_tensor(ks[g][:], b.ke[:, g, :, bass.ds(t0, C)], ginv[g][:], ALU.mult))
                    if need_out:
                        dve_s[g].mark(v.tensor_tensor(pr[g][:, :, C:2 * C], f[:, 0:4, bass.ds(t0, C)], cur, ALU.mult))
                for g in range(2):
                    pe_s[g].wait(v, i, "Q")
                    dve_s[g].mark(v.tensor_tensor(quad(tm[g]), wide(g, 0, 0), mask(g, M_NEG1_ST, four), ALU.mult))
                    dve_s[g].wait(v, i, "tt_m")
                    dve_s[g].mark(v.tensor_tensor(tt[g][:, :, 1, :], tm[g][:],
                                                  b.unit[:].unsqueeze(1).to_broadcast(small), ALU.add))
                    if need_out:
                        dve_s[g].mark(v.tensor_tensor(quad(bt[g]), wide(g, 0, C), mask(g, M_NEG_INCL, four), ALU.mult))
                for g in range(2):
                    pe_s[g].wait(v, i, "K")
                    dve_s[g].mark(v.tensor_tensor(quad(mt[g]), wide(g, 1, 0), mask(g, M_STRICT, four), ALU.mult))
                    if need_out:
                        dve_s[g].mark(v.tensor_tensor(quad(at[g]), wide(g, 1, C), mask(g, M_INCL, four), ALU.mult))
                for g in range(2):
                    pe_s[g].wait(v, i, "LV")
                    dve_s[g].wait(v, i, "tt")
                    dve_s[g].mark(v.tensor_tensor(tm[g][:], psw[g][0][:, 0, :].rearrange(
                        "p (m x) -> p m x", m=PAIRS)[:, :, 0:C], mask(g, M_NEG1_TS, small), ALU.mult))
                    dve_s[g].wait(v, i, "t_m")
                    dve_s[g].mark(v.tensor_tensor(tt[g][:, :, 0, :], tm[g][:],
                                                  b.unit[:].unsqueeze(1).to_broadcast(small), ALU.add))
                for n, s in enumerate(LEVELS):
                    for g in range(2):
                        pe_s[g].wait(v, i, f"X{s}")
                        dve_s[g].mark(v.tensor_tensor(xx[g][:], psw[g][0][:, 1, 0:PAIRS * C].rearrange(
                            "p (m x) -> p m x", m=PAIRS), mask(g, M_OFF + n, small), ALU.mult))
                    for g in range(2):
                        pe_s[g].wait(v, i, f"Y{s}")
                        dve_s[g].mark(v.tensor_tensor(tt[g][:].rearrange("p m k x -> p (m k x)"),
                                                      tt[g][:].rearrange("p m k x -> p (m k x)"),
                                                      psw[g][1][:, 0, :], ALU.subtract))
                for g in range(2):
                    pe_s[g].wait(v, i, "S")
                    dve_s[g].mark(v.tensor_tensor(tm[g][:], psw[g][1][:, 1, 0:PAIRS * C].rearrange(
                        "p (m x) -> p m x", m=PAIRS), st[g][:], ALU.add))
                    dve_s[g].wait(v, i, "s1")
                    dve_s[g].mark(v.tensor_tensor(
                        st[g][:], tm[g][:],
                        b.G[:, g, :, bass.ds(start_of(i, g, C + 1, C * (1 - g)), 1)].to_broadcast(small), ALU.mult))
            if not need_out:
                for g in range(2):
                    dve_s[g].wait_last(v, nch)
                    v.tensor_copy(b.state[:, g], st[g][:]).then_inc(state_in, 1)


def phase_rwkv_output(nc, a, b):
    f = b.fX
    with ExitStack() as ctx:
        sb = alloc(nc, ctx)

        def sem(name):
            return b.semaphore(nc, name)

        g_up = sb("g_up", [P, D_RWKV])
        vecs = sb("rwo_vecs", [P, 3, PAIRS])
        sq = sb("rwo_sq", [P, 2, PAIRS, TX])
        bonus = sb("rwo_bonus", [P, PAIRS, TX])
        gd = sb("rwo_gd", [P, TX])
        ps = [ctx.enter_context(nc.psum_tensor(f"ps_ro{k}", [P, TX], F32)) for k in range(8)]
        vec_in, tanh_done, gd_done = sem("rwo_in"), sem("rwo_tanh"), sem("rwo_gd_done")
        bonus_in, mean_mm, centred, squared = sem("rwo_bonus_in"), sem("rwo_mean"), sem("rwo_centred"), sem("rwo_squared")
        var_mm, rooted, gate_mm, evac, dve = (sem("rwo_var"), sem("rwo_root"), sem("rwo_gate"), sem("rwo_evac"),
                                              sem("rwo_dve"))
        block = ctx.enter_context(nc.Block())
        units = [(z, c) for z in range(2) for c in range(PAIRS)]

        @block.sync
        def _(sp):
            sp.dma_start(g_up[:], a["g_up"]).then_inc(vec_in, 16)
            sp.dma_start(vecs[:], a["rwo_vecs"]).then_inc(vec_in, 16)

        @block.scalar
        def _(act):
            act.activation(gd[:], f[:, 13, :], ACT.Tanh, scale=0.5).then_inc(tanh_done, 1)
            for n, (z, c) in enumerate(units):
                act.wait_ge(centred, n + 1)
                act.activation(sq[:, z, c], b.rwo[:, z, c], ACT.Square).then_inc(squared, 1)
            for n, (z, c) in enumerate(units):
                act.wait_ge(var_mm, n + 1)
                act.activation(sq[:, z, c], ps[n % 4][:], ACT.Sqrt, bias=b.eps[:, 1:2], scale=1.0 / C).then_inc(rooted, 1)

        @block.tensor
        def _(pe):
            for n, (z, c) in enumerate(units):
                if n >= 4:
                    pe.wait_ge(centred, n - 3)
                pe.matmul(ps[n % 4][:], b.block_ones[:], b.rwo[:, z, c], start=True, stop=True).then_inc(mean_mm, 1)
            for n, (z, c) in enumerate(units):
                pe.wait_ge(squared, n + 1)
                if n < 4:
                    pe.wait_ge(centred, n + 5)
                else:
                    pe.wait_ge(rooted, n - 3)
                pe.matmul(ps[n % 4][:], b.block_ones[:], sq[:, z, c], start=True, stop=True).then_inc(var_mm, 1)
            pe.wait_ge(bonus_in, 1)
            for c in range(PAIRS):
                mm = pe.matmul(ps[4 + c][:], b.block_ones[:], bonus[:, c], start=True, stop=True)
            mm.then_inc(gate_mm, 1)
            pe.wait_ge(vec_in, 32)
            pe.wait_ge(gd_done, 1)
            pe.wait_ge(evac, 1)
            for c in range(PAIRS):
                mm = pe.matmul(ps[4 + c][:], g_up[:, c * P:(c + 1) * P], gd[:], start=True, stop=True)
            mm.then_inc(gate_mm, 1)

        @block.vector
        def _(v):
            link = Count(v, dve)
            for n, (z, c) in enumerate(units):
                v.wait_ge(mean_mm, n + 1)
                v.scalar_tensor_tensor(out=b.rwo[:, z, c], in0=ps[n % 4][:], scalar=-1.0 / C, in1=b.rwo[:, z, c],
                                       op0=ALU.mult, op1=ALU.add).then_inc(centred, 1)
            link(v.tensor_tensor(bonus[:], b.ke[:, 0], b.ke[:, 1], ALU.add))
            link(v.tensor_tensor(bonus[:], bonus[:], f[:, 0:4, :], ALU.mult))
            v.wait_ge(vec_in, 32)
            for c in range(PAIRS):
                m = v.tensor_scalar(bonus[:, c], bonus[:, c], vecs[:, 0, c:c + 1], None, ALU.mult)
            m.then_inc(bonus_in, 1)
            v.wait_ge(tanh_done, 1)
            v.tensor_scalar(gd[:], gd[:], 0.5, 0.5, ALU.mult, ALU.add).then_inc(gd_done, 1)
            v.wait_ge(rooted, 8)
            link(v.reciprocal(sq[:], sq[:]))
            link(v.tensor_tensor(sq[:], sq[:], b.rwo[:], ALU.mult))
            link(v.tensor_tensor(b.ya[:], sq[:, 0], sq[:, 1], ALU.add))
            link(v.tensor_scalar(vecs[:, 2, :], vecs[:, 2, :], 2.0, None, ALU.mult))
            for c in range(PAIRS):
                m = v.tensor_scalar(b.ya[:, c], b.ya[:, c], vecs[:, 1, c:c + 1], vecs[:, 2, c:c + 1], ALU.mult, ALU.add)
            link(m)
            v.wait_ge(gate_mm, 1)
            for c in range(PAIRS):
                m = v.tensor_tensor(bonus[:, c], ps[4 + c][:], f[:, 8 + c, :], ALU.mult)
            m.then_inc(evac, 1)
            v.wait_ge(evac, 1)
            link(v.tensor_tensor(b.ya[:], b.ya[:], bonus[:], ALU.add))
            v.wait_ge(gate_mm, 2)
            for c in range(PAIRS):
                m = v.tensor_tensor(b.ya[:, c], ps[4 + c][:], b.ya[:, c], ALU.mult)
            link(m)


NEG_M, INTER, FLOOR = 0, 1, 2
COL_C, COL_W = 0, 1
LN_MAX = 85.0
UNITS = 2 * MH


def phase_mlstm_gates(nc, a, b):
    T = TX + TC
    NCH = T // MC
    with ExitStack() as ctx:
        sb = alloc(nc, ctx)

        def sem(name):
            return b.semaphore(nc, name)

        sg = sb("gate_scan", [GROWS, 2, T])
        bias = sb("gate_bias", [GROWS, 2])
        resets = sb("gate_resets", [GROWS, 2, NCH, MC])
        bsum = sb("gate_b", [GROWS, T])
        m = sb("gate_m", [GROWS, T])
        mp = sb("gate_mprev", [GROWS, NCH])
        c2 = sb("gate_c2", [GROWS, T])
        rows = sb("gate_rows", [GROWS, 5, T])
        ident = sb("gate_ident", [GROWS, GROWS])
        ps_t = ctx.enter_context(nc.psum_tensor("ps_gt", [P, 512], F32))
        small_in, dve, act_done, t_done = sem("mlg_in"), sem("mlg_dve"), sem("mlg_act"), sem("mlg_t")
        want = [sem(f"mlg_want{k}") for k in range(3)]
        rows_done = sem("mlg_rows")
        mod = Modulation(nc, ctx, a, b, "_2", MOD_FIRST, MOD_TILES, b.acc[0:2, :, :])
        n_mod = MOD_TILES - MOD_FIRST
        block = ctx.enter_context(nc.Block())
        f, ig = sg[:, 1, :], sg[:, 0, :]

        @block.sync
        def _(sp):
            sp.dma_start(bias[:], a["gate_bias"]).then_inc(small_in, 16)
            sp.dma_start(resets[:], a["gate_resets"]).then_inc(small_in, 16)
            sp.dma_start(ident[:], a["ident"][0:GROWS, 0:GROWS]).then_inc(small_in, 16)
            sp.dma_start(b.select[:], a["select"]).then_inc(small_in, 16)
            sp.dma_start(b.m_mask[:], a["m_mask"]).then_inc(small_in, 16)
            mod.load_bias(sp)
            for n in range(n_mod):
                mod.load(sp, n)

        @block.scalar
        def _(act):
            act.wait_ge(want[0], 1)
            act.activation(bsum[:], f, ACT.Abs).then_inc(act_done, 1)
            act.wait_ge(act_done, 1)
            act.activation(bsum[:], bsum[:], ACT.Exp, scale=-1.0).then_inc(act_done, 1)
            act.wait_ge(act_done, 2)
            act.activation(bsum[:], bsum[:], ACT.Ln, bias=1.0).then_inc(act_done, 1)
            for n in range(2):
                mod.copy_row(act, n)
            act.wait_ge(want[1], 1)
            act.activation(rows[:, INTER], rows[:, INTER], ACT.Exp).then_inc(act_done, 1)
            act.activation(rows[:, FLOOR], rows[:, FLOOR], ACT.Exp, scale=-1.0).then_inc(act_done, 1)
            act.activation(rows[:, 4], rows[:, 4], ACT.Exp).then_inc(act_done, 1)
            for n in range(2, n_mod):
                mod.copy_row(act, n)

        @block.vector
        def _(v):
            link = Count(v, dve)
            for lo, hi, rev in ((0, 32, False), (32, GROWS, True)):
                for dst, src in (((0, TC), (TX, T)), ((TC, T), (0, TX))):
                    s = b.gates[lo:hi, :, src[0]:src[1]]
                    m_ = v.tensor_copy(sg[lo:hi, :, dst[0]:dst[1]], s[:, :, ::-1] if rev else s)
            link(m_)
            v.wait_ge(small_in, 80)
            link(v.tensor_scalar(ig, ig, bias[:, 0:1], None, ALU.add))
            v.tensor_scalar(f, f, bias[:, 1:2], None, ALU.add).then_inc(want[0], 1)
            v.wait_ge(act_done, 3)
            link(v.scalar_tensor_tensor(out=f, in0=f, scalar=0.0, in1=bsum[:], op0=ALU.min, op1=ALU.subtract))
            link(v.tensor_tensor_scan(out=m[:], data0=f, data1=ig, initial=0.0, op0=ALU.add, op1=ALU.max))
            link(v.tensor_tensor_scan(out=bsum[:], data0=resets[:, 0].rearrange("p n t -> p (n t)"), data1=f,
                                      initial=0.0, op0=ALU.mult, op1=ALU.add))
            link(v.tensor_tensor(rows[:, 3], ig, bsum[:], ALU.subtract))
            link(v.memset(mp[:, 0:1], 0.0))
            link(v.tensor_copy(mp[:, 1:], m[:, MC - 1:T - 1:MC]))
            link(v.tensor_copy(c2[:], rows[:, 3]))
            link(v.tensor_tensor(c2[:, 0:T:MC], c2[:, 0:T:MC], mp[:], ALU.max))
            link(v.tensor_tensor_scan(out=rows[:, NEG_M], data0=resets[:, 1].rearrange("p n t -> p (n t)"),
                                      data1=c2[:], initial=0.0, op0=ALU.add, op1=ALU.max))
            big = [GROWS, NCH, MC]

            def chunks(ap):
                return ap.rearrange("p (n t) -> p n t", t=MC)

            link(v.tensor_tensor(chunks(rows[:, INTER]), mp[:].unsqueeze(2).to_broadcast(big),
                                 chunks(rows[:, NEG_M]), ALU.subtract))
            link(v.tensor_tensor(chunks(rows[:, 4]), chunks(rows[:, 3]),
                                 chunks(rows[:, NEG_M])[:, :, MC - 1:MC].to_broadcast(big), ALU.subtract))
            link(v.tensor_scalar(rows[:, FLOOR], m[:], -LN_MAX, None, ALU.max))
            v.tensor_scalar(rows[:, NEG_M], rows[:, NEG_M], -1.0, None, ALU.mult).then_inc(want[1], 1)
            v.wait_ge(want[1], 1)
            v.wait_ge(act_done, 6)
            for lo, hi in ((0, 32), (32, GROWS)):
                for k in range(5):
                    src = chunks(rows[lo:hi, k])
                    dst = (b.g_rows[lo:hi, k] if k < 3 else b.g_turn[lo:hi, k - 3])
                    m_ = v.tensor_copy(chunks(dst), src[:, :, ::-1] if lo else src)
            m_.then_inc(rows_done, 1)
            v.wait_ge(t_done, 1)
            v.tensor_copy(b.g_cols[:].rearrange("p n k r -> p (n k r)"),
                          ps_t[:, 0:NCH * 2 * GROWS]).then_inc(want[2], 1)
            mod.add_bias(v)

        @block.tensor
        def _(pe):
            for n in range(4):
                mod.multiply(pe, n)
            pe.wait_ge(rows_done, 1)
            for n in range(NCH):
                for k in range(2):
                    o = (n * 2 + k) * GROWS
                    t = pe.transpose(ps_t[:, o:o + GROWS], b.g_turn[:, k, n * MC:(n + 1) * MC], ident[:])
            t.then_inc(t_done, 1)
            for n in range(4, n_mod):
                mod.multiply(pe, n)
            mod.turn(pe)


def phase_mlstm(nc, a, b, q, T, v0, n0, tag, need_out):
    nch = T // MC
    with ExitStack() as ctx:
        sb = alloc(nc, ctx)

        def sem(name):
            return b.semaphore(nc, name + tag)

        kz = sb("kz" + tag, [P, 2, MH, MC])
        qc = sb("qc" + tag, [P, 2, MH // 2, MC])
        vc = sb("vc" + tag, [P, 2, MH, DV + 1])
        ktw = sb("ktw" + tag, [P, 2, P])
        pw = sb("pw" + tag, [P, 2, MC])
        qa = sb("mqa" + tag, [P, 2, MC])
        ab = sb("mab" + tag, [P, 2, MC])
        ps_b, ps_s, ps_n, ps_c = ([ctx.enter_context(nc.psum_tensor(f"ps_{n}{k}" + tag, [P, 512], F32))
                                   for k in range(2)] for n in ("mb", "ms", "mn", "mc"))

        def pipelined(first, second):
            names = []
            for u in range(UNITS + 1):
                if u < UNITS:
                    names += [f"{x}{u}" for x in first]
                if u:
                    names += [f"{x}{u - 1}" for x in second]
            return names

        pool_names = [x for z in range(2) for x in [f"k{z}0", f"k{z}1"] + [f"q{z}"] * need_out + [f"v{z}"]]
        pe_names = pipelined(["S"], ["N"])
        if need_out:
            act_names = pipelined(["kt", "e"], ["ab"])
            dve_names = []
            for u in range(UNITS + 1):
                dve_names += [f"m{u}", f"qa{u}"] * (u < UNITS)
                dve_names += [f"{x}{u - 1}" for x in ("mx", "rc", "h", "c")] * (u > 0)
                dve_names += [f"P{u}"] * (u < UNITS)
        else:
            act_names = [f"kt{u}" for u in range(UNITS)]
            dve_names = [f"c{u}" for u in range(UNITS)]
        pool_s, pe_s, act_s, dve_s = (Steps(sem(n), names) for n, names in (
            ("mls_pool", pool_names), ("mls_pe", pe_names), ("mls_act", act_names), ("mls_dve", dve_names)))
        zeroed, state_in = sem("mls_zero"), sem("mls_state")
        block = ctx.enter_context(nc.Block())
        units = [(u, u // MH, u % MH) for u in range(UNITS)]

        def start_of(i, z):
            return i * MC if z == 0 else i * (-MC) + (nch - 1) * MC

        def chunk_of(i, z):
            return i if z == 0 else i * (-1) + (nch - 1)

        @block.gpsimd
        def _(g):
            pool_s.start(g)
            g.memset(kz[:], 0.0).then_inc(zeroed, 1)
            g.wait_ge(zeroed, 1)
            with g.Fori(0, nch) as i:
                pe_s.wait_last(g, i)
                dve_s.wait_last(g, i)
                for z in range(2):
                    t0 = start_of(i, z)
                    for par in range(2):
                        lo = par * DQK
                        pool_s.mark(g.tensor_copy(kz[lo:lo + DQK, z, par::2, :], q[lo:lo + DQK, 2:4, bass.ds(t0, MC)]))
                        pool_s.wait(g, i, f"k{z}{par}")
                    if need_out:
                        pool_s.mark(g.tensor_copy(qc[:, z], q[:, 0:2, bass.ds(t0, MC)]))
                    pool_s.mark(g.tensor_copy(vc[:, z], b.vM[:, bass.ds(chunk_of(i, z) + v0, 1), :, :].rearrange(
                        "p n h v -> p (n h) v")))
                    pool_s.wait(g, i, f"v{z}")

        @block.tensor
        def _(pe):
            pe_s.start(pe)
            with pe.Fori(0, nch) as i:
                for u, z, h in units + [(UNITS, 0, 0)]:
                    k = u % 2
                    if u < UNITS:
                        if u == 0:
                            pool_s.wait(pe, i, "v1")
                        if u >= 2:
                            dve_s.wait(pe, i, f"c{u - 2}")
                        rows = b.g_rows[:, 1 - need_out:(3 if need_out else 2), bass.ds(i * MC + n0 * MC, MC)]
                        if need_out:
                            pe.matmul(ps_s[k][:, 0:MC], kz[:, z, h, :], qc[:, z, h // 2, :], start=True, stop=True)
                        pe.transpose(ps_s[k][:, MC:2 * MC], kz[:, z, h, :], b.ident[:])
                        pe_s.mark(pe.matmul(ps_b[k][:, (0 if need_out else MC):(3 if need_out else 2) * MC],
                                            b.select[:, u, :], rows, start=True, stop=True))
                    if u:
                        w, zw, hw = units[u - 1]
                        k = w % 2
                        if need_out:
                            dve_s.wait(pe, i, f"P{w}")
                            pe.matmul(ps_n[k][:, 0:MC], vc[:, zw, hw, 0:DV], pw[:, k], start=True, stop=False)
                            pe.matmul(ps_n[k][:, 0:MC], b.mC[:, w, 0:DV], qa[:, k], start=False, stop=True)
                            pe.matmul(ps_n[k][:, MC:2 * MC], b.ones[:], pw[:, k], start=True, stop=False)
                            pe.matmul(ps_n[k][:, MC:2 * MC], b.mC[:, w, DV:DV + 1].to_broadcast([P, P]), qa[:, k],
                                      start=False, stop=True)
                        act_s.wait(pe, i, f"kt{w}")
                        pe_s.mark(pe.matmul(ps_c[k][:, 0:DV + 1], ktw[:, k], vc[:, zw, hw, :], start=True, stop=True))

        @block.scalar
        def _(act):
            act_s.start(act)
            with act.Fori(0, nch) as i:
                for u, z, h in units + [(UNITS, 0, 0)]:
                    k = u % 2
                    if u < UNITS:
                        pe_s.wait(act, i, f"S{u}")
                        row = h + 32 * z
                        act_s.mark(act.activation(ktw[:, k], ps_s[k][:, MC:2 * MC], ACT.Copy,
                                                  scale=b.g_cols[:, bass.ds(i + n0, 1), COL_W, row]))
                        if need_out:
                            dve_s.wait(act, i, f"m{u}")
                            act_s.mark(act.activation(pw[:, k], pw[:, k], ACT.Exp))
                    if u and need_out:
                        k = (u - 1) % 2
                        pe_s.wait(act, i, f"N{u - 1}")
                        act_s.mark(act.activation(ab[:, k], ps_n[k][:, MC:2 * MC], ACT.Abs))

        @block.vector
        def _(v):
            dve_s.start(v)
            if not need_out:
                v.memset(b.mC[:], 0.0).then_inc(state_in, 1)
                v.wait_ge(state_in, 1)
            with v.Fori(0, nch) as i:
                for u, z, h in units + [(UNITS, 0, 0)]:
                    k = u % 2
                    if u < UNITS and need_out:
                        row = h + 32 * z
                        pe_s.wait(v, i, f"S{u}")
                        dve_s.mark(v.scalar_tensor_tensor(out=pw[:, k], in0=ps_b[k][:, 0:MC],
                                                          scalar=b.g_cols[:, bass.ds(i + n0, 1), COL_C, row],
                                                          in1=b.m_mask[:, z], op0=ALU.add, op1=ALU.min))
                        dve_s.mark(v.tensor_tensor(qa[:, k], ps_b[k][:, MC:2 * MC], qc[:, z, h // 2, :], ALU.mult))
                    if u:
                        w, zw, hw = units[u - 1]
                        kw = w % 2
                        pe_s.wait(v, i, f"N{w}")
                        end = MC + (MC - 1 if zw == 0 else 0)
                        if need_out:
                            act_s.wait(v, i, f"ab{w}")
                            dve_s.mark(v.tensor_tensor(ab[:, kw], ab[:, kw], ps_b[kw][:, 2 * MC:3 * MC], ALU.max))
                            dve_s.wait(v, i, f"mx{w}")
                            dve_s.mark(v.reciprocal(ab[:, kw], ab[:, kw]))
                            dve_s.wait(v, i, f"rc{w}")
                            dve_s.mark(v.tensor_tensor(b.mh[:, zw, hw, bass.ds(start_of(i, zw), MC)],
                                                       ps_n[kw][:, 0:MC], ab[:, kw], ALU.mult))
                        dve_s.mark(v.scalar_tensor_tensor(out=b.mC[:, w], in0=b.mC[:, w],
                                                          scalar=ps_b[kw][:, end:end + 1],
                                                          in1=ps_c[kw][:, 0:DV + 1], op0=ALU.mult, op1=ALU.add))
                    if u < UNITS and need_out:
                        act_s.wait(v, i, f"e{u}")
                        dve_s.mark(v.tensor_tensor(pw[:, k], ps_s[k][:, 0:MC], pw[:, k], ALU.mult))


def phase_mlstm_output(nc, a, b):
    with ExitStack() as ctx:
        sb = alloc(nc, ctx)

        def sem(name):
            return b.semaphore(nc, name)

        ng = sb("mlstm_g", [P, MH])
        sq = sb("mlo_sq", [P, 2, MH, TX])
        ps = [ctx.enter_context(nc.psum_tensor(f"ps_mo{k}", [P, TX], F32)) for k in range(8)]
        small_in, squared, mm, rooted, dve = sem("mlo_in"), sem("mlo_sq"), sem("mlo_mm"), sem("mlo_root"), sem("mlo_dve")
        block = ctx.enter_context(nc.Block())
        units = [(z, h) for z in range(2) for h in range(MH)]

        @block.sync
        def _(sp):
            sp.dma_start(ng[:], a["mlstm_g"]).then_inc(small_in, 16)

        @block.scalar
        def _(act):
            for z, h in units:
                act.activation(sq[:, z, h], b.mh[:, z, h], ACT.Square).then_inc(squared, 1)
            for n, (z, h) in enumerate(units):
                act.wait_ge(mm, n + 1)
                act.activation(sq[:, z, h], ps[n][:], ACT.Sqrt, bias=b.eps[:, 0:1], scale=1.0 / DV).then_inc(rooted, 1)

        @block.tensor
        def _(pe):
            for n, (z, h) in enumerate(units):
                pe.wait_ge(squared, n + 1)
                pe.matmul(ps[n][:], b.ones[:], sq[:, z, h], start=True, stop=True).then_inc(mm, 1)

        @block.vector
        def _(v):
            link = Count(v, dve)
            v.wait_ge(small_in, 16)
            v.wait_ge(rooted, 8)
            link(v.reciprocal(sq[:], sq[:]))
            link(v.tensor_tensor(sq[:], sq[:], b.mh[:], ALU.mult))
            link(v.tensor_tensor(sq[:, 0], sq[:, 0], sq[:, 1], ALU.add))
            for h in range(MH):
                v.tensor_scalar(b.yb[:, h, :].rearrange("p (r w) -> p w r", w=GRID_W),
                                sq[:, 0, h].rearrange("p (w r) -> p w r", r=ROWS), ng[:, h:h + 1], None,
                                ALU.mult).then_inc(dve, 1)


def phase_merge(nc, a, b, h_dram):
    with ExitStack() as ctx:
        sb = alloc(nc, ctx)

        def sem(name):
            return b.semaphore(nc, name)

        h = sb("mg_h", [P, KT, TX])
        x = sb("mg_x", [P, KT, TX])
        wo = sb("mg_wo", [P, MH, KT, P])
        ring = sb("mg_ring", [P, 2, 3, KT, P])
        wout = sb("mg_wout", [P, 2, KT, P])
        merged = sb("merged", [P, KT, TX])
        sg = sb("mg_sg", [P, 4, TX])
        sq = sb("mg_sq", [P, KT, TX])
        rs = sb("mg_rs", [P, TX])
        g2 = sb("mg_g2", [P, KT])
        h2 = h
        gt = sb("mg_gt", [P, KT])
        ps = [ctx.enter_context(nc.psum_tensor(f"ps_mg{k}", [P, TX], F32)) for k in range(8)]
        h_in, x_in, g_in, o_in = sem("mg_h_in"), sem("mg_x_in"), sem("mg_g_in"), sem("mg_o_in")
        ring_in = [sem(f"mg_ring{k}") for k in range(2)]
        out_in = [sem(f"mg_out{k}") for k in range(2)]
        o_mm, o_tanh = sem("mg_o_mm"), sem("mg_o_tanh")
        m_mm = [sem(f"mg_m_mm{k}") for k in range(2)]
        m_tanh = [sem(f"mg_m_tanh{k}") for k in range(2)]
        m_used = [sem(f"mg_m_used{k}") for k in range(2)]
        w_mm = [sem(f"mg_w_mm{k}") for k in range(2)]
        x_done = [sem(f"mg_x_done{k}") for k in range(2)]
        squared, sum_mm, rooted, dve, pair = sem("mg_sq"), sem("mg_sum"), sem("mg_root"), sem("mg_dve"), sem("mg_pair")
        yb_done, h2_done, h2_hi = sem("mg_yb"), sem("mg_h2_done"), sem("mg_h2_hi")
        block = ctx.enter_context(nc.Block())
        half = KT // 2

        @block.sync
        def _(sp):
            sp.dma_start(h[:], h_dram).then_inc(h_in, 16)
            sp.dma_start(wo[:], a["w_o"]).then_inc(o_in, 16)
            for k in range(2):
                sp.dma_start(ring[:, k], a["w_merge"][k]).then_inc(ring_in[k], 16)
            sp.dma_start(g2[:], a["norm2_g"]).then_inc(g_in, 16)
            sp.dma_start(x[:], a["xT"]).then_inc(x_in, 16)
            with sp.Fori(1, half) as i:
                for k in range(2):
                    sp.wait_ge(m_mm[k], i)
                    sp.dma_start(ring[:, k], a["w_merge"][i * 2 + k]).then_inc(ring_in[k], 16)
            for k in range(2):
                sp.dma_start(wout[:, k], a["w_out"][k]).then_inc(out_in[k], 16)
            with sp.Fori(1, half) as i:
                for k in range(2):
                    sp.wait_ge(w_mm[k], i)
                    sp.dma_start(wout[:, k], a["w_out"][i * 2 + k]).then_inc(out_in[k], 16)

        @block.tensor
        def _(pe):
            pe.wait_ge(h_in, 16)
            pe.wait_ge(o_in, 16)
            for n in range(MH):
                for j in range(KT):
                    mm = pe.matmul(ps[n][:], wo[:, n, j, :], h[:, j, :], start=(j == 0), stop=(j == KT - 1))
                mm.then_inc(o_mm, 1)
            pe.wait_ge(yb_done, 1)
            with pe.Fori(0, half) as i:
                for k in range(2):
                    pe.wait_ge(ring_in[k], i * 16 + 16)
                    pe.wait_ge(m_used[k], i + 1)
                    for n in range(2):
                        for j in range(KT):
                            pe.matmul(ps[4 * k + n][:], ring[:, k, n, j, :], h[:, j, :],
                                      start=(j == 0), stop=(j == KT - 1))
                    for n, y in enumerate((b.ya, b.yb)):
                        for j in range(4):
                            mm = pe.matmul(ps[4 * k + 2 + n][:], ring[:, k, 2, 4 * n + j, :], y[:, j, :],
                                           start=(j == 0), stop=(j == 3))
                    mm.then_inc(m_mm[k], 1)
            for k in range(2):
                pe.wait_ge(m_used[k], half + 1)
            with pe.Fori(0, half) as i:
                for k in range(2):
                    pe.wait_ge(out_in[k], i * 16 + 16)
                    pe.wait_ge(x_done[k], i + 1)
                    for j in range(KT):
                        mm = pe.matmul(ps[4 * k][:], wout[:, k, j, :], merged[:, j, :], start=(j == 0), stop=(j == KT - 1))
                    mm.then_inc(w_mm[k], 1)
            for j in range(KT):
                pe.wait_ge(squared, j + 1)
                mm = pe.matmul(ps[1][:], b.ones[:], sq[:, j, :], start=(j == 0), stop=(j == KT - 1))
            mm.then_inc(sum_mm, 1)

        @block.scalar
        def _(act):
            for n in range(MH):
                act.wait_ge(o_mm, n + 1)
                act.activation(sg[:, n], ps[n][:], ACT.Tanh, scale=0.5).then_inc(o_tanh, 1)
            act.wait_ge(yb_done, 1)
            with act.Fori(0, half) as i:
                for k in range(2):
                    act.wait_ge(m_mm[k], i + 1)
                    act.wait_ge(m_used[k], i + 1)
                    for n in range(2):
                        m = act.activation(sg[:, 2 * k + n], ps[4 * k + n][:], ACT.Tanh, scale=0.5)
                    m.then_inc(m_tanh[k], 1)
            for j in range(KT):
                act.wait_ge(x_done[j % 2], j // 2 + 2)
                act.activation(sq[:, j], b.x1[:, j], ACT.Square).then_inc(squared, 1)
            act.wait_ge(sum_mm, 1)
            act.activation(rs[:], ps[1][:], ACT.Sqrt, bias=b.eps[:, 0:1], scale=1.0 / D).then_inc(rooted, 1)
            for j in range(KT):
                act.wait_ge(h2_done, j + 1)
                act.activation(b.h2h[:, j], h2[:, j], ACT.Copy).then_inc(h2_hi, 1)

        @block.vector
        def _(v):
            link = Count(v, dve)
            for k in range(2):
                v.sem_inc(m_used[k], 1)
                v.sem_inc(x_done[k], 1)
            for n in range(MH):
                v.wait_ge(o_tanh, n + 1)
                m = v.scalar_tensor_tensor(out=b.yb[:, n], in0=sg[:, n], scalar=1.0, in1=b.yb[:, n],
                                           op0=ALU.add, op1=ALU.mult)
            link(m)
            v.tensor_scalar(b.yb[:], b.yb[:], 0.5, None, ALU.mult).then_inc(yb_done, 1)
            v.wait_ge(yb_done, 1)
            link(v.tensor_scalar(gt[:], b.mod[:, 2 * KT:3 * KT, 0], 0.5, None, ALU.mult))
            with v.Fori(0, half) as i:
                for k in range(2):
                    v.wait_ge(m_tanh[k], i + 1)
                    for n in range(2):
                        m = v.scalar_tensor_tensor(out=sg[:, 2 * k + n], in0=sg[:, 2 * k + n], scalar=1.0,
                                                   in1=ps[4 * k + 2 + n][:], op0=ALU.add, op1=ALU.mult)
                    m.then_inc(pair, 1)
                    v.wait_ge(pair, i * 2 + k + 1)
                    v.tensor_tensor(merged[:, bass.ds(i * 2 + k, 1), :], sg[:, 2 * k:2 * k + 1], sg[:, 2 * k + 1:2 * k + 2],
                                    ALU.add).then_inc(m_used[k], 1)
            v.wait_ge(x_in, 16)
            with v.Fori(0, half) as i:
                for k in range(2):
                    v.wait_ge(w_mm[k], i + 1)
                    t = i * 2 + k
                    v.scalar_tensor_tensor(out=b.x1[:, bass.ds(t, 1), :], in0=ps[4 * k][:].unsqueeze(1),
                                           scalar=gt[:, bass.ds(t, 1)], in1=x[:, bass.ds(t, 1), :],
                                           op0=ALU.mult, op1=ALU.add).then_inc(x_done[k], 1)
            for k in range(2):
                v.wait_ge(x_done[k], half + 1)
            v.wait_ge(g_in, 16)
            link(v.scalar_tensor_tensor(out=g2[:], in0=b.mod[:, 4 * KT:5 * KT, 0], scalar=1.0, in1=g2[:],
                                        op0=ALU.add, op1=ALU.mult))
            v.wait_ge(rooted, 1)
            link(v.reciprocal(rs[:], rs[:]))
            for j in range(KT):
                link(v.scalar_tensor_tensor(out=h2[:, j], in0=b.x1[:, j], scalar=g2[:, j:j + 1], in1=rs[:],
                                            op0=ALU.mult, op1=ALU.mult))
                v.tensor_scalar(h2[:, j], h2[:, j], b.mod[:, 3 * KT + j, 0:1], None, ALU.add).then_inc(h2_done, 1)
            for j in range(KT):
                v.wait_ge(h2_hi, j + 1)
                v.tensor_tensor(b.h2l[:, j], h2[:, j], b.h2h[:, j], ALU.subtract).then_inc(dve, 1)


TT = TX // P
LOW = -3.0e38


def phase_route(nc, a, b):
    with ExitStack() as ctx:
        sb = alloc(nc, ctx)

        def sem(name):
            return b.semaphore(nc, name)

        keys = sb("keys", [P, 2 * PH, NK])
        ring = sb("wq_ring", [P, 2, KT, P])
        wh, wl = sb("wq_hi", [P, 2, KT, P], F32R), sb("wq_lo", [P, 2, KT, P], F32R)
        qT = sb("q_T", [P, 2, TX])
        S = sb("scores", [P, 2, 2, TT, NK])
        left = sb("scores_left", [P, TT, 2, NK])
        top = sb("top", [P, TT, 2, TOPK])
        ix = sb("top_ix", [P, TT, 2, TOPK], U32)
        cand = sb("cand", [P, TT, TOPK, TOPK])
        cleft = sb("cand_left", [P, TT, TOPK * TOPK])
        ctop = sb("cand_top", [P, TT, TOPK])
        cix = sb("cand_top_ix", [P, TT, TOPK], U32)
        ps_q = [ctx.enter_context(nc.psum_tensor(f"ps_q{k}", [P, TX], F32)) for k in range(2)]
        ps_s = [ctx.enter_context(nc.psum_tensor(f"ps_sc{k}", [P, TT, NK], F32)) for k in range(2)]
        keys_in = sem("rt_keys")
        ring_in = [sem(f"rt_ring{k}") for k in range(2)]
        w_hi = [sem(f"rt_w_hi{k}") for k in range(2)]
        w_lo = [sem(f"rt_w_lo{k}") for k in range(2)]
        q_mm = [sem(f"rt_q_mm{k}") for k in range(2)]
        q_out = [sem(f"rt_q_out{k}") for k in range(2)]
        s_mm = [sem(f"rt_s_mm{k}") for k in range(2)]
        s_out = [sem(f"rt_s_out{k}") for k in range(2)]
        s_free = [sem(f"rt_s_free{k}") for k in range(2)]
        groups = ("max1", "ix1", "left", "max2", "ix2", "cand", "cmax1", "cix1", "cleft", "cmax2", "cix2", "keep")
        dve_s = Steps(sem("rt_dve"), [f"{x}{hh}" for hh in range(2) for x in groups])
        turn = sem("rt_turn")
        block = ctx.enter_context(nc.Block())

        @block.sync
        def _(sp):
            for k in range(2):
                sp.dma_start(ring[:, k], a["w_q"][k]).then_inc(ring_in[k], 16)
            sp.dma_start(keys[:], a["keys"]).then_inc(keys_in, 16)
            with sp.Fori(1, PH) as i:
                for k in range(2):
                    sp.wait_ge(w_lo[k], i)
                    sp.dma_start(ring[:, k], a["w_q"][i * 2 + k]).then_inc(ring_in[k], 16)

        @block.gpsimd
        def _(g):
            with g.Fori(0, PH) as i:
                for k in range(2):
                    g.wait_ge(w_hi[k], i + 1)
                    g.tensor_tensor(wl[:, k], ring[:, k], wh[:, k], ALU.subtract).then_inc(w_lo[k], 1)

        @block.tensor
        def _(pe):
            pe.wait_ge(keys_in, 16)
            with pe.Fori(0, PH) as i:
                for k in range(2):
                    pe.wait_ge(w_lo[k], i + 1)
                    pe.wait_ge(q_out[k], i + 1)
                    for j in range(KT):
                        mm = product(pe, ps_q[k][:], wh[:, k, j, :], wl[:, k, j, :], b.h2h[:, j, :], b.h2l[:, j, :],
                                     j == 0, j == KT - 1)
                    mm.then_inc(q_mm[k], 1)
                for k in range(2):
                    pe.wait_ge(q_out[k], i + 2)
                    pe.wait_ge(s_out[k], i + 1)
                    for t in range(TT):
                        mm = pe.matmul(ps_s[k][:, t, :], qT[:, k, t * P:(t + 1) * P],
                                       keys[:, bass.ds(i * 2 + k, 1), :].rearrange("p o n -> p (o n)"),
                                       start=True, stop=True)
                    mm.then_inc(s_mm[k], 1)

        @block.scalar
        def _(act):
            for k in range(2):
                act.sem_inc(q_out[k], 1)
                act.sem_inc(s_out[k], 1)
            with act.Fori(0, PH // 2) as i:
                for hh in range(2):
                    for k in range(2):
                        act.wait_ge(ring_in[k], i * 32 + (hh + 1) * 16)
                        act.wait_ge(q_out[k], i * 2 + (hh + 1))
                        act.activation(wh[:, k], ring[:, k], ACT.Copy).then_inc(w_hi[k], 1)
                    for k in range(2):
                        act.wait_ge(q_mm[k], i * 2 + (hh + 1))
                        act.activation(qT[:, k], ps_q[k][:], ACT.Copy).then_inc(q_out[k], 1)
                    act.wait_ge(s_free[hh], i + 1)
                    for k in range(2):
                        act.wait_ge(s_mm[k], i * 2 + (hh + 1))
                        act.activation(S[:, hh, k], ps_s[k][:], ACT.Copy).then_inc(s_out[k], 1)

        @block.vector
        def _(v):
            dve_s.start(v)
            for hh in range(2):
                v.sem_inc(s_free[hh], 1)
            both = [(t, p) for t in range(TT) for p in range(2)]

            def when(i, name, gate=None):
                dve_s.wait(v, i, name)
                v.sem_inc(turn if gate is None else gate, 1)

            with v.Fori(0, PH // 2) as i:
                for hh in range(2):
                    s = S[:, hh]
                    for k in range(2):
                        v.wait_ge(s_out[k], i * 2 + (hh + 2))
                        v.sem_inc(turn, 1)
                    for t, p in both:
                        m = v.max(top[:, t, p, 0:8], s[:, p, t, :])
                    dve_s.mark(m)
                    when(i, f"max1{hh}")
                    for t, p in both:
                        m = v.max_index(ix[:, t, p, 0:8], top[:, t, p, 0:8], s[:, p, t, :])
                    dve_s.mark(m)
                    for t, p in both:
                        m = v.match_replace(left[:, t, p], top[:, t, p, 0:8], s[:, p, t, :], LOW)
                    dve_s.mark(m)
                    when(i, f"left{hh}", s_free[hh])
                    for t, p in both:
                        m = v.max(top[:, t, p, 8:16], left[:, t, p])
                    dve_s.mark(m)
                    when(i, f"max2{hh}")
                    for t, p in both:
                        m = v.max_index(ix[:, t, p, 8:16], top[:, t, p, 8:16], left[:, t, p])
                    dve_s.mark(m)
                    for t in range(TT):
                        m = v.tensor_tensor(cand[:, t], top[:, t, 0, :].unsqueeze(2).to_broadcast([P, TOPK, TOPK]),
                                            top[:, t, 1, :].unsqueeze(1).to_broadcast([P, TOPK, TOPK]), ALU.add)
                    dve_s.mark(m)
                    when(i, f"cand{hh}")
                    flat = [cand[:, t].rearrange("p a c -> p (a c)") for t in range(TT)]
                    for t in range(TT):
                        m = v.max(ctop[:, t, 0:8], flat[t])
                    dve_s.mark(m)
                    when(i, f"cmax1{hh}")
                    for t in range(TT):
                        m = v.max_index(cix[:, t, 0:8], ctop[:, t, 0:8], flat[t])
                    dve_s.mark(m)
                    for t in range(TT):
                        m = v.match_replace(cleft[:, t], ctop[:, t, 0:8], flat[t], LOW)
                    dve_s.mark(m)
                    when(i, f"cleft{hh}")
                    for t in range(TT):
                        m = v.max(ctop[:, t, 8:16], cleft[:, t])
                    dve_s.mark(m)
                    when(i, f"cmax2{hh}")
                    for t in range(TT):
                        m = v.max_index(cix[:, t, 8:16], ctop[:, t, 8:16], cleft[:, t])
                    dve_s.mark(m)
                    when(i, f"cix2{hh}")
                    head = bass.ds(i * 2 + hh, 1)
                    for p in range(2):
                        v.tensor_copy(b.IX[:, p, :, head, :].rearrange("p t o k -> p t (o k)"), ix[:, :, p, :])
                    v.tensor_copy(b.CI[:, :, head, :].rearrange("p t o k -> p t (o k)"), cix[:])
                    dve_s.mark(v.tensor_copy(b.SC[:, :, head, :].rearrange("p t o k -> p t (o k)"), ctop[:]))


def phase_slots(nc, a, b):
    N = TT * PH
    with ExitStack() as ctx:
        sb = alloc(nc, ctx)

        def sem(name):
            return b.semaphore(nc, name)

        half_ix = sb("cand_half", [P, 2, N, TOPK], U32)
        half_f = sb("cand_half_f", [P, 2, N, TOPK])
        eq = sb("pick", [P, N, TOPK, TOPK])
        idx = sb("slot_src", [P, 3, TT, PH * TOPK])
        total = sb("soft_total", [P, N])
        iota = sb("iota16", [P, TOPK])
        ps = [ctx.enter_context(nc.psum_tensor(f"ps_sl{k}", [P, TX], F32)) for k in range(3)]
        small_in, sub_done, exp_done, dve, src_done, turned, out = (
            sem(f"sl_{n}") for n in ("in", "sub", "exp", "dve", "src", "turned", "out"))
        block = ctx.enter_context(nc.Block())
        sc = b.SC[:].rearrange("p t h k -> p (t h) k")
        w = idx[:, 2].rearrange("p t (h k) -> p (t h) k", k=TOPK)

        @block.sync
        def _(sp):
            sp.dma_start(iota[:], a["iota"][:, 0:TOPK]).then_inc(small_in, 16)

        @block.scalar
        def _(act):
            act.wait_ge(sub_done, 1)
            act.activation(w, w, ACT.Exp).then_inc(exp_done, 1)

        @block.vector
        def _(v):
            link = Count(v, dve)
            v.tensor_tensor(w, sc, sc[:, :, 0:1].to_broadcast([P, N, TOPK]), ALU.subtract).then_inc(sub_done, 1)
            ci = b.CI[:].rearrange("p t h k -> p (t h) k")
            link(v.tensor_scalar(half_ix[:, 0], ci, 4, None, ALU.logical_shift_right))
            link(v.tensor_scalar(half_ix[:, 1], ci, TOPK - 1, None, ALU.bitwise_and))
            link(v.tensor_copy(half_f[:], half_ix[:]))
            v.wait_ge(small_in, 16)
            for side in range(2):
                link(v.tensor_tensor(eq[:], half_f[:, side].unsqueeze(3).to_broadcast([P, N, TOPK, TOPK]),
                                     iota[:].unsqueeze(1).unsqueeze(1).to_broadcast([P, N, TOPK, TOPK]), ALU.is_equal))
                link(v.tensor_tensor(eq[:], eq[:], b.IX[:, side].rearrange("p t h k -> p (t h) k").unsqueeze(2)
                                     .to_broadcast([P, N, TOPK, TOPK]), ALU.mult))
                link(v.tensor_reduce(idx[:, side].rearrange("p t s -> p (t s)"),
                                     eq[:].rearrange("p n k m -> p (n k) m"), AX.X, ALU.add))
            v.wait_ge(exp_done, 1)
            link(v.tensor_reduce(total[:], w, AX.X, ALU.add))
            link(v.reciprocal(total[:], total[:]))
            v.tensor_tensor(w, w, total[:].unsqueeze(2).to_broadcast([P, N, TOPK]), ALU.mult).then_inc(src_done, 1)
            v.wait_ge(turned, 3)
            for k in range(3):
                v.tensor_copy(b.slots[:, k], ps[k][:]).then_inc(out, 1)

        @block.tensor
        def _(pe):
            pe.wait_ge(src_done, 1)
            for k in range(3):
                for t in range(TT):
                    m = pe.transpose(ps[k][:, t * P:(t + 1) * P], idx[:, k, t, :], b.ident[:])
                m.then_inc(turned, 1)


def phase_weights(nc, a, b, w_dram):
    SUB = 4
    HALF = 64
    LOOPS = HALF // (2 * SUB)
    with ExitStack() as ctx:
        sb = alloc(nc, ctx)

        def sem(name):
            return b.semaphore(nc, name)

        iota = sb("iota128", [P, NK])
        oi = sb("onehot_i", [P, 2, SUB, NK])
        oj = sb("onehot_j", [P, 2, SUB, NK])
        wb = sb("w_block", [P, 2, NK, HALF])
        ps = [ctx.enter_context(nc.psum_tensor(f"ps_w{k}", [P, SUB, NK], F32)) for k in range(2)]
        small_in = sem("w_in")
        built, mm, evac = ([sem(f"w_{n}{k}") for k in range(2)] for n in ("built", "mm", "evac"))
        stored = [sem(f"w_stored{k}") for k in range(2)]
        block = ctx.enter_context(nc.Block())
        dst = w_dram.rearrange("j i (n t) -> n i j t", t=HALF)
        n_outer = TX // (2 * HALF)

        @block.sync
        def _(sp):
            sp.dma_start(iota[:], a["iota"]).then_inc(small_in, 16)
            for half in range(2):
                sp.sem_inc(stored[half], 16)
            with sp.Fori(0, n_outer) as o:
                for half in range(2):
                    for s in range(2):
                        sp.wait_ge(evac[s], o * (2 * LOOPS) + ((half + 1) * LOOPS + 1))
                    sp.dma_start(dst[o * 2 + half], wb[:, half]).then_inc(stored[half], 16)
            for half in range(2):
                sp.wait_ge(stored[half], 16 * (n_outer + 1))

        def tokens(eng, body):
            with eng.Fori(0, n_outer) as o:
                for half in range(2):
                    with eng.Fori(0, LOOPS) as g:
                        for s in range(2):
                            body(o, half, g, s, o * (2 * LOOPS) + g + half * LOOPS)

        @block.vector
        def _(v):
            for s in range(2):
                v.sem_inc(built[s], 1)
            v.wait_ge(small_in, 16)

            def body(o, half, g, s, n):
                v.wait_ge(mm[s], n + 1)
                for k in range(SUB):
                    t = o * (2 * HALF) + g * (2 * SUB) + (half * HALF + s * SUB + k)
                    v.tensor_scalar(oi[:, s, k], iota[:], b.slots[:, 0, bass.ds(t, 1)],
                                    b.slots[:, 2, bass.ds(t, 1)], ALU.is_equal, ALU.mult)
                    m = v.tensor_scalar(oj[:, s, k], iota[:], b.slots[:, 1, bass.ds(t, 1)], None, ALU.is_equal)
                m.then_inc(built[s], 1)

            tokens(v, body)

        @block.tensor
        def _(pe):
            for s in range(2):
                pe.sem_inc(mm[s], 1)

            def body(o, half, g, s, n):
                pe.wait_ge(built[s], n + 2)
                pe.wait_ge(evac[s], n + 1)
                for k in range(SUB):
                    m = pe.matmul(ps[s][:, k, :], oi[:, s, k], oj[:, s, k], start=True, stop=True)
                m.then_inc(mm[s], 1)

            tokens(pe, body)

        @block.scalar
        def _(act):
            for s in range(2):
                act.sem_inc(evac[s], 1)

            def body(o, half, g, s, n):
                act.wait_ge(mm[s], n + 2)
                act.wait_ge(stored[half], o * 16 + 16)
                act.activation(wb[:, half, :, bass.ds(g * (2 * SUB) + s * SUB, SUB)].rearrange("p j t -> p t j"),
                               ps[s][:], ACT.Copy).then_inc(evac[s], 1)

            tokens(act, body)


def phase_experts(nc, a, b, w_dram):
    G = 4
    RAW = 2
    rounds = NK // G
    half = G // RAW
    with ExitStack() as ctx:
        sb = alloc(nc, ctx)

        def sem(name):
            return b.semaphore(nc, name)

        u_raw, v_raw = sb("u_raw", [P, RAW, KT * P]), sb("v_raw", [P, RAW, D])
        uh, ul = sb("u_hi", [P, G, KT * P], F32R), sb("u_lo", [P, G, KT * P], F32R)
        vh, vl = sb("v_hi", [P, G, D], F32R), sb("v_lo", [P, G, D], F32R)
        wr = sb("w_ring", [P, G, TX])
        ga = sb("act", [P, G, TX])
        gh, gl = sb("act_hi", [P, G, TX], F32R), sb("act_lo", [P, G, TX], F32R)
        ps_a = [ctx.enter_context(nc.psum_tensor(f"ps_a{g}", [P, TX], F32)) for g in range(G)]
        ps_y = [ctx.enter_context(nc.psum_tensor(f"ps_y{k}", [P, TX], F32)) for k in range(4)]
        u_in, v_in = ([sem(f"ex_{n}{k}") for k in range(RAW)] for n in ("u_in", "v_in"))
        w_in = [sem(f"ex_w_in{g}") for g in range(G)]
        u_hi, u_lo, v_hi, v_lo, a_mm, gelu, gated, g_hi, g_lo, y_mm, y_add, zeroed = (sem(f"ex_{n}") for n in (
            "u_hi", "u_lo", "v_hi", "v_lo", "a_mm", "gelu", "gated", "g_hi", "g_lo", "y_mm", "y_add", "zeroed"))
        block = ctx.enter_context(nc.Block())

        def in_rounds(eng, body):
            with eng.Fori(0, rounds - 1) as i:
                body(i, True)
            body(rounds - 1, False)

        def j_tile(ap, i, g):
            return ap[i * G + g]

        @block.sync
        def _(sp):
            def load_u(i, g, wait=True):
                if wait:
                    sp.wait_ge(u_lo, i * G + (g - RAW + 1))
                sp.dma_start(u_raw[:, g % RAW], j_tile(a["uT"], i, g)).then_inc(u_in[g % RAW], 16)

            def load_vw(i, first=False):
                for g in range(G):
                    if not first:
                        sp.wait_ge(gated, i * G + (g - G + 1))
                    sp.dma_start(wr[:, g], j_tile(w_dram, i, g)).then_inc(w_in[g], 16)
                for g in range(G):
                    if not first or g >= RAW:
                        sp.wait_ge(v_lo, i * G + (g - RAW + 1))
                    sp.dma_start(v_raw[:, g % RAW], j_tile(a["v"], i, g)).then_inc(v_in[g % RAW], 16)

            for g in range(G):
                load_u(0, g, g >= RAW)
            load_vw(0, first=True)
            with sp.Fori(1, rounds) as i:
                for g in range(G):
                    load_u(i, g)
                load_vw(i)

        @block.scalar
        def _(act):
            def split_u(i, g):
                act.wait_ge(u_in[g % RAW], (i * half + (g // RAW + 1)) * 16)
                act.activation(uh[:, g], u_raw[:, g % RAW], ACT.Copy).then_inc(u_hi, 1)

            for g in range(G):
                split_u(0, g)

            def body(i, more):
                for g in range(G):
                    act.wait_ge(a_mm, i * G + (g + 1))
                    act.activation(ga[:, g], ps_a[g][:], ACT.Gelu).then_inc(gelu, 1)
                    act.wait_ge(v_in[g % RAW], (i * half + (g // RAW + 1)) * 16)
                    act.activation(vh[:, g], v_raw[:, g % RAW], ACT.Copy).then_inc(v_hi, 1)
                    act.wait_ge(gated, i * G + (g + 1))
                    act.activation(gh[:, g], ga[:, g], ACT.Copy).then_inc(g_hi, 1)
                if more:
                    for g in range(G):
                        split_u(i + 1, g)

            in_rounds(act, body)

        @block.vector
        def _(v):
            def split_u(i, g):
                v.wait_ge(u_hi, i * G + (g + 1))
                v.tensor_tensor(ul[:, g], u_raw[:, g % RAW], uh[:, g], ALU.subtract).then_inc(u_lo, 1)

            for g in range(G):
                split_u(0, g)
            v.memset(b.acc[:], 0.0).then_inc(zeroed, 1)
            v.wait_ge(zeroed, 1)
            v.sem_inc(y_add, KT)

            def body(i, more):
                for g in range(G):
                    v.wait_ge(w_in[g], i * 16 + 16)
                    v.wait_ge(gelu, i * G + (g + 1))
                    v.tensor_tensor(ga[:, g], ga[:, g], wr[:, g], ALU.mult).then_inc(gated, 1)
                    v.wait_ge(v_hi, i * G + (g + 1))
                    v.tensor_tensor(vl[:, g], v_raw[:, g % RAW], vh[:, g], ALU.subtract).then_inc(v_lo, 1)
                    v.wait_ge(g_hi, i * G + (g + 1))
                    v.tensor_tensor(gl[:, g], ga[:, g], gh[:, g], ALU.subtract).then_inc(g_lo, 1)
                for m in range(KT):
                    v.wait_ge(y_mm, i * KT + (m + 1))
                    v.wait_ge(y_add, i * KT + (m + 1))
                    v.tensor_tensor(b.acc[:, m], b.acc[:, m], ps_y[m % 4][:], ALU.add).then_inc(y_add, 1)
                    if more and m % 2:
                        split_u(i + 1, m // 2)

            in_rounds(v, body)

        @block.tensor
        def _(pe):
            def body(i, more):
                for g in range(G):
                    pe.wait_ge(u_lo, i * G + (g + 1))
                    for j in range(KT):
                        w = slice(j * P, (j + 1) * P)
                        mm = product(pe, ps_a[g][:], uh[:, g, w], ul[:, g, w], b.h2h[:, j, :], b.h2l[:, j, :],
                                     j == 0, j == KT - 1)
                    mm.then_inc(a_mm, 1)
                for m0 in range(0, KT, 4):
                    for gs in ((0, 1, 2), (3,)) if m0 == 0 else ((0, 1, 2, 3),):
                        for m in range(m0, m0 + 4):
                            if gs[0] == 0:
                                pe.wait_ge(y_add, i * KT + (m + 5))
                            for g in gs:
                                if m == 0 or g == 3:
                                    pe.wait_ge(g_lo, i * G + (g + 1))
                                w = slice(m * P, (m + 1) * P)
                                mm = product(pe, ps_y[m % 4][:], vh[:, g, w], vl[:, g, w], gh[:, g], gl[:, g],
                                             g == 0, g == G - 1)
                            if gs[-1] == G - 1:
                                mm.then_inc(y_mm, 1)

            in_rounds(pe, body)


def phase_final(nc, a, b, out):
    with ExitStack() as ctx:
        sb = alloc(nc, ctx)

        def sem(name):
            return b.semaphore(nc, name)

        fg = sb("final_g", [P, KT])
        sq = sb("fin_sq", [P, KT, TX])
        rs = sb("fin_rs", [P, TX])
        ps = ctx.enter_context(nc.psum_tensor("ps_fin", [P, TX], F32))
        small_in, x_done, squared, summed, rooted, dve, y_done, stored = (
            sem(f"fin_{n}") for n in ("in", "x", "sq", "sum", "root", "dve", "y", "stored"))
        block = ctx.enter_context(nc.Block())

        @block.sync
        def _(sp):
            sp.dma_start(fg[:], a["final_g"]).then_inc(small_in, 16)
            for j in range(KT):
                sp.wait_ge(y_done, j + 1)
                sp.dma_start(out[:, j, :], b.acc[:, j]).then_inc(stored, 16)
            sp.wait_ge(stored, 16 * KT)

        @block.vector
        def _(v):
            link = Count(v, dve)
            for j in range(KT):
                v.scalar_tensor_tensor(out=b.x1[:, j], in0=b.acc[:, j], scalar=b.mod[:, 5 * KT + j, 0:1],
                                       in1=b.x1[:, j], op0=ALU.mult, op1=ALU.add).then_inc(x_done, 1)
            v.wait_ge(small_in, 16)
            v.wait_ge(rooted, 1)
            link(v.reciprocal(rs[:], rs[:]))
            v.wait_ge(x_done, KT)
            for j in range(KT):
                v.scalar_tensor_tensor(out=b.acc[:, j], in0=b.x1[:, j], scalar=fg[:, j:j + 1], in1=rs[:],
                                       op0=ALU.mult, op1=ALU.mult).then_inc(y_done, 1)

        @block.scalar
        def _(act):
            for j in range(KT):
                act.wait_ge(x_done, j + 1)
                act.activation(sq[:, j], b.x1[:, j], ACT.Square).then_inc(squared, 1)
            act.wait_ge(summed, 1)
            act.activation(rs[:], ps[:], ACT.Sqrt, bias=b.eps[:, 0:1], scale=1.0 / D).then_inc(rooted, 1)

        @block.tensor
        def _(pe):
            for j in range(KT):
                pe.wait_ge(squared, j + 1)
                mm = pe.matmul(ps[:], b.ones[:], sq[:, j], start=(j == 0), stop=(j == KT - 1))
            mm.then_inc(summed, 1)


def build_program(nc, a, out):
    with ExitStack() as ctx:
        sb = alloc(nc, ctx)
        b = Buffers()
        b.ones = sb("ones", [P, P])
        b.eps = sb("eps", [P, 4])
        b.masks = sb("rwkv_masks", [P, 2, N_MASKS, C])
        b.unit = sb("unit", [P, C])
        b.block_ones = sb("block_ones", [P, P])
        b.ident = sb("ident", [P, P])
        b.mod = sb("mod", [P, N_MOD * KT, 2])
        b.silu_c = sb("silu_c", [P, KT, 2])
        const = ctx.enter_context(nc.semaphore("const_done"))
        const_in = ctx.enter_context(nc.semaphore("const_in"))
        with nc.Block() as block:
            @block.gpsimd
            def _(g):
                g.memset(b.ones[:], 1.0).then_inc(const, 1)
                g.memset(b.eps[:, 0:1], NORM_EPS).then_inc(const, 1)
                g.memset(b.eps[:, 1:2], GN_EPS).then_inc(const, 1)
                g.memset(b.eps[:, 2:3], -HALF_DECAY).then_inc(const, 1)
                g.wait_ge(const, 4)

            @block.sync
            def _(sp):
                sp.dma_start(b.masks[:], a["rwkv_masks"]).then_inc(const_in, 16)
                sp.dma_start(b.unit[:], a["unit"]).then_inc(const_in, 16)
                sp.dma_start(b.block_ones[:], a["block_ones"]).then_inc(const_in, 16)
                sp.dma_start(b.ident[:], a["ident"]).then_inc(const_in, 16)
                sp.wait_ge(const_in, 64)
        b.acc = sb("mixed", [P, KT, TX])
        b.ya, b.yb = b.acc[:, 0:PAIRS], b.acc[:, PAIRS:]
        h_dram = nc.dram_tensor("h_scratch", [P, KT, TX], F32, kind="Internal").ap()
        with ExitStack() as mixers:
            sm = alloc(nc, mixers)
            b.fX = sm("fX", [P, RW_TILES, TX])
            b.fC = sm("fC", [P, RW_TILES, TC])
            with ExitStack() as ml:
                sl = alloc(nc, ml)
                b.qX = sl("qX", [P, QK_TILES, TX])
                b.qC = sl("qC", [P, QK_TILES, TC])
                b.vM = sl("vM", [P, (TX + TC) // MC, MH, DV + 1])
                b.gates = sl("gates", [GROWS, 2, TX + TC])
                with ExitStack() as norm:
                    sn = alloc(nc, norm)
                    b.hh, b.hl = sn("h_hi", [P, KT, TX + TC], F32R), sn("h_lo", [P, KT, TX + TC], F32R)
                    phase_modulation(nc, a, b, h_dram)
                    b.hf = sn("h_both", [P, KT, TX + TC])
                    phase_projection(nc, a, b)
                    phase_values(nc, a, b)
                b.g_rows = sl("g_rows", [GROWS, 3, TX + TC])
                b.g_turn = sl("g_turn", [GROWS, 2, TX + TC])
                b.g_cols = sl("g_cols", [P, (TX + TC) // MC, 2, GROWS])
                b.select = sl("select", [GROWS, UNITS, P])
                b.m_mask = sl("m_mask", [P, 2, MC])
                b.mC = sl("mC", [P, UNITS, DV + 1])
                b.mh = sl("mh", [P, 2, MH, TX])
                phase_mlstm_gates(nc, a, b)
                phase_mlstm(nc, a, b, b.qC, TC, TX // MC, 0, "_c", False)
                phase_mlstm(nc, a, b, b.qX, TX, 0, TC // MC, "_x", True)
                phase_mlstm_output(nc, a, b)
            with ExitStack() as rw:
                sr = alloc(nc, rw)
                b.kk = sr("kk", [P, PAIRS, TX])
                b.ke = sr("ke", [P, 2, PAIRS, TX])
                b.qa = sr("qa", [P, 2, PAIRS, TX])
                b.G = sr("G", [P, 2, PAIRS, TX // C * (C + 1)])
                b.state = sr("rw_state", [P, 2, PAIRS, C])
                phase_rwkv_features(nc, a, b, b.fC, TC, "_c")
                phase_rwkv_scan(nc, a, b, b.fC, TC, "_c", False)
                phase_rwkv_features(nc, a, b, b.fX, TX, "_x")
                b.rwo = sr("rwo", [P, 2, PAIRS, TX])
                phase_rwkv_scan(nc, a, b, b.fX, TX, "_x", True)
                phase_rwkv_output(nc, a, b)
        w_dram = nc.dram_tensor("w_scratch", [NK, P, TX], F32, kind="Internal").ap()
        b.x1 = sb("x1", [P, KT, TX])
        b.h2h = sb("h2_hi", [P, KT, TX], F32R)
        b.h2l = sb("h2_lo", [P, KT, TX], F32R)
        b.clear_semaphores(nc)
        phase_merge(nc, a, b, h_dram)
        with ExitStack() as route:
            st = alloc(nc, route)
            b.slots = st("slots", [P, 3, TX])
            b.IX = st("IX", [P, 2, TT, PH, TOPK])
            b.CI = st("CI", [P, TT, PH, TOPK], U32)
            b.SC = st("SC", [P, TT, PH, TOPK])
            phase_route(nc, a, b)
            phase_slots(nc, a, b)
            phase_weights(nc, a, b, w_dram)
        b.clear_semaphores(nc)
        phase_experts(nc, a, b, w_dram)
        phase_final(nc, a, b, out)


def column(v):
    return v.reshape(-1, P).T


def weight_tiles(w):
    k, n = w.shape
    return w.reshape(k // P, P, n // P, P).transpose(2, 1, 0, 3)


def turned(x):
    return x.T.reshape(-1, P, x.shape[0]).transpose(1, 0, 2)


def laid_out(x, c, ctx, c_ctx, ada_w, ada_b, norm1_g, w_in, rwkv_conv, rwkv_w0, rwkv_w_up, rwkv_a0,
             rwkv_a_up, rwkv_g_up, rwkv_k_k, rwkv_k_a, rwkv_r_k, rwkv_ln_w, rwkv_ln_b, mlstm_conv,
             mlstm_i_b, mlstm_f_b, mlstm_norm_g, w_branch_a, w_branch_b, w_out, norm2_g, peer_wq,
             peer_keys, peer_u, peer_v, final_g):
    rw_cols = RW_TILES * P
    ends = np.cumsum([rw_cols, 2 * MH * DQK, MH * DV, 2 * MH, 2 * MH, MH * DV, D, D])
    w_rw, w_qk, w_mv, w_i, w_f, w_o, w_ga, w_gb = np.split(w_in[0], ends[:-1], axis=1)
    gates = np.zeros((D, 2, GROWS), w_in.dtype)
    gate_bias = np.zeros((GROWS, 2), w_in.dtype)
    for k, (w, bias) in enumerate(((w_i, mlstm_i_b[0]), (w_f, mlstm_f_b[0]))):
        for z in range(2):
            gates[:, k, 32 * z:32 * z + MH] = w[:, z * MH:(z + 1) * MH]
            gate_bias[32 * z:32 * z + MH, k] = bias[z]
    w_ab = np.concatenate([w_branch_a[0], w_branch_b[0]], 0)
    merge = np.stack([weight_tiles(w_ga), weight_tiles(w_gb), weight_tiles(w_ab)], 2)
    r = np.arange(P)
    mask = np.zeros((P, 2, MC), np.float32)
    mask[:, 0] = np.where(r[:, None] <= r[None, :], 0.0, NEG)
    mask[:, 1] = np.where(r[:, None] >= r[None, :], 0.0, NEG)
    resets = np.zeros((GROWS, 2, (TX + TC) // MC, MC), np.float32)
    resets[:, 0, :, 1:] = 1.0
    resets[:, 1, :, 0] = NEG
    select = np.zeros((GROWS, UNITS, P), np.float32)
    for u in range(UNITS):
        select[u % MH + 32 * (u // MH), u] = 1.0
    return {
        "xT": turned(x[0]), "ctxT": turned(ctx[0]),
        "cc": np.stack([c[0], c_ctx], -1).reshape(KT, P, 2).transpose(1, 0, 2),
        "ada_w": ada_w[0].reshape(KT, P, MOD_TILES, MOD_W).transpose(2, 1, 0, 3), "ada_b": column(ada_b[0]), "norm1_g": column(norm1_g[0]),
        "w_rw": weight_tiles(np.concatenate([w_rw, w_qk], 1)),
        "w_mv": w_mv.reshape(KT, P, MH * DV).transpose(1, 0, 2),
        "w_gates": gates.reshape(KT, P, 2, GROWS).transpose(1, 0, 2, 3),
        "rwkv_conv": rwkv_conv[0].reshape(3, RW_TILES, P).transpose(2, 1, 0),
        "mlstm_conv": mlstm_conv[0].reshape(3, QK_TILES, P).transpose(2, 1, 0),
        "wa_up": np.concatenate([rwkv_w_up[0], rwkv_a_up[0]], 1).transpose(1, 0, 2),
        "rw_vecs": np.stack([column(v) for v in (rwkv_w0[0, 0], rwkv_w0[0, 1], rwkv_a0[0, 0], rwkv_a0[0, 1],
                                                 rwkv_k_k[0], rwkv_k_a[0])], 1),
        "g_up": rwkv_g_up[0],
        "rwo_vecs": np.stack([column(v[0]) for v in (rwkv_r_k, rwkv_ln_w, rwkv_ln_b)], 1),
        "gate_bias": gate_bias, "mlstm_g": column(mlstm_norm_g[0]),
        "w_o": weight_tiles(w_o).transpose(1, 0, 2, 3), "w_merge": merge, "w_out": weight_tiles(w_out[0]),
        "norm2_g": column(norm2_g[0]),
        "w_q": weight_tiles(peer_wq[0]),
        "keys": peer_keys[0].transpose(3, 0, 1, 2).reshape(P, 2 * PH, NK),
        "uT": peer_u[0].reshape(NK, NK, KT, P).transpose(1, 3, 2, 0),
        "v": peer_v[0].reshape(NK, NK, D).transpose(1, 0, 2),
        "final_g": column(final_g),
        "rwkv_masks": rwkv_masks(), "unit": np.tile(np.eye(C, dtype=np.float32), (2, 1)),
        "block_ones": np.kron(np.eye(2, dtype=np.float32), np.ones((C, C), np.float32)),
        "ident": np.eye(P, dtype=np.float32), "gate_resets": resets, "select": select, "m_mask": mask,
        "iota": np.tile(np.arange(NK, dtype=np.float32), (P, 1)),
    }


def kernel(**inputs):
    import concourse.bacc as _bacc
    from concourse.bass_utils import run_bass_kernel_spmd as _run

    nc = _bacc.Bacc("TRN2", target_bir_lowering=False, num_devices=1)
    arrays, args = {}, {}
    for name, v in laid_out(**inputs).items():
        v = np.ascontiguousarray(v)
        arrays[f"in_{name}"] = v
        args[name] = nc.dram_tensor(f"in_{name}", v.shape, mybir.dt.from_np(v.dtype), kind="ExternalInput").ap()
    out = nc.dram_tensor("out_y", (P, KT, TX), F32, kind="ExternalOutput").ap()
    build_program(nc, args, out)
    y = _run(nc, [arrays], core_ids=[0]).results[0]["out_y"]
    return y.transpose(1, 0, 2).reshape(D, TX).T[None]
```

```python
from contextlib import ExitStack

import numpy as np

import concourse.bass as bass
from concourse import mybir

F32 = mybir.dt.float32
F32R = mybir.dt.float32r
U32 = mybir.dt.uint32
ALU = mybir.AluOpType
ACT = mybir.ActivationFunctionType
AX = mybir.AxisListType

P = 128
D = 1024
KT = D // P
TX, TC = 512, 256
GRID_W = 64
ROWS = TX // GRID_W
N_MOD = 6
NORM_EPS = 1e-6
NEG = -1e30

D_RWKV = 512
RW_TILES = 14
PAIRS = 4
C = 64
GN_EPS = 64e-5
DECAY = float(np.exp(-0.5))

MH = 4
DQK, DV = 64, 128
MC = 128
GROWS = 36
QK_TILES = 4

PH, NK, TOPK = 8, 128, 16


class Count:

    def __init__(self, eng, sem):
        self.eng, self.sem, self.n = eng, sem, 0

    def __call__(self, ins):
        ins.then_inc(self.sem, 1)
        self.n += 1
        self.eng.wait_ge(self.sem, self.n)


class Steps:

    def __init__(self, sem, names):
        self.sem, self.names = sem, list(names)

    def start(self, eng):
        eng.sem_inc(self.sem, 1)

    def wait(self, eng, i, name):
        eng.wait_ge(self.sem, i * len(self.names) + (self.names.index(name) + 2))

    def wait_last(self, eng, i):
        eng.wait_ge(self.sem, i * len(self.names) + 1)

    def mark(self, ins):
        ins.then_inc(self.sem, 1)


def product(pe, out, wh, wl, xh, xl, first, last):
    pe.matmul(out, wh, xh, start=first, stop=False)
    pe.matmul(out, wl, xh, start=False, stop=False)
    return pe.matmul(out, wh, xl, start=False, stop=last)


class Buffers:

    def __init__(self):
        self.used = []

    def semaphore(self, nc, name):
        s = nc.alloc_semaphore(name)
        self.used.append(s)
        return s

    def clear_semaphores(self, nc):
        nc.clear_and_free_semaphores(self.used)
        self.used = []
        nc.all_engine_barrier()


def alloc(nc, ctx):
    def sb(name, shape, dt=F32):
        return ctx.enter_context(nc.sbuf_tensor(name, shape, dt))
    return sb


MOD_W = 512
MOD_TILES = N_MOD * D // MOD_W
MOD_FIRST = 2 * D // MOD_W
PER = MOD_W // P


class Modulation:

    def __init__(self, nc, ctx, a, b, tag, lo, hi, row):
        self.a, self.b, self.lo, self.hi = a, b, lo, hi
        self.ring = ctx.enter_context(nc.sbuf_tensor("ada_ring" + tag, [P, 2, KT, MOD_W], F32))
        self.bias = ctx.enter_context(nc.sbuf_tensor("ada_bias" + tag, [P, N_MOD * KT], F32))
        self.row = row
        self.ps_row = [ctx.enter_context(nc.psum_tensor(f"ps_row{k}" + tag, [P, MOD_W], F32)) for k in range(2)]
        self.ps_mod = ctx.enter_context(nc.psum_tensor("ps_mod" + tag, [P, 512], F32))
        self.ring_in = [b.semaphore(nc, f"ada_in{k}" + tag) for k in range(2)]
        self.bias_in, self.mm, self.out, self.turned, self.done = (
            b.semaphore(nc, f"mod_{n}" + tag) for n in ("bias_in", "mm", "row_out", "turned", "done"))

    def load(self, sp, n):
        if n >= 2:
            sp.wait_ge(self.mm, n - 1)
        sp.dma_start(self.ring[:, n % 2], self.a["ada_w"][self.lo + n]).then_inc(self.ring_in[n % 2], 16)

    def load_bias(self, sp):
        sp.dma_start(self.bias[:], self.a["ada_b"]).then_inc(self.bias_in, 16)

    def multiply(self, pe, n):
        pe.wait_ge(self.ring_in[n % 2], (n // 2 + 1) * 16)
        if n >= 2:
            pe.wait_ge(self.out, n - 1)
        for k in range(KT):
            mm = pe.matmul(self.ps_row[n % 2][0:2, :], self.b.silu_c[:, k, :], self.ring[:, n % 2, k, :],
                           start=(k == 0), stop=(k == KT - 1))
        mm.then_inc(self.mm, 1)

    def copy_row(self, act, n):
        act.wait_ge(self.mm, n + 1)
        act.activation(self.row[:, n, :], self.ps_row[n % 2][0:2, :], ACT.Copy).then_inc(self.out, 1)

    def turn(self, pe):
        pe.wait_ge(self.out, self.hi - self.lo)
        for n in range(self.hi - self.lo):
            for q in range(PER):
                o = 2 * (n * PER + q)
                mm = pe.matmul(self.ps_mod[:, o:o + 2], self.row[:, n, q * P:(q + 1) * P], self.b.ident[0:2, 0:2],
                               start=True, stop=True)
        mm.then_inc(self.turned, 1)

    def add_bias(self, v):
        lo, hi = self.lo * PER, self.hi * PER
        v.wait_ge(self.bias_in, 16)
        v.wait_ge(self.turned, 1)
        v.tensor_tensor(self.b.mod[:, lo:hi, :], self.ps_mod[:, 0:2 * (hi - lo)].rearrange("p (g s) -> p g s", s=2),
                        self.bias[:, lo:hi].unsqueeze(2).to_broadcast([P, hi - lo, 2]), ALU.add).then_inc(self.done, 1)
        v.wait_ge(self.done, 1)


def phase_modulation(nc, a, b, h_dram):
    with ExitStack() as ctx:
        sb = alloc(nc, ctx)

        def sem(name):
            return b.semaphore(nc, name)

        cc = sb("cc", [P, KT, 2])
        th = sb("cc_th", [P, KT, 2])
        g1 = sb("g1", [P, KT])
        h = sb("h_f32", [P, KT, TX + TC])
        xx, xc = b.acc, b.fC[:, 0:KT, :]
        rs = sb("rs", [P, TX + TC])
        scale = sb("scale1", [P, 2, KT])
        ps_sx = ctx.enter_context(nc.psum_tensor("ps_sx", [P, TX], F32))
        ps_sc = ctx.enter_context(nc.psum_tensor("ps_sc", [P, 512], F32))
        small_in, x_in, h_out = sem("mod_small_in"), sem("mod_x_in"), sem("mod_h_out")
        tanh_done, silu_done = sem("mod_tanh"), sem("mod_silu")
        sq_done, sum_done, root_done = sem("sq_done"), sem("sum_done"), sem("root_done")
        scaled, shifted, rounded, rest = sem("h_scaled"), sem("h_shifted"), sem("h_rounded"), sem("h_rest")
        dve = sem("mod_dve")
        mod = Modulation(nc, ctx, a, b, "_1", 0, MOD_FIRST, b.qX[0:2, :, :])
        block = ctx.enter_context(nc.Block())

        @block.sync
        def _(sp):
            sp.dma_start(cc[:], a["cc"]).then_inc(small_in, 16)
            sp.dma_start(g1[:], a["norm1_g"]).then_inc(small_in, 16)
            mod.load_bias(sp)
            sp.dma_start(xx[:], a["xT"]).then_inc(x_in, 16)
            sp.dma_start(xc, a["ctxT"]).then_inc(x_in, 16)
            for n in range(MOD_FIRST):
                mod.load(sp, n)
            for j in range(0, KT, 2):
                sp.wait_ge(shifted, j + 2)
                sp.dma_start(h_dram[:, j:j + 2], h[:, j:j + 2, 0:TX]).then_inc(h_out, 16)
            sp.wait_ge(h_out, 16 * (KT // 2))

        @block.scalar
        def _(act):
            act.wait_ge(small_in, 32)
            act.activation(th[:], cc[:], ACT.Tanh, scale=0.5).then_inc(tanh_done, 1)
            act.wait_ge(x_in, 32)
            act.activation(h[:, :, 0:TX], xx[:], ACT.Square).then_inc(sq_done, 1)
            act.activation(h[:, :, TX:], xc, ACT.Square).then_inc(sq_done, 1)
            act.wait_ge(sum_done, 1)
            act.activation(rs[:, 0:TX], ps_sx[:], ACT.Ln, bias=b.eps[:, 0:1], scale=1.0 / D).then_inc(root_done, 1)
            act.activation(rs[:, TX:], ps_sc[:, 0:TC], ACT.Ln, bias=b.eps[:, 0:1], scale=1.0 / D).then_inc(root_done, 1)
            act.wait_ge(root_done, 2)
            act.activation(rs[:], rs[:], ACT.Exp, scale=-0.5).then_inc(root_done, 1)
            for n in range(MOD_FIRST):
                mod.copy_row(act, n)
            for j in range(KT):
                act.wait_ge(scaled, 2 * j + 2)
                for s, (lo, hi) in enumerate(((0, TX), (TX, TX + TC))):
                    m = act.activation(h[:, j, lo:hi], h[:, j, lo:hi], ACT.Identity, bias=b.mod[:, j, s:s + 1])
                m.then_inc(shifted, 1)
                act.wait_ge(shifted, j + 1)
                act.activation(b.hh[:, j], h[:, j], ACT.Copy).then_inc(rounded, 1)

        @block.gpsimd
        def _(g):
            for j in range(0, KT, 2):
                g.wait_ge(rounded, j + 1)
                g.tensor_tensor(b.hl[:, j], h[:, j], b.hh[:, j], ALU.subtract).then_inc(rest, 1)

        @block.tensor
        def _(pe):
            pe.wait_ge(sq_done, 2)
            for k in range(KT):
                pe.matmul(ps_sx[:], b.ones[:], h[:, k, 0:TX], start=(k == 0), stop=(k == KT - 1))
            for k in range(KT):
                mm = pe.matmul(ps_sc[:, 0:TC], b.ones[:], h[:, k, TX:], start=(k == 0), stop=(k == KT - 1))
            mm.then_inc(sum_done, 1)
            pe.wait_ge(silu_done, 1)
            for n in range(MOD_FIRST):
                mod.multiply(pe, n)
            mod.turn(pe)

        @block.vector
        def _(v):
            link = Count(v, dve)
            v.wait_ge(small_in, 32)
            v.wait_ge(tanh_done, 1)
            link(v.scalar_tensor_tensor(out=b.silu_c[:], in0=th[:], scalar=1.0, in1=cc[:], op0=ALU.add, op1=ALU.mult))
            v.tensor_scalar(b.silu_c[:], b.silu_c[:], 0.5, None, ALU.mult).then_inc(silu_done, 1)
            v.wait_ge(root_done, 3)
            mod.add_bias(v)
            for s in range(2):
                link(v.scalar_tensor_tensor(out=scale[:, s], in0=b.mod[:, KT:2 * KT, s], scalar=1.0, in1=g1[:],
                                            op0=ALU.add, op1=ALU.mult))
            for k in range(KT):
                for s, (src, lo, hi) in enumerate(((xx, 0, TX), (xc, TX, TX + TC))):
                    v.scalar_tensor_tensor(out=h[:, k, lo:hi], in0=src[:, k, :], scalar=scale[:, s, k:k + 1],
                                           in1=rs[:, lo:hi], op0=ALU.mult, op1=ALU.mult).then_inc(scaled, 1)
            for j in range(1, KT, 2):
                v.wait_ge(rounded, j + 1)
                v.tensor_tensor(b.hl[:, j], h[:, j], b.hh[:, j], ALU.subtract).then_inc(dve, 1)


def phase_projection(nc, a, b):
    with ExitStack() as ctx:
        sb = alloc(nc, ctx)

        def sem(name):
            return b.semaphore(nc, name)

        ring = sb("win_ring", [P, 2, KT, P])
        wh, wl = sb("win_hi", [P, 2, KT, P], F32R), sb("win_lo", [P, 2, KT, P], F32R)
        cw = sb("conv_r", [P, RW_TILES, 3])
        cq = sb("conv_q", [P, QK_TILES, 3])
        ps_x = [ctx.enter_context(nc.psum_tensor(f"ps_px{k}", [P, TX], F32)) for k in range(2)]
        ps_c = [ctx.enter_context(nc.psum_tensor(f"ps_pc{k}", [P, 512], F32)) for k in range(2)]
        small_in = sem("proj_small_in")
        ring_in = [sem(f"proj_in{k}") for k in range(2)]
        mm_done = [sem(f"proj_mm{k}") for k in range(2)]
        centre = [sem(f"proj_centre{k}") for k in range(2)]
        taps = [sem(f"proj_taps{k}") for k in range(2)]
        w_hi = [sem(f"proj_w_hi{k}") for k in range(2)]
        w_lo = [sem(f"proj_w_lo{k}") for k in range(2)]
        one, col_done = sem("proj_vec"), sem("proj_col")
        n_r, n_q = RW_TILES // 2, QK_TILES // 2
        block = ctx.enter_context(nc.Block())

        @block.gpsimd
        def _(g):
            def rest(i, k):
                g.wait_ge(w_hi[k], i + 1)
                g.tensor_tensor(wl[:, k], ring[:, k], wh[:, k], ALU.subtract).then_inc(w_lo[k], 1)

            def both_parts(j):
                g.tensor_tensor(b.hf[:, j, 0:TX].rearrange("p (w r) -> p w r", r=ROWS),
                                b.hh[:, j, 0:TX].rearrange("p (r w) -> p w r", w=GRID_W),
                                b.hl[:, j, 0:TX].rearrange("p (r w) -> p w r", w=GRID_W), ALU.add).then_inc(col_done, 1)
                g.tensor_tensor(b.hf[:, j, TX:], b.hh[:, j, TX:], b.hl[:, j, TX:], ALU.add).then_inc(col_done, 1)

            for i in range(2):
                for k in range(2):
                    rest(i, k)
                for j in range(KT // 2 * i, KT // 2 * (i + 1)):
                    both_parts(j)
            with g.Fori(2, n_r + n_q) as i:
                for k in range(2):
                    rest(i, k)

        @block.sync
        def _(sp):
            for k in range(2):
                sp.dma_start(ring[:, k], a["w_rw"][k]).then_inc(ring_in[k], 16)
            sp.dma_start(cw[:], a["rwkv_conv"]).then_inc(small_in, 16)
            sp.dma_start(cq[:], a["mlstm_conv"]).then_inc(small_in, 16)
            with sp.Fori(1, n_r + n_q) as i:
                for k in range(2):
                    sp.wait_ge(w_lo[k], i)
                    sp.dma_start(ring[:, k], a["w_rw"][i * 2 + k]).then_inc(ring_in[k], 16)

        @block.tensor
        def _(pe):
            with pe.Fori(0, n_r + n_q) as i:
                for k in range(2):
                    pe.wait_ge(w_lo[k], i + 1)
                    pe.wait_ge(taps[k], i + 1)
                    for out, lo, hi in ((ps_x[k][:], 0, TX), (ps_c[k][:, 0:TC], TX, TX + TC)):
                        for j in range(KT):
                            mm = product(pe, out, wh[:, k, j, :], wl[:, k, j, :], b.hh[:, j, lo:hi], b.hl[:, j, lo:hi],
                                         j == 0, j == KT - 1)
                    mm.then_inc(mm_done[k], 1)

        @block.scalar
        def _(act):
            act.wait_ge(small_in, 32)
            for k in range(2):
                act.sem_inc(taps[k], 1)

            def round_weights(i, k):
                act.wait_ge(ring_in[k], i * 16 + 16)
                act.activation(wh[:, k], ring[:, k], ACT.Copy).then_inc(w_hi[k], 1)

            for k in range(2):
                round_weights(0, k)
            with act.Fori(0, n_r) as i:
                for k in range(2):
                    act.wait_ge(mm_done[k], i + 1)
                    t = i * 2 + k
                    act.activation(b.fX[:, bass.ds(t, 1), :], ps_x[k][:].unsqueeze(1), ACT.Copy,
                                   scale=cw[:, bass.ds(t, 1), 1]).then_inc(centre[k], 1)
                    act.activation(b.fC[:, bass.ds(t, 1), :], ps_c[k][:, 0:TC].unsqueeze(1), ACT.Copy,
                                   scale=cw[:, bass.ds(t, 1), 1]).then_inc(centre[k], 1)
                    round_weights(i + 1, k)
            for i in range(n_q):
                for k in range(2):
                    act.wait_ge(mm_done[k], n_r + i + 1)
                    t = 2 * i + k
                    act.activation(b.qX[:, t, :].rearrange("p (w r) -> p r w", r=ROWS),
                                   ps_x[k][:].rearrange("p (r w) -> p r w", w=GRID_W), ACT.Copy,
                                   scale=cq[:, t, 1:2]).then_inc(centre[k], 1)
                    act.activation(b.qC[:, t, :], ps_c[k][:, 0:TC], ACT.Copy, scale=cq[:, t, 1:2]).then_inc(centre[k], 1)
                    if i < n_q - 1:
                        round_weights(n_r + i + 1, k)

        @block.vector
        def _(v):
            with v.Fori(0, n_r) as i:
                for k in range(2):
                    v.wait_ge(centre[k], i * 2 + 2)
                    t = i * 2 + k
                    z = ps_x[k][:].rearrange("p (r w) -> p r w", w=GRID_W)
                    o = b.fX[:, bass.ds(t, 1), :].rearrange("p o (r w) -> p (o r) w", w=GRID_W)
                    zc, oc = ps_c[k][:, 0:TC], b.fC[:, bass.ds(t, 1), :].rearrange("p o w -> p (o w)")
                    v.scalar_tensor_tensor(out=o[:, :, 1:], in0=z[:, :, :-1], scalar=cw[:, bass.ds(t, 1), 0],
                                           in1=o[:, :, 1:], op0=ALU.mult, op1=ALU.add)
                    v.scalar_tensor_tensor(out=oc[:, 1:], in0=zc[:, :-1], scalar=cw[:, bass.ds(t, 1), 0],
                                           in1=oc[:, 1:], op0=ALU.mult, op1=ALU.add).then_inc(one, 1)
                    v.wait_ge(one, i * 2 + k + 1)
                    v.scalar_tensor_tensor(out=o[:, :, :-1], in0=z[:, :, 1:], scalar=cw[:, bass.ds(t, 1), 2],
                                           in1=o[:, :, :-1], op0=ALU.mult, op1=ALU.add)
                    v.scalar_tensor_tensor(out=oc[:, :-1], in0=zc[:, 1:], scalar=cw[:, bass.ds(t, 1), 2],
                                           in1=oc[:, :-1], op0=ALU.mult, op1=ALU.add).then_inc(taps[k], 1)
            for i in range(n_q):
                for k in range(2):
                    v.wait_ge(centre[k], 2 * (n_r + i) + 2)
                    t = 2 * i + k
                    z = ps_x[k][:].rearrange("p (r w) -> p r w", w=GRID_W)
                    o = b.qX[:, t, :].rearrange("p (w r) -> p r w", r=ROWS)
                    zc, oc = ps_c[k][:, 0:TC], b.qC[:, t, :]
                    v.scalar_tensor_tensor(out=o[:, 1:, :], in0=z[:, :-1, :], scalar=cq[:, t, 0:1],
                                           in1=o[:, 1:, :], op0=ALU.mult, op1=ALU.add)
                    v.scalar_tensor_tensor(out=oc[:, 1:], in0=zc[:, :-1], scalar=cq[:, t, 0:1],
                                           in1=oc[:, 1:], op0=ALU.mult, op1=ALU.add).then_inc(one, 1)
                    v.wait_ge(one, RW_TILES + t + 1)
                    v.scalar_tensor_tensor(out=o[:, :-1, :], in0=z[:, 1:, :], scalar=cq[:, t, 2:3],
                                           in1=o[:, :-1, :], op0=ALU.mult, op1=ALU.add)
                    v.scalar_tensor_tensor(out=oc[:, :-1], in0=zc[:, 1:], scalar=cq[:, t, 2:3],
                                           in1=oc[:, :-1], op0=ALU.mult, op1=ALU.add).then_inc(taps[k], 1)


def phase_values(nc, a, b):
    with ExitStack() as ctx:
        sb = alloc(nc, ctx)

        def sem(name):
            return b.semaphore(nc, name)

        wv = sb("win_v", [P, KT, MH * DV])
        wg = sb("win_gates", [P, KT, 2, GROWS])
        th = sb("qk_tanh", [P, QK_TILES, TX])
        ps_v = [ctx.enter_context(nc.psum_tensor(f"ps_pv{k}", [P, 512], F32)) for k in range(2)]
        ps_x = [ctx.enter_context(nc.psum_tensor(f"ps_gx{k}", [P, TX], F32)) for k in range(2)]
        ps_c = [ctx.enter_context(nc.psum_tensor(f"ps_gc{k}", [P, 512], F32)) for k in range(2)]
        v_in = sem("val_in")
        v_mm, v_out = sem("val_mm"), sem("val_out")
        g_mm, g_out = sem("val_g_mm"), sem("val_g_out")
        tanh_done, dve, ones_col = sem("val_tanh"), sem("val_dve"), sem("ones_column")
        block = ctx.enter_context(nc.Block())

        @block.sync
        def _(sp):
            sp.dma_start(wv[:], a["w_mv"]).then_inc(v_in, 16)
            sp.dma_start(wg[:], a["w_gates"]).then_inc(v_in, 16)

        @block.tensor
        def _(pe):
            pe.wait_ge(v_in, 32)
            for t in range((TX + TC) // MC):
                if t >= 2:
                    pe.wait_ge(v_out, t - 1)
                for j in range(KT):
                    mm = pe.matmul(ps_v[t % 2][:], b.hf[:, j, t * MC:(t + 1) * MC], wv[:, j, :],
                                   start=(j == 0), stop=(j == KT - 1))
                mm.then_inc(v_mm, 1)
            for gt in range(2):
                for lo, hi, bank in ((0, TX, ps_x[gt]), (TX, TX + TC, ps_c[gt])):
                    for j in range(KT):
                        mm = pe.matmul(bank[0:GROWS, 0:hi - lo], wg[:, j, gt, :], b.hf[:, j, lo:hi],
                                       start=(j == 0), stop=(j == KT - 1))
            mm.then_inc(g_mm, 1)

        @block.scalar
        def _(act):
            act.activation(th[:], b.qX[:], ACT.Tanh, scale=0.5).then_inc(tanh_done, 1)
            for t in range((TX + TC) // MC):
                act.wait_ge(v_mm, t + 1)
                act.activation(b.vM[:, t, :, 0:DV], ps_v[t % 2][:].rearrange("p (h v) -> p h v", v=DV),
                               ACT.Copy).then_inc(v_out, 1)
            act.wait_ge(dve, 1)
            act.activation(th[:, :, 0:TC], b.qC[:], ACT.Tanh, scale=0.5).then_inc(tanh_done, 1)
            act.wait_ge(g_mm, 1)
            for gt in range(2):
                act.activation(b.gates[:, gt, 0:TX], ps_x[gt][0:GROWS], ACT.Copy).then_inc(g_out, 1)
                act.activation(b.gates[:, gt, TX:], ps_c[gt][0:GROWS, 0:TC], ACT.Copy).then_inc(g_out, 1)

        @block.vector
        def _(v):
            v.memset(b.vM[:, :, :, DV:], 1.0).then_inc(ones_col, 1)
            link = Count(v, dve)
            for s, (z, n) in enumerate(((b.qX, TX), (b.qC, TC))):
                v.wait_ge(tanh_done, s + 1)
                zf, tf = z[:], th[:, :, 0:n]
                link(v.scalar_tensor_tensor(out=zf, in0=tf, scalar=1.0, in1=zf, op0=ALU.add, op1=ALU.mult))
                half = QK_TILES // 2
                link(v.tensor_scalar(z[:, 0:half], z[:, 0:half], 0.5, None, ALU.mult))
                link(v.tensor_scalar(z[:, half:], z[:, half:], 0.5 * DQK ** -0.5, None, ALU.mult))


HALF_DECAY = 0.5 * DECAY
LEVELS = [2, 4, 8, 16, 32]
M_NEG1_ST, M_STRICT, M_NEG_INCL, M_INCL, M_OFF = 0, 1, 2, 3, 4
N_MASKS = 4 + len(LEVELS)


def rwkv_masks():
    r = np.arange(C)
    out = np.zeros((C, 2, N_MASKS, C), np.float32)
    for z in range(2):
        first = (lambda s, t: s < t) if z == 0 else (lambda s, t: s > t)
        s_t = first(r[:, None], r[None, :])
        t_s = s_t.T

        def off(size):
            same = (r[:, None] // (2 * size)) == (r[None, :] // (2 * size))
            return same & ((r[:, None] // size) != (r[None, :] // size))

        out[:, z, M_NEG1_ST] = -(off(1) & s_t).astype(np.float32)
        out[:, z, M_STRICT] = s_t
        out[:, z, M_NEG_INCL] = -(s_t | np.eye(C, dtype=bool)).astype(np.float32)
        out[:, z, M_INCL] = s_t | np.eye(C, dtype=bool)
        for n, size in enumerate(LEVELS):
            out[:, z, M_OFF + n] = off(size) & t_s
    return np.concatenate([out, out], 0)


def phase_rwkv_features(nc, a, b, f, T, tag):
    nch = T // C
    with ExitStack() as ctx:
        sb = alloc(nc, ctx)

        def sem(name):
            return b.semaphore(nc, name + tag)

        wa_up = sb("wa_up" + tag, [P, 2, D_RWKV])
        vecs = sb("rw_vecs" + tag, [P, 6, PAIRS])
        half = sb("rw_half" + tag, [P, 4, PAIRS])
        one_ka = sb("rw_1ka" + tag, [P, PAIRS])
        w65 = sb("w65" + tag, [P, PAIRS, nch, C + 1])
        first = sb("w65_first" + tag, [P, nch, C + 1])
        tmp = sb("rw_tmp" + tag, [P, PAIRS, T])
        th = sb("rw_th" + tag, [P, 2, T])
        ps = [ctx.enter_context(nc.psum_tensor(f"ps_rf{k}" + tag, [P, 512], F32)) for k in range(8)]
        vec_in = sem("rwf_in")
        tanh_wd, half_done, proj = sem("rwf_tanh"), sem("rwf_half"), sem("rwf_proj")
        th_done, dec_done, a_done = sem("rwf_th"), sem("rwf_decay"), sem("rwf_a")
        sq_in, sq_done, norm_mm, norm_max, norm_root = (sem("rwf_kk"), sem("rwf_sq"), sem("rwf_norm"),
                                                        sem("rwf_max"), sem("rwf_sqrt"))
        dve, scanned = sem("rwf_dve"), sem("rwf_scanned")
        block = ctx.enter_context(nc.Block())

        @block.sync
        def _(sp):
            sp.dma_start(wa_up[:], a["wa_up"]).then_inc(vec_in, 16)
            sp.dma_start(vecs[:], a["rw_vecs"]).then_inc(vec_in, 16)

        @block.scalar
        def _(act):
            act.activation(f[0:64, 12, :], f[0:64, 12, :], ACT.Tanh).then_inc(tanh_wd, 1)
            act.wait_ge(half_done, 1)
            act.wait_ge(sq_in, 1)
            act.activation(tmp[:], b.kk[:, :, 0:T], ACT.Square).then_inc(sq_done, 1)
            for z in range(2):
                for c in range(PAIRS):
                    n = z * PAIRS + c
                    act.wait_ge(proj, n + 1)
                    act.activation(th[:, n % 2], ps[2 * (n % 2)][:, 0:T], ACT.Tanh, bias=half[:, z, c:c + 1],
                                   scale=0.5).then_inc(th_done, 1)
                    act.wait_ge(th_done, n + 1)
                    if z == 1:
                        act.wait_ge(scanned, c + 1)
                    act.activation(w65[:, c, :, 1:] if z == 0 else w65[:, c, :, 0:C],
                                   th[:, n % 2].rearrange("p (n t) -> p n t", t=C), ACT.Exp,
                                   bias=b.eps[:, 2:3], scale=-HALF_DECAY).then_inc(dec_done, 1)
                    act.activation(b.qa[:, z, c, 0:T], ps[2 * (n % 2) + 1][:, 0:T], ACT.Tanh,
                                   bias=half[:, 2 + z, c:c + 1], scale=0.5).then_inc(a_done, 1)
            act.wait_ge(norm_max, 1)
            act.activation(tmp[:], tmp[:], ACT.Ln).then_inc(norm_root, 1)
            act.wait_ge(norm_root, 1)
            act.activation(tmp[:], tmp[:], ACT.Exp, scale=-0.5).then_inc(norm_root, 1)

        @block.tensor
        def _(pe):
            pe.wait_ge(vec_in, 32)
            pe.wait_ge(tanh_wd, 1)
            for n in range(2 * PAIRS):
                z, c = n // PAIRS, n % PAIRS
                if n >= 2:
                    pe.wait_ge(a_done, n - 1)
                pe.matmul(ps[2 * (n % 2)][:, 0:T], wa_up[0:64, z, c * P:(c + 1) * P], f[0:64, 12, :],
                          start=True, stop=True)
                pe.matmul(ps[2 * (n % 2) + 1][:, 0:T], wa_up[64:P, z, c * P:(c + 1) * P], f[64:P, 12, :],
                          start=True, stop=True).then_inc(proj, 1)
            pe.wait_ge(sq_done, 1)
            for c in range(PAIRS):
                mm = pe.matmul(ps[4 + c][:, 0:T], b.block_ones[:], tmp[:, c, :], start=True, stop=True)
            mm.then_inc(norm_mm, 1)

        @block.vector
        def _(v):
            link = Count(v, dve)
            v.wait_ge(vec_in, 32)
            link(v.tensor_scalar(half[:], vecs[:, 0:4, :], 0.5, None, ALU.mult))
            v.tensor_scalar(one_ka[:], vecs[:, 5, :], -1.0, 1.0, ALU.mult, ALU.add).then_inc(half_done, 1)
            v.wait_ge(half_done, 1)
            for c in range(PAIRS):
                m = v.tensor_scalar(b.kk[:, c, 0:T], f[:, 4 + c, :], vecs[:, 4, c:c + 1], None, ALU.mult)
            m.then_inc(sq_in, 1)
            link(v.memset(first[:], 0.0))
            link(v.memset(first[:, :, 0:1], 1.0))
            for z in range(2):
                slot = 0 if z == 0 else C
                if z == 1:
                    v.wait_ge(scanned, PAIRS)
                    v.wait_ge(dec_done, 2 * PAIRS)
                link(v.memset(w65[:, :, :, slot:slot + 1], 0.0))
                for c in range(PAIRS):
                    v.wait_ge(dec_done, z * PAIRS + c + 1)
                    w = w65[:, c].rearrange("p n t -> p (n t)")
                    g = b.G[:, z, c, 0:nch * (C + 1)]
                    if z:
                        w, g = w[:, ::-1], g[:, ::-1]
                    v.tensor_tensor_scan(out=g, data0=w, data1=first[:].rearrange("p n t -> p (n t)"), initial=0.0,
                                         op0=ALU.mult, op1=ALU.add).then_inc(scanned, 1)
            v.wait_ge(norm_mm, 1)
            v.wait_ge(sq_done, 1)
            for c in range(PAIRS):
                m = v.tensor_scalar(tmp[:, c, :], ps[4 + c][:, 0:T], 1e-24, None, ALU.max)
            m.then_inc(norm_max, 1)
            v.wait_ge(norm_root, 2)
            link(v.tensor_tensor(b.kk[:, :, 0:T], b.kk[:, :, 0:T], tmp[:], ALU.mult))
            for z in range(2):
                v.wait_ge(a_done, (z + 1) * PAIRS)
                qa, ke = b.qa[:, z, :, 0:T], b.ke[:, z, :, 0:T]
                link(v.tensor_scalar(qa, qa, 0.5, 0.5, ALU.mult, ALU.add))
                for c in range(PAIRS):
                    m = v.tensor_scalar(ke[:, c], qa[:, c], vecs[:, 5, c:c + 1], one_ka[:, c:c + 1], ALU.mult, ALU.add)
                link(m)
                link(v.tensor_tensor(ke, ke, f[:, 4:8, :], ALU.mult))
                link(v.tensor_tensor(qa, qa, b.kk[:, :, 0:T], ALU.mult))


def phase_rwkv_scan(nc, a, b, f, T, tag, need_out):
    nch = T // C
    with ExitStack() as ctx:
        sb = alloc(nc, ctx)

        def sem(name):
            return b.semaphore(nc, name + tag)

        def each(name, shape):
            return [sb(f"{name}{g}" + tag, shape) for g in range(2)]

        RW = 3 * C
        pr, ginv = each("pr", [P, PAIRS, RW]), each("ginv", [P, PAIRS, C])
        diagonal = {n: each(n, [P, PAIRS, P]) for n in ("pd", "qs", "ks", "vs", "lt", "mt", "qt", "kt", "ti", "td", "xd")}
        pd, qs, ks, vs, lt, mt, qt, kt, ti, td, xd = diagonal.values()
        at, bt, vv, ro = (each(n, [P, PAIRS, C]) for n in ("at", "bt", "vv", "ro"))
        rr, uu, st, tm = (each(n, [P, PAIRS, C]) for n in ("rr", "uu", "st", "tm"))
        psw = [[ctx.enter_context(nc.psum_tensor(f"ps_rs{g}{k}" + tag, [P, 2, 512], F32)) for k in range(2)]
               for g in range(2)]
        pe_names = ["Q", "K", "T", "V"] + [x + str(s) for s in LEVELS for x in ("X", "Y", "YT")
                                           if x + str(s) != f"Y{LEVELS[-1]}"] + ["R", "U"] + ["O"] * need_out + ["S"]
        prep_names = ["p"] + ["rho"] * need_out + ["q0", "q1", "k0", "k1"]
        copy_names = ["vs", "pd"] + ["ro"] * need_out
        dve_names = (["tt_m", "td"] + ["bt"] * need_out + ["mt"]
                     + ["at"] * need_out + [x + str(s) for s in LEVELS for x in ("x", "ti", "td")
                                          if x + str(s) != f"ti{LEVELS[-1]}"] + ["s1", "s2"])
        act_names = ["lt", "qt", "kt", "ti", "v", "r", "u"] + ["out"] * need_out
        pe_s = [Steps(sem(f"rws_pe{g}"), pe_names) for g in range(2)]
        dve_s = [Steps(sem(f"rws_dve{g}"), dve_names) for g in range(2)]
        act_s = [Steps(sem(f"rws_act{g}"), act_names) for g in range(2)]
        prep_s = [Steps(sem(f"rws_prep{g}"), prep_names) for g in range(2)]
        gi_s = [Steps(sem(f"rws_gi{g}"), ["gi"]) for g in range(2)]
        copy_s = [Steps(sem(f"rws_copy{g}"), copy_names) for g in range(2)]
        unit, state_in = sem("rws_unit"), sem("rws_state")
        zeroed = sem("rws_zeroed")
        turn, turn_g = sem("rws_turn"), sem("rws_turn_pool")
        block = ctx.enter_context(nc.Block())

        def start_of(i, g, stride, base=0):
            return i * stride + base if g == 0 else i * (-stride) + ((nch - 1) * stride + base)

        def mask(g, m, shape):
            ap = b.masks[:, g, m, :]
            for _ in shape[1:-1]:
                ap = ap.unsqueeze(1)
            return ap.to_broadcast(shape)

        def wide(g, k, lo):
            return psw[g][k][:, :, 0:2 * RW].rearrange("p b (m x) -> p b m x", x=RW)[:, :, :, lo:lo + C]

        def quad(t):
            return t[:].rearrange("p (b m) x -> p b m x", b=2)

        def blocks(t):
            for h in range(2):
                part = slice(h * C, (h + 1) * C)
                yield part, t[part, :, part]

        def both_blocks(eng_op, t):
            for part, block_ in blocks(t):
                m = eng_op(part, block_)
            return m

        def flat(t):
            return t[:].rearrange("p m x -> p (m x)")

        def quad_part(ap):
            return ap.rearrange("p (b m) x -> p b m x", b=2)

        def in_chunks(eng, body):
            with eng.Fori(0, nch - 1) as i:
                body(i, True)
            body(nch - 1, False)

        @block.gpsimd
        def _(g_):
            for pair in diagonal.values():
                for t in pair:
                    g_.memset(t[:], 0.0).then_inc(zeroed, 1)
            g_.wait_ge(zeroed, 2 * len(diagonal))

            def prepare(n, g, first=False):
                t0 = start_of(n, g, C)
                cur = b.G[:, g, :, bass.ds(start_of(n, g, C + 1, 1 - g), C)]
                prev = b.G[:, g, :, bass.ds(start_of(n, g, C + 1, g), C)]

                def step(ins, name):
                    prep_s[g].mark(ins)
                    prep_s[g].wait(g_, n, name)

                if not first:
                    pe_s[g].wait(g_, n + (-1), "K")
                    copy_s[g].wait(g_, n + (-1), copy_names[-1])
                gi_s[g].wait(g_, n, "gi")
                g_.sem_inc(turn_g, 1)
                step(g_.tensor_tensor(pr[g][:, :, 0:C], b.kk[:, :, bass.ds(t0, C)], prev, ALU.mult), "p")
                g_.sem_inc(turn_g, 1)
                if need_out:
                    step(g_.tensor_tensor(pr[g][:, :, C:2 * C], f[:, 0:4, bass.ds(t0, C)], cur, ALU.mult), "rho")
                    g_.sem_inc(turn_g, 1)
                for name, to, src in (("q", qs[g], b.qa), ("k", ks[g], b.ke)):
                    for h, (part, o) in enumerate(blocks(to)):
                        step(g_.tensor_tensor(o, src[part, g, :, bass.ds(t0, C)], ginv[g][part], ALU.mult),
                             f"{name}{h}")
                        g_.sem_inc(turn_g, 1)

            if not need_out:
                g_.wait_ge(state_in, 2)
            for g in range(2):
                prep_s[g].start(g_)
                prepare(0, g, first=True)

            def body(i, more):
                if more:
                    for g in range(2):
                        prepare(i + 1, g)

            in_chunks(g_, body)

        @block.scalar
        def _(act):
            act.wait_ge(zeroed, 2 * len(diagonal))
            for g in range(2):
                act_s[g].start(act)
                act.activation(pr[g][:, :, 2 * C:], b.unit[:].unsqueeze(1).to_broadcast([P, PAIRS, C]),
                               ACT.Copy).then_inc(unit, 1)

            def values(n, g):
                copy_s[g].mark(both_blocks(lambda part, o: act.activation(
                    o, f[part, 8:12, bass.ds(start_of(n, g, C), C)], ACT.Copy), vs[g]))

            def keys(n, g):
                prep_s[g].wait(act, n, "rho" if need_out else "p")
                copy_s[g].mark(both_blocks(lambda part, o: act.activation(o, pr[g][part, :, 0:C], ACT.Copy), pd[g]))
                if need_out:
                    copy_s[g].mark(act.activation(ro[g][:], pr[g][:, :, C:2 * C], ACT.Copy))

            for g in range(2):
                copy_s[g].start(act)
                values(0, g)
                keys(0, g)

            def body(i, more):
                for g in range(2):
                    pe_s[g].wait(act, i, "Q")
                    dve_s[g].wait(act, i, "bt" if need_out else "tt_m")
                    act_s[g].mark(both_blocks(lambda part, o: act.activation(
                        quad_part(o), wide(g, 0, 0)[part], ACT.Copy), lt[g]))
                    act_s[g].mark(both_blocks(lambda part, o: act.activation(
                        quad_part(o), wide(g, 0, 2 * C)[part], ACT.Copy, scale=-1.0), qt[g]))
                for g in range(2):
                    pe_s[g].wait(act, i, "K")
                    dve_s[g].wait(act, i, "at" if need_out else "mt")
                    act_s[g].mark(both_blocks(lambda part, o: act.activation(
                        quad_part(o), wide(g, 1, 2 * C)[part], ACT.Copy), kt[g]))
                for g in range(2):
                    pe_s[g].wait(act, i, "T")
                    act_s[g].mark(act.activation(flat(ti[g]), psw[g][0][:, 0, :], ACT.Copy))
                    pe_s[g].wait(act, i, "V")
                    act_s[g].mark(act.activation(vv[g][:], psw[g][0][:, 1, 0:PAIRS * C].rearrange(
                        "p (m x) -> p m x", m=PAIRS), ACT.Copy))
                if more:
                    for g in range(2):
                        values(i + 1, g)
                for g in range(2):
                    pe_s[g].wait(act, i, "R")
                    act_s[g].mark(act.activation(rr[g][:], psw[g][0][:, 0, 0:PAIRS * C].rearrange(
                        "p (m x) -> p m x", m=PAIRS), ACT.Copy))
                for g in range(2):
                    pe_s[g].wait(act, i, "U")
                    act_s[g].mark(act.activation(uu[g][:], psw[g][1][:, 1, 0:PAIRS * C].rearrange(
                        "p (m x) -> p m x", m=PAIRS), ACT.Copy))
                if need_out:
                    for g in range(2):
                        pe_s[g].wait(act, i, "O")
                        act_s[g].mark(act.activation(b.rwo[:, g, :, bass.ds(start_of(i, g, C), C)],
                                                     psw[g][0][:, 0, 0:PAIRS * C].rearrange("p (m x) -> p m x", m=PAIRS),
                                                     ACT.Copy))
                if more:
                    for g in range(2):
                        keys(i + 1, g)

            in_chunks(act, body)

        @block.tensor
        def _(pe):
            for g in range(2):
                pe_s[g].start(pe)

            def heads():
                return ((m, h * C) for m in range(PAIRS) for h in range(2))

            pe.wait_ge(unit, 2)

            def body(i, more):
                for k, (name, step, buf) in enumerate((("Q", "q", qs), ("K", "k", ks))):
                    for g in range(2):
                        if k == 0:
                            prep_s[g].wait(pe, i, prep_names[-1])
                            dve_s[g].wait_last(pe, i)
                            act_s[g].wait_last(pe, i)
                        pe.sem_inc(turn, 1)
                        for m in range(PAIRS):
                            mm = pe.matmul(psw[g][k][:, m // 2, (m % 2) * RW:(m % 2 + 1) * RW],
                                           buf[g][:, m, :], pr[g][:, m, :], start=True, stop=True)
                        pe_s[g].mark(mm)
                for g in range(2):
                    dve_s[g].wait(pe, i, "bt" if need_out else "td")
                    act_s[g].wait(pe, i, "qt")
                    copy_s[g].wait(pe, i, "vs")
                    pe.sem_inc(turn, 1)
                    for m in range(PAIRS):
                        mm = pe.matmul(psw[g][0][:, 0, m * P:(m + 1) * P], td[g][:, m, :], b.ident[:],
                                       start=True, stop=True)
                    pe_s[g].mark(mm)
                    for m in range(PAIRS):
                        mm = pe.matmul(psw[g][0][:, 1, m * C:(m + 1) * C], vs[g][:, m, :], b.unit[:],
                                       start=True, stop=True)
                    pe_s[g].mark(mm)
                for n, s in enumerate(LEVELS):
                    for g in range(2):
                        if n == 0:
                            act_s[g].wait(pe, i, "v")
                        else:
                            dve_s[g].wait(pe, i, f"ti{LEVELS[n - 1]}")
                        pe.sem_inc(turn, 1)
                        for m in range(PAIRS):
                            mm = pe.matmul(psw[g][0][:, 1, m * P:(m + 1) * P], lt[g][:, m, :],
                                           ti[g][:, m, :], start=True, stop=True)
                        pe_s[g].mark(mm)
                    for g in range(2):
                        dve_s[g].wait(pe, i, f"x{s}")
                        if n == 0:
                            act_s[g].wait(pe, i, "kt")
                        pe.sem_inc(turn, 1)
                        if s != LEVELS[-1]:
                            for m in range(PAIRS):
                                mm = pe.matmul(psw[g][1][:, 0, m * P:(m + 1) * P], td[g][:, m, :],
                                               xd[g][:, m, :], start=True, stop=True)
                            pe_s[g].mark(mm)
                        for m in range(PAIRS):
                            mm = pe.matmul(psw[g][1][:, 1, m * P:(m + 1) * P], xd[g][:, m, :],
                                           td[g][:, m, :], start=True, stop=True)
                        pe_s[g].mark(mm)
                for g in range(2):
                    act_s[g].wait(pe, i, "v")
                    copy_s[g].wait(pe, i, copy_names[-1])
                    pe.sem_inc(turn, 1)
                    for m in range(PAIRS):
                        o = psw[g][0][:, 0, m * C:(m + 1) * C]
                        pe.matmul(o, pd[g][:, m, :], st[g][:, m, :], start=True, stop=False)
                        mm = pe.matmul(o, mt[g][:, m, :], vv[g][:, m, :], start=False, stop=True)
                    pe_s[g].mark(mm)
                for g in range(2):
                    dve_s[g].wait(pe, i, f"td{LEVELS[-1]}")
                    act_s[g].wait(pe, i, "r")
                    pe.sem_inc(turn, 1)
                    for m in range(PAIRS):
                        mm = pe.matmul(psw[g][1][:, 1, m * C:(m + 1) * C], td[g][:, m, :],
                                       rr[g][:, m, :], start=True, stop=True)
                    pe_s[g].mark(mm)
                for g in range(2):
                    act_s[g].wait(pe, i, "u")
                    pe.sem_inc(turn, 1)
                    if need_out:
                        for m, h in heads():
                            o = psw[g][0][h:h + C, 0, m * C:(m + 1) * C]
                            pe.matmul(o, st[g][h:h + C, m, :], ro[g][h:h + C, m, :], start=True, stop=False)
                            pe.matmul(o, vv[g][h:h + C, m, :], at[g][h:h + C, m, :], start=False, stop=False)
                            mm = pe.matmul(o, uu[g][h:h + C, m, :], bt[g][h:h + C, m, :], start=False, stop=True)
                        pe_s[g].mark(mm)
                    for m in range(PAIRS):
                        o = psw[g][1][:, 1, m * C:(m + 1) * C]
                        pe.matmul(o, kt[g][:, m, :], vv[g][:, m, :], start=True, stop=False)
                        mm = pe.matmul(o, qt[g][:, m, :], uu[g][:, m, :], start=False, stop=True)
                    pe_s[g].mark(mm)

            in_chunks(pe, body)

        @block.vector
        def _(v):
            v.wait_ge(zeroed, 2 * len(diagonal))
            for g in range(2):
                dve_s[g].start(v)
                if not need_out:
                    v.memset(pr[g][:, :, C:2 * C], 0.0).then_inc(state_in, 1)
                    v.memset(st[g][:], 0.0).then_inc(state_in, 1)
                else:
                    v.tensor_copy(st[g][:], b.state[:, g]).then_inc(state_in, 1)
            v.wait_ge(state_in, 2 if need_out else 4)
            small = [P, PAIRS, C]
            four = [P, 2, 2, C]

            def inverse(n, g):
                prep_s[g].wait_last(v, n)
                gi_s[g].mark(v.reciprocal(ginv[g][:], b.G[:, g, :, bass.ds(start_of(n, g, C + 1, 1 - g), C)]))

            for g in range(2):
                gi_s[g].start(v)
                inverse(0, g)

            def body(i, more):
                for g in range(2):
                    dve_s[g].wait_last(v, i)
                for g in range(2):
                    pe_s[g].wait(v, i, "Q")
                    dve_s[g].mark(v.tensor_tensor(quad(tm[g]), wide(g, 0, 0), mask(g, M_NEG1_ST, four), ALU.mult))
                    dve_s[g].wait(v, i, "tt_m")
                    dve_s[g].mark(both_blocks(lambda part, o: v.tensor_tensor(
                        o, tm[g][part], b.unit[part].unsqueeze(1).to_broadcast([C, PAIRS, C]), ALU.add), td[g]))
                    if need_out:
                        dve_s[g].mark(v.tensor_tensor(quad(bt[g]), wide(g, 0, C), mask(g, M_NEG_INCL, four), ALU.mult))
                for g in range(2):
                    pe_s[g].wait(v, i, "K")
                    dve_s[g].mark(both_blocks(lambda part, o: v.tensor_tensor(
                        quad_part(o), wide(g, 1, 0)[part], mask(g, M_STRICT, four)[part], ALU.mult), mt[g]))
                    if need_out:
                        dve_s[g].mark(v.tensor_tensor(quad(at[g]), wide(g, 1, C), mask(g, M_INCL, four), ALU.mult))
                for n, s in enumerate(LEVELS):
                    for g in range(2):
                        pe_s[g].wait(v, i, f"X{s}")
                        dve_s[g].mark(v.tensor_tensor(
                            xd[g][:].rearrange("p m (h x) -> p (m h) x", x=C),
                            psw[g][0][:, 1, :].rearrange("p (m x) -> p m x", x=C), mask(g, M_OFF + n, [P, 2 * PAIRS, C]),
                            ALU.mult))
                    for g in range(2):
                        if s != LEVELS[-1]:
                            pe_s[g].wait(v, i, f"Y{s}")
                            dve_s[g].mark(v.tensor_tensor(flat(ti[g]), flat(ti[g]), psw[g][1][:, 0, :], ALU.subtract))
                        pe_s[g].wait(v, i, f"YT{s}")
                        dve_s[g].mark(v.tensor_tensor(flat(td[g]), flat(td[g]), psw[g][1][:, 1, :], ALU.subtract))
                    if more and n < 2:
                        inverse(i + 1, n)
                for g in range(2):
                    pe_s[g].wait(v, i, "S")
                    dve_s[g].mark(v.tensor_tensor(tm[g][:], psw[g][1][:, 1, 0:PAIRS * C].rearrange(
                        "p (m x) -> p m x", m=PAIRS), st[g][:], ALU.add))
                    dve_s[g].wait(v, i, "s1")
                    dve_s[g].mark(v.tensor_tensor(
                        st[g][:], tm[g][:],
                        b.G[:, g, :, bass.ds(start_of(i, g, C + 1, C * (1 - g)), 1)].to_broadcast(small), ALU.mult))

            in_chunks(v, body)
            if not need_out:
                for g in range(2):
                    dve_s[g].wait_last(v, nch)
                    v.tensor_copy(b.state[:, g], st[g][:]).then_inc(state_in, 1)


def phase_rwkv_output(nc, a, b):
    f = b.fX
    with ExitStack() as ctx:
        sb = alloc(nc, ctx)

        def sem(name):
            return b.semaphore(nc, name)

        g_up = sb("g_up", [P, D_RWKV])
        vecs = sb("rwo_vecs", [P, 3, PAIRS])
        sq = sb("rwo_sq", [P, 2, PAIRS, TX])
        bonus = sb("rwo_bonus", [P, PAIRS, TX])
        gd = sb("rwo_gd", [P, TX])
        ps = [ctx.enter_context(nc.psum_tensor(f"ps_ro{k}", [P, TX], F32)) for k in range(8)]
        vec_in, tanh_done, gd_done = sem("rwo_in"), sem("rwo_tanh"), sem("rwo_gd_done")
        bonus_in, mean_mm, centred, squared = sem("rwo_bonus_in"), sem("rwo_mean"), sem("rwo_centred"), sem("rwo_squared")
        var_mm, rooted, inverse, gate_mm, evac, dve = (
            sem("rwo_var"), sem("rwo_root"), sem("rwo_inverse"), sem("rwo_gate"), sem("rwo_evac"), sem("rwo_dve"))
        block = ctx.enter_context(nc.Block())
        units = [(z, c) for z in range(2) for c in range(PAIRS)]

        @block.sync
        def _(sp):
            sp.dma_start(g_up[:], a["g_up"]).then_inc(vec_in, 16)
            sp.dma_start(vecs[:], a["rwo_vecs"]).then_inc(vec_in, 16)

        @block.scalar
        def _(act):
            act.activation(gd[:], f[:, 13, :], ACT.Tanh, scale=0.5).then_inc(tanh_done, 1)
            for n, (z, c) in enumerate(units):
                act.wait_ge(centred, n + 1)
                act.activation(sq[:, z, c], b.rwo[:, z, c], ACT.Square).then_inc(squared, 1)
            for n, (z, c) in enumerate(units):
                act.wait_ge(var_mm, n + 1)
                act.activation(sq[:, z, c], ps[n % 4][:], ACT.Ln, bias=b.eps[:, 1:2], scale=1.0 / C).then_inc(rooted, 1)
            for n, (z, c) in enumerate(units):
                act.wait_ge(rooted, n + 1)
                act.activation(sq[:, z, c], sq[:, z, c], ACT.Exp, scale=-0.5).then_inc(inverse, 1)

        @block.tensor
        def _(pe):
            for n, (z, c) in enumerate(units):
                if n >= 4:
                    pe.wait_ge(centred, n - 3)
                pe.matmul(ps[n % 4][:], b.block_ones[:], b.rwo[:, z, c], start=True, stop=True).then_inc(mean_mm, 1)
            for n, (z, c) in enumerate(units):
                pe.wait_ge(squared, n + 1)
                if n < 4:
                    pe.wait_ge(centred, n + 5)
                else:
                    pe.wait_ge(rooted, n - 3)
                pe.matmul(ps[n % 4][:], b.block_ones[:], sq[:, z, c], start=True, stop=True).then_inc(var_mm, 1)
            pe.wait_ge(bonus_in, 1)
            for c in range(PAIRS):
                mm = pe.matmul(ps[4 + c][:], b.block_ones[:], bonus[:, c], start=True, stop=True)
            mm.then_inc(gate_mm, 1)
            pe.wait_ge(vec_in, 32)
            pe.wait_ge(gd_done, 1)
            pe.wait_ge(evac, 1)
            for c in range(PAIRS):
                mm = pe.matmul(ps[4 + c][:], g_up[:, c * P:(c + 1) * P], gd[:], start=True, stop=True)
            mm.then_inc(gate_mm, 1)

        @block.vector
        def _(v):
            link = Count(v, dve)
            for n, (z, c) in enumerate(units):
                v.wait_ge(mean_mm, n + 1)
                v.scalar_tensor_tensor(out=b.rwo[:, z, c], in0=ps[n % 4][:], scalar=-1.0 / C, in1=b.rwo[:, z, c],
                                       op0=ALU.mult, op1=ALU.add).then_inc(centred, 1)
            link(v.tensor_tensor(bonus[:], b.ke[:, 0], b.ke[:, 1], ALU.add))
            link(v.tensor_tensor(bonus[:], bonus[:], f[:, 0:4, :], ALU.mult))
            v.wait_ge(vec_in, 32)
            for c in range(PAIRS):
                m = v.tensor_scalar(bonus[:, c], bonus[:, c], vecs[:, 0, c:c + 1], None, ALU.mult)
            m.then_inc(bonus_in, 1)
            v.wait_ge(tanh_done, 1)
            v.tensor_scalar(gd[:], gd[:], 0.5, 0.5, ALU.mult, ALU.add).then_inc(gd_done, 1)
            for n, (z, c) in enumerate(units):
                v.wait_ge(inverse, n + 1)
                m = v.tensor_tensor(sq[:, z, c], sq[:, z, c], b.rwo[:, z, c], ALU.mult)
            link(m)
            link(v.tensor_tensor(b.ya[:], sq[:, 0], sq[:, 1], ALU.add))
            link(v.tensor_scalar(vecs[:, 2, :], vecs[:, 2, :], 2.0, None, ALU.mult))
            for c in range(PAIRS):
                m = v.tensor_scalar(b.ya[:, c], b.ya[:, c], vecs[:, 1, c:c + 1], vecs[:, 2, c:c + 1], ALU.mult, ALU.add)
            link(m)
            v.wait_ge(gate_mm, 1)
            for c in range(PAIRS):
                m = v.tensor_tensor(bonus[:, c], ps[4 + c][:], f[:, 8 + c, :], ALU.mult)
            m.then_inc(evac, 1)
            v.wait_ge(evac, 1)
            link(v.tensor_tensor(b.ya[:], b.ya[:], bonus[:], ALU.add))
            v.wait_ge(gate_mm, 2)
            for c in range(PAIRS):
                m = v.tensor_tensor(b.ya[:, c], ps[4 + c][:], b.ya[:, c], ALU.mult)
            link(m)


NEG_M, INTER, FLOOR = 0, 1, 2
COL_C, COL_W = 0, 1
LN_MAX = 85.0
UNITS = 2 * MH


def phase_mlstm_gates(nc, a, b):
    T = TX + TC
    NCH = T // MC
    with ExitStack() as ctx:
        sb = alloc(nc, ctx)

        def sem(name):
            return b.semaphore(nc, name)

        sg = sb("gate_scan", [GROWS, 2, T])
        bias = sb("gate_bias", [GROWS, 2])
        resets = sb("gate_resets", [GROWS, 2, NCH, MC])
        bsum = sb("gate_b", [GROWS, T])
        m = sb("gate_m", [GROWS, T])
        mp = sb("gate_mprev", [GROWS, NCH])
        c2 = sb("gate_c2", [GROWS, T])
        rows = sb("gate_rows", [GROWS, 5, T])
        ident = sb("gate_ident", [GROWS, GROWS])
        ps_t = ctx.enter_context(nc.psum_tensor("ps_gt", [P, 512], F32))
        small_in, dve, act_done, t_done = sem("mlg_in"), sem("mlg_dve"), sem("mlg_act"), sem("mlg_t")
        want = [sem(f"mlg_want{k}") for k in range(3)]
        rows_done = sem("mlg_rows")
        mod = Modulation(nc, ctx, a, b, "_2", MOD_FIRST, MOD_TILES, b.acc[0:2, :, :])
        n_mod = MOD_TILES - MOD_FIRST
        block = ctx.enter_context(nc.Block())
        f, ig = sg[:, 1, :], sg[:, 0, :]

        @block.sync
        def _(sp):
            sp.dma_start(bias[:], a["gate_bias"]).then_inc(small_in, 16)
            sp.dma_start(resets[:], a["gate_resets"]).then_inc(small_in, 16)
            sp.dma_start(ident[:], a["ident"][0:GROWS, 0:GROWS]).then_inc(small_in, 16)
            sp.dma_start(b.select[:], a["select"]).then_inc(small_in, 16)
            sp.dma_start(b.m_mask[:], a["m_mask"]).then_inc(small_in, 16)
            mod.load_bias(sp)
            for n in range(n_mod):
                mod.load(sp, n)

        @block.scalar
        def _(act):
            act.wait_ge(want[0], 1)
            act.activation(bsum[:], f, ACT.Abs).then_inc(act_done, 1)
            act.wait_ge(act_done, 1)
            act.activation(bsum[:], bsum[:], ACT.Exp, scale=-1.0).then_inc(act_done, 1)
            act.wait_ge(act_done, 2)
            act.activation(bsum[:], bsum[:], ACT.Ln, bias=1.0).then_inc(act_done, 1)
            for n in range(2):
                mod.copy_row(act, n)
            act.wait_ge(want[1], 1)
            act.activation(rows[:, INTER], rows[:, INTER], ACT.Exp).then_inc(act_done, 1)
            act.activation(rows[:, FLOOR], rows[:, FLOOR], ACT.Exp, scale=-1.0).then_inc(act_done, 1)
            act.activation(rows[:, 4], rows[:, 4], ACT.Exp).then_inc(act_done, 1)
            for n in range(2, n_mod):
                mod.copy_row(act, n)

        @block.vector
        def _(v):
            link = Count(v, dve)
            for lo, hi, rev in ((0, 32, False), (32, GROWS, True)):
                for dst, src in (((0, TC), (TX, T)), ((TC, T), (0, TX))):
                    s = b.gates[lo:hi, :, src[0]:src[1]]
                    m_ = v.tensor_copy(sg[lo:hi, :, dst[0]:dst[1]], s[:, :, ::-1] if rev else s)
            link(m_)
            v.wait_ge(small_in, 80)
            link(v.tensor_scalar(ig, ig, bias[:, 0:1], None, ALU.add))
            v.tensor_scalar(f, f, bias[:, 1:2], None, ALU.add).then_inc(want[0], 1)
            v.wait_ge(act_done, 3)
            link(v.scalar_tensor_tensor(out=f, in0=f, scalar=0.0, in1=bsum[:], op0=ALU.min, op1=ALU.subtract))
            link(v.tensor_tensor_scan(out=m[:], data0=f, data1=ig, initial=0.0, op0=ALU.add, op1=ALU.max))
            link(v.tensor_tensor_scan(out=bsum[:], data0=resets[:, 0].rearrange("p n t -> p (n t)"), data1=f,
                                      initial=0.0, op0=ALU.mult, op1=ALU.add))
            link(v.tensor_tensor(rows[:, 3], ig, bsum[:], ALU.subtract))
            link(v.memset(mp[:, 0:1], 0.0))
            link(v.tensor_copy(mp[:, 1:], m[:, MC - 1:T - 1:MC]))
            link(v.tensor_copy(c2[:], rows[:, 3]))
            link(v.tensor_tensor(c2[:, 0:T:MC], c2[:, 0:T:MC], mp[:], ALU.max))
            link(v.tensor_tensor_scan(out=rows[:, NEG_M], data0=resets[:, 1].rearrange("p n t -> p (n t)"),
                                      data1=c2[:], initial=0.0, op0=ALU.add, op1=ALU.max))
            big = [GROWS, NCH, MC]

            def chunks(ap):
                return ap.rearrange("p (n t) -> p n t", t=MC)

            link(v.tensor_tensor(chunks(rows[:, INTER]), mp[:].unsqueeze(2).to_broadcast(big),
                                 chunks(rows[:, NEG_M]), ALU.subtract))
            link(v.tensor_tensor(chunks(rows[:, 4]), chunks(rows[:, 3]),
                                 chunks(rows[:, NEG_M])[:, :, MC - 1:MC].to_broadcast(big), ALU.subtract))
            link(v.tensor_scalar(rows[:, FLOOR], m[:], -LN_MAX, None, ALU.max))
            v.tensor_scalar(rows[:, NEG_M], rows[:, NEG_M], -1.0, None, ALU.mult).then_inc(want[1], 1)
            v.wait_ge(want[1], 1)
            v.wait_ge(act_done, 6)
            for lo, hi in ((0, 32), (32, GROWS)):
                for k in range(5):
                    src = chunks(rows[lo:hi, k])
                    dst = (b.g_rows[lo:hi, k] if k < 3 else b.g_turn[lo:hi, k - 3])
                    m_ = v.tensor_copy(chunks(dst), src[:, :, ::-1] if lo else src)
            m_.then_inc(rows_done, 1)
            v.wait_ge(t_done, 1)
            v.tensor_copy(b.g_cols[:].rearrange("p n k r -> p (n k r)"),
                          ps_t[:, 0:NCH * 2 * GROWS]).then_inc(want[2], 1)
            mod.add_bias(v)

        @block.tensor
        def _(pe):
            for n in range(4):
                mod.multiply(pe, n)
            pe.wait_ge(rows_done, 1)
            for n in range(NCH):
                for k in range(2):
                    o = (n * 2 + k) * GROWS
                    t = pe.transpose(ps_t[:, o:o + GROWS], b.g_turn[:, k, n * MC:(n + 1) * MC], ident[:])
            t.then_inc(t_done, 1)
            for n in range(4, n_mod):
                mod.multiply(pe, n)
            mod.turn(pe)


def phase_mlstm(nc, a, b, q, T, v0, n0, tag, need_out):
    nch = T // MC
    with ExitStack() as ctx:
        sb = alloc(nc, ctx)

        def sem(name):
            return b.semaphore(nc, name + tag)

        kz = sb("kz" + tag, [P, 2, MH, MC])
        qc = sb("qc" + tag, [P, 2, MH // 2, MC])
        vc = sb("vc" + tag, [P, 2, MH, DV + 1])
        ktw = sb("ktw" + tag, [P, 2, P])
        pw = sb("pw" + tag, [P, 2, MC])
        qa = sb("mqa" + tag, [P, 2, MC])
        ab = sb("mab" + tag, [P, 2, MC])
        ps_b, ps_s, ps_n, ps_c = ([ctx.enter_context(nc.psum_tensor(f"ps_{n}{k}" + tag, [P, 512], F32))
                                   for k in range(2)] for n in ("mb", "ms", "mn", "mc"))

        def pipelined(first, second):
            names = []
            for u in range(UNITS + 1):
                if u:
                    names += [f"{x}{u - 1}" for x in second]
                if u < UNITS:
                    names += [f"{x}{u}" for x in first]
            return names

        pool_names = [f"k{z}{par}" for z in range(2) for par in range(2)]
        copy_names = [x for z in range(2) for x in [f"v{z}"] + [f"q{z}"] * need_out]
        pe_names = pipelined(["S"], ["N"])
        if need_out:
            act_names = copy_names + pipelined(["kt", "e"], ["ab"])
            dve_names = pipelined(["m", "qa", "P"], ["mx", "rc", "h", "c"])
        else:
            act_names = copy_names + [f"kt{u}" for u in range(UNITS)]
            dve_names = [f"c{u}" for u in range(UNITS)]
        pool_s, pe_s, act_s, dve_s = (Steps(sem(n), names) for n, names in (
            ("mls_pool", pool_names), ("mls_pe", pe_names), ("mls_act", act_names), ("mls_dve", dve_names)))
        zeroed, state_in = sem("mls_zero"), sem("mls_state")
        block = ctx.enter_context(nc.Block())
        units = [(u, u // MH, u % MH) for u in range(UNITS)]

        def start_of(i, z):
            return i * MC if z == 0 else i * (-MC) + (nch - 1) * MC

        def chunk_of(i, z):
            return i if z == 0 else i * (-1) + (nch - 1)

        @block.gpsimd
        def _(g):
            pool_s.start(g)
            g.memset(kz[:], 0.0).then_inc(zeroed, 1)
            g.wait_ge(zeroed, 1)
            with g.Fori(0, nch) as i:
                pe_s.wait_last(g, i)
                for z in range(2):
                    t0 = start_of(i, z)
                    for par in range(2):
                        lo = par * DQK
                        pool_s.mark(g.tensor_copy(kz[lo:lo + DQK, z, par::2, :], q[lo:lo + DQK, 2:4, bass.ds(t0, MC)]))
                        pool_s.wait(g, i, f"k{z}{par}")

        @block.tensor
        def _(pe):
            pe_s.start(pe)
            with pe.Fori(0, nch) as i:
                for u, z, h in units + [(UNITS, 0, 0)]:
                    if u:
                        w, zw, hw = units[u - 1]
                        k = w % 2
                        if need_out:
                            dve_s.wait(pe, i, f"P{w}")
                            pe.matmul(ps_n[k][:, 0:MC], vc[:, zw, hw, 0:DV], pw[:, k], start=True, stop=False)
                            pe.matmul(ps_n[k][:, 0:MC], b.mC[:, w, 0:DV], qa[:, k], start=False, stop=True)
                            pe.matmul(ps_n[k][:, MC:2 * MC], b.ones[:], pw[:, k], start=True, stop=False)
                            pe.matmul(ps_n[k][:, MC:2 * MC], b.mC[:, w, DV:DV + 1].to_broadcast([P, P]), qa[:, k],
                                      start=False, stop=True)
                        act_s.wait(pe, i, f"kt{w}")
                        pe_s.mark(pe.matmul(ps_c[k][:, 0:DV + 1], ktw[:, k], vc[:, zw, hw, :], start=True, stop=True))
                    k = u % 2
                    if u < UNITS:
                        if u == 0:
                            pool_s.wait(pe, i, "k11")
                            act_s.wait(pe, i, copy_names[-1])
                        if u >= 2:
                            dve_s.wait(pe, i, f"c{u - 2}")
                        rows = b.g_rows[:, 1 - need_out:(3 if need_out else 2), bass.ds(i * MC + n0 * MC, MC)]
                        if need_out:
                            pe.matmul(ps_s[k][:, 0:MC], kz[:, z, h, :], qc[:, z, h // 2, :], start=True, stop=True)
                        pe.transpose(ps_s[k][:, MC:2 * MC], kz[:, z, h, :], b.ident[:])
                        pe_s.mark(pe.matmul(ps_b[k][:, (0 if need_out else MC):(3 if need_out else 2) * MC],
                                            b.select[:, u, :], rows, start=True, stop=True))

        @block.scalar
        def _(act):
            act_s.start(act)
            with act.Fori(0, nch) as i:
                pe_s.wait_last(act, i)
                dve_s.wait_last(act, i)
                for z in range(2):
                    act_s.mark(act.activation(vc[:, z], b.vM[:, bass.ds(chunk_of(i, z) + v0, 1), :, :].rearrange(
                        "p n h v -> p (n h) v"), ACT.Copy))
                    if need_out:
                        act_s.mark(act.activation(qc[:, z], q[:, 0:2, bass.ds(start_of(i, z), MC)], ACT.Copy))
                for u, z, h in units + [(UNITS, 0, 0)]:
                    if u and need_out:
                        k = (u - 1) % 2
                        pe_s.wait(act, i, f"N{u - 1}")
                        act_s.mark(act.activation(ab[:, k], ps_n[k][:, MC:2 * MC], ACT.Abs))
                    k = u % 2
                    if u < UNITS:
                        pe_s.wait(act, i, f"S{u}")
                        row = h + 32 * z
                        act_s.mark(act.activation(ktw[:, k], ps_s[k][:, MC:2 * MC], ACT.Copy,
                                                  scale=b.g_cols[:, bass.ds(i + n0, 1), COL_W, row]))
                        if need_out:
                            dve_s.wait(act, i, f"m{u}")
                            act_s.mark(act.activation(pw[:, k], pw[:, k], ACT.Exp))

        @block.vector
        def _(v):
            dve_s.start(v)
            if not need_out:
                v.memset(b.mC[:], 0.0).then_inc(state_in, 1)
                v.wait_ge(state_in, 1)
            with v.Fori(0, nch) as i:
                for u, z, h in units + [(UNITS, 0, 0)]:
                    if u:
                        w, zw, hw = units[u - 1]
                        kw = w % 2
                        pe_s.wait(v, i, f"N{w}")
                        end = MC + (MC - 1 if zw == 0 else 0)
                        if need_out:
                            act_s.wait(v, i, f"ab{w}")
                            dve_s.mark(v.tensor_tensor(ab[:, kw], ab[:, kw], ps_b[kw][:, 2 * MC:3 * MC], ALU.max))
                            dve_s.wait(v, i, f"mx{w}")
                            dve_s.mark(v.reciprocal(ab[:, kw], ab[:, kw]))
                            dve_s.wait(v, i, f"rc{w}")
                            dve_s.mark(v.tensor_tensor(b.mh[:, zw, hw, bass.ds(start_of(i, zw), MC)],
                                                       ps_n[kw][:, 0:MC], ab[:, kw], ALU.mult))
                        dve_s.mark(v.scalar_tensor_tensor(out=b.mC[:, w], in0=b.mC[:, w],
                                                          scalar=ps_b[kw][:, end:end + 1],
                                                          in1=ps_c[kw][:, 0:DV + 1], op0=ALU.mult, op1=ALU.add))
                    k = u % 2
                    if u < UNITS and need_out:
                        row = h + 32 * z
                        pe_s.wait(v, i, f"S{u}")
                        dve_s.mark(v.scalar_tensor_tensor(out=pw[:, k], in0=ps_b[k][:, 0:MC],
                                                          scalar=b.g_cols[:, bass.ds(i + n0, 1), COL_C, row],
                                                          in1=b.m_mask[:, z], op0=ALU.add, op1=ALU.min))
                        dve_s.mark(v.tensor_tensor(qa[:, k], ps_b[k][:, MC:2 * MC], qc[:, z, h // 2, :], ALU.mult))
                        act_s.wait(v, i, f"e{u}")
                        dve_s.mark(v.tensor_tensor(pw[:, k], ps_s[k][:, 0:MC], pw[:, k], ALU.mult))


def phase_mlstm_output(nc, a, b):
    with ExitStack() as ctx:
        sb = alloc(nc, ctx)

        def sem(name):
            return b.semaphore(nc, name)

        ng = sb("mlstm_g", [P, MH])
        sq = sb("mlo_sq", [P, 2, MH, TX])
        ps = [ctx.enter_context(nc.psum_tensor(f"ps_mo{k}", [P, TX], F32)) for k in range(8)]
        small_in, squared, mm, rooted, inverse, dve = (sem(f"mlo_{n}") for n in ("in", "sq", "mm", "root", "inverse", "dve"))
        block = ctx.enter_context(nc.Block())
        units = [(z, h) for z in range(2) for h in range(MH)]

        @block.sync
        def _(sp):
            sp.dma_start(ng[:], a["mlstm_g"]).then_inc(small_in, 16)

        @block.scalar
        def _(act):
            for z, h in units:
                act.activation(sq[:, z, h], b.mh[:, z, h], ACT.Square).then_inc(squared, 1)
            for n, (z, h) in enumerate(units):
                act.wait_ge(mm, n + 1)
                act.activation(sq[:, z, h], ps[n][:], ACT.Ln, bias=b.eps[:, 0:1], scale=1.0 / DV).then_inc(rooted, 1)
            for n, (z, h) in enumerate(units):
                act.wait_ge(rooted, n + 1)
                act.activation(sq[:, z, h], sq[:, z, h], ACT.Exp, scale=-0.5).then_inc(inverse, 1)

        @block.tensor
        def _(pe):
            for n, (z, h) in enumerate(units):
                pe.wait_ge(squared, n + 1)
                pe.matmul(ps[n][:], b.ones[:], sq[:, z, h], start=True, stop=True).then_inc(mm, 1)

        @block.vector
        def _(v):
            link = Count(v, dve)
            v.wait_ge(small_in, 16)
            for n, (z, h) in enumerate(units):
                v.wait_ge(inverse, n + 1)
                m = v.tensor_tensor(sq[:, z, h], sq[:, z, h], b.mh[:, z, h], ALU.mult)
            link(m)
            link(v.tensor_tensor(sq[:, 0], sq[:, 0], sq[:, 1], ALU.add))
            for h in range(MH):
                v.tensor_scalar(b.yb[:, h, :].rearrange("p (r w) -> p w r", w=GRID_W),
                                sq[:, 0, h].rearrange("p (w r) -> p w r", r=ROWS), ng[:, h:h + 1], None,
                                ALU.mult).then_inc(dve, 1)


def phase_merge(nc, a, b, h_dram):
    O_TILES, PART, N_TILES = MH, 3, MH + 3 * KT + KT
    with ExitStack() as ctx:
        sb = alloc(nc, ctx)

        def sem(name):
            return b.semaphore(nc, name)

        h = sb("mg_h", [P, KT, TX])
        hh, hl = b.h2h, b.h2l
        raw = sb("mg_raw", [P, 2, KT, P])
        wh, wl = sb("mg_w_hi", [P, 2, KT, P], F32R), sb("mg_w_lo", [P, 2, KT, P], F32R)
        yh, yl = sb("mg_y_hi", [P, KT, TX], F32R), sb("mg_y_lo", [P, KT, TX], F32R)
        mh, ml = sb("merged_hi", [P, KT, TX], F32R), sb("merged_lo", [P, KT, TX], F32R)
        sg = sb("mg_sg", [P, 4, TX])
        sq = h2 = h
        rs = sb("mg_rs", [P, TX])
        g2 = sb("mg_g2", [P, KT])
        gt = sb("mg_gt", [P, KT])
        ps = [ctx.enter_context(nc.psum_tensor(f"ps_mg{k}", [P, TX], F32)) for k in range(8)]
        h_in, x_in, g_in = sem("mg_h_in"), sem("mg_x_in"), sem("mg_g_in")
        raw_in = [sem(f"mg_raw{k}") for k in range(2)]
        w_hi, w_lo, w_mm = sem("mg_w_hi_done"), sem("mg_w_lo_done"), sem("mg_w_mm")
        h_hi, h_lo, y_hi, y_lo = sem("mg_h_hi"), sem("mg_h_lo"), sem("mg_y_hi_done"), sem("mg_y_lo_done")
        o_tanh, yb_done = sem("mg_o_tanh"), sem("mg_yb")
        m_tanh = [sem(f"mg_m_tanh{k}") for k in range(2)]
        m_used = [sem(f"mg_m_used{k}") for k in range(2)]
        x_done = [sem(f"mg_x_done{k}") for k in range(2)]
        squared, sum_mm, rooted, dve, pair = sem("mg_sq"), sem("mg_sum"), sem("mg_root"), sem("mg_dve"), sem("mg_pair")
        h2_done, h2_hi = sem("mg_h2_done"), sem("mg_h2_hi")
        block = ctx.enter_context(nc.Block())
        half = KT // 2
        quarters = [slice(q * 2, q * 2 + 2) for q in range(KT // 2)]

        def merge_tile(i, k, q):
            return i * (2 * PART) + (O_TILES + k * PART + q)

        def out_tile(i, k):
            return i * 2 + (O_TILES + PART * KT + k)

        @block.sync
        def _(sp):
            sp.dma_start(h[:], h_dram).then_inc(h_in, 16)
            for k in range(2):
                sp.dma_start(raw[:, k], a["w_merge"][k]).then_inc(raw_in[k], 16)
            sp.dma_start(g2[:], a["norm2_g"]).then_inc(g_in, 16)
            sp.dma_start(b.x1[:], a["xT"]).then_inc(x_in, 16)
            with sp.Fori(1, N_TILES // 2) as i:
                for k in range(2):
                    sp.wait_ge(w_lo, i * 2 + (k - 1))
                    sp.dma_start(raw[:, k], a["w_merge"][i * 2 + k]).then_inc(raw_in[k], 16)

        @block.gpsimd
        def _(g):
            with g.Fori(0, N_TILES // 2) as i:
                for k in range(2):
                    g.wait_ge(w_hi, i * 2 + (k + 1))
                    g.tensor_tensor(wl[:, k], raw[:, k], wh[:, k], ALU.subtract).then_inc(w_lo, 1)

        @block.tensor
        def _(pe):
            for n in range(O_TILES):
                pe.wait_ge(w_lo, n + 1)
                for j in range(KT):
                    if n == 0 and j % 2 == 0:
                        pe.wait_ge(h_lo, j // 2 + 1)
                    mm = product(pe, ps[n][:], wh[:, n % 2, j, :], wl[:, n % 2, j, :], hh[:, j, :], hl[:, j, :],
                                 j == 0, j == KT - 1)
                mm.then_inc(w_mm, 1)
            pe.wait_ge(y_lo, 2)
            with pe.Fori(0, half) as i:
                for k in range(2):
                    pe.wait_ge(m_used[k], i + 1)
                    for q in range(PART):
                        slot = (k * PART + q) % 2
                        pe.wait_ge(w_lo, merge_tile(i, k, q) + 1)
                        for j in range(KT):
                            if q < 2:
                                mm = product(pe, ps[4 * k + q][:], wh[:, slot, j, :], wl[:, slot, j, :],
                                             hh[:, j, :], hl[:, j, :], j == 0, j == KT - 1)
                            else:
                                mm = product(pe, ps[4 * k + 2 + j // 4][:], wh[:, slot, j, :], wl[:, slot, j, :],
                                             yh[:, j, :], yl[:, j, :], j % 4 == 0, j % 4 == 3)
                        mm.then_inc(w_mm, 1)
            for k in range(2):
                pe.wait_ge(m_used[k], half + 1)
            with pe.Fori(0, half) as i:
                for k in range(2):
                    pe.wait_ge(w_lo, out_tile(i, k) + 1)
                    pe.wait_ge(x_done[k], i + 1)
                    for j in range(KT):
                        mm = product(pe, ps[4 * k][:], wh[:, k, j, :], wl[:, k, j, :], mh[:, j, :], ml[:, j, :],
                                     j == 0, j == KT - 1)
                    mm.then_inc(w_mm, 1)
            for j in range(KT):
                pe.wait_ge(squared, j + 1)
                mm = pe.matmul(ps[1][:], b.ones[:], sq[:, j, :], start=(j == 0), stop=(j == KT - 1))
            mm.then_inc(sum_mm, 1)

        @block.scalar
        def _(act):
            def split(t, slot, turns):
                act.wait_ge(raw_in[slot], turns * 16 + 16)
                act.activation(wh[:, slot], raw[:, slot], ACT.Copy).then_inc(w_hi, 1)

            for k in range(2):
                split(k, k, 0)
            act.wait_ge(h_in, 16)
            for q in quarters:
                act.activation(hh[:, q], h[:, q], ACT.Copy).then_inc(h_hi, 1)
            act.activation(yh[:, 0:4], b.ya, ACT.Copy).then_inc(y_hi, 1)
            for n in range(O_TILES):
                act.wait_ge(w_mm, n + 1)
                act.activation(sg[:, n], ps[n][:], ACT.Tanh, scale=0.5).then_inc(o_tanh, 1)
                split(n + 2, n % 2, n // 2 + 1)
            act.wait_ge(yb_done, 1)
            act.activation(yh[:, 4:], b.yb, ACT.Copy).then_inc(y_hi, 1)
            with act.Fori(0, half) as i:
                for k in range(2):
                    act.wait_ge(m_used[k], i + 1)
                    for q in range(PART):
                        act.wait_ge(w_mm, merge_tile(i, k, q) + 1)
                        if q < 2:
                            m = act.activation(sg[:, 2 * k + q], ps[4 * k + q][:], ACT.Tanh, scale=0.5)
                        if q == 1:
                            m.then_inc(m_tanh[k], 1)
                        ahead = O_TILES + k * PART + q + 2
                        split(i * (2 * PART) + ahead, ahead % 2, i * PART + ahead // 2)
            with act.Fori(0, half - 1) as i:
                for k in range(2):
                    act.wait_ge(w_mm, out_tile(i, k) + 1)
                    split(out_tile(i, k) + 2, k, i + ((O_TILES + PART * KT) // 2 + 1))
            for j in range(KT):
                act.wait_ge(x_done[j % 2], j // 2 + 2)
                act.activation(sq[:, j], b.x1[:, j], ACT.Square).then_inc(squared, 1)
            act.wait_ge(sum_mm, 1)
            act.activation(rs[:], ps[1][:], ACT.Ln, bias=b.eps[:, 0:1], scale=1.0 / D).then_inc(rooted, 1)
            act.wait_ge(rooted, 1)
            act.activation(rs[:], rs[:], ACT.Exp, scale=-0.5).then_inc(rooted, 1)
            for j in range(KT):
                act.wait_ge(h2_done, j + 1)
                act.activation(b.h2h[:, j], h2[:, j], ACT.Copy).then_inc(h2_hi, 1)

        @block.vector
        def _(v):
            link = Count(v, dve)
            for k in range(2):
                v.sem_inc(m_used[k], 1)
                v.sem_inc(x_done[k], 1)
            for n, q in enumerate(quarters):
                v.wait_ge(h_hi, n + 1)
                v.tensor_tensor(hl[:, q], h[:, q], hh[:, q], ALU.subtract).then_inc(h_lo, 1)
            v.wait_ge(y_hi, 1)
            v.tensor_tensor(yl[:, 0:4], b.ya, yh[:, 0:4], ALU.subtract).then_inc(y_lo, 1)
            for n in range(MH):
                v.wait_ge(o_tanh, n + 1)
                m = v.scalar_tensor_tensor(out=b.yb[:, n], in0=sg[:, n], scalar=1.0, in1=b.yb[:, n],
                                           op0=ALU.add, op1=ALU.mult)
            link(m)
            v.tensor_scalar(b.yb[:], b.yb[:], 0.5, None, ALU.mult).then_inc(yb_done, 1)
            v.wait_ge(y_hi, 2)
            v.tensor_tensor(yl[:, 4:], b.yb, yh[:, 4:], ALU.subtract).then_inc(y_lo, 1)
            link(v.tensor_scalar(gt[:], b.mod[:, 2 * KT:3 * KT, 0], 0.5, None, ALU.mult))
            with v.Fori(0, half) as i:
                for k in range(2):
                    s0, s1 = sg[:, 2 * k:2 * k + 1], sg[:, 2 * k + 1:2 * k + 2]
                    tile = bass.ds(i * 2 + k, 1)

                    def step(ins, n):
                        ins.then_inc(pair, 1)
                        v.wait_ge(pair, i * 6 + (3 * k + n + 1))

                    v.wait_ge(m_tanh[k], i + 1)
                    v.wait_ge(w_mm, merge_tile(i, k, 2) + 1)
                    for n, s_ in enumerate((s0, s1)):
                        m = v.scalar_tensor_tensor(out=s_, in0=s_, scalar=1.0, in1=ps[4 * k + 2 + n][:].unsqueeze(1),
                                                   op0=ALU.add, op1=ALU.mult)
                    step(m, 0)
                    step(v.tensor_tensor(s0, s0, s1, ALU.add), 1)
                    step(v.tensor_scalar(mh[:, tile, :], s0, 1.0, None, ALU.mult), 2)
                    v.tensor_tensor(ml[:, tile, :], s0, mh[:, tile, :], ALU.subtract).then_inc(m_used[k], 1)
            v.wait_ge(x_in, 16)
            with v.Fori(0, half) as i:
                for k in range(2):
                    v.wait_ge(w_mm, out_tile(i, k) + 1)
                    tile = bass.ds(i * 2 + k, 1)
                    v.scalar_tensor_tensor(out=b.x1[:, tile, :], in0=ps[4 * k][:].unsqueeze(1),
                                           scalar=gt[:, tile], in1=b.x1[:, tile, :],
                                           op0=ALU.mult, op1=ALU.add).then_inc(x_done[k], 1)
            for k in range(2):
                v.wait_ge(x_done[k], half + 1)
            v.wait_ge(g_in, 16)
            link(v.scalar_tensor_tensor(out=g2[:], in0=b.mod[:, 4 * KT:5 * KT, 0], scalar=1.0, in1=g2[:],
                                        op0=ALU.add, op1=ALU.mult))
            v.wait_ge(rooted, 2)
            for j in range(KT):
                link(v.scalar_tensor_tensor(out=h2[:, j], in0=b.x1[:, j], scalar=g2[:, j:j + 1], in1=rs[:],
                                            op0=ALU.mult, op1=ALU.mult))
                v.tensor_scalar(h2[:, j], h2[:, j], b.mod[:, 3 * KT + j, 0:1], None, ALU.add).then_inc(h2_done, 1)
            for j in range(KT):
                v.wait_ge(h2_hi, j + 1)
                v.tensor_tensor(b.h2l[:, j], h2[:, j], b.h2h[:, j], ALU.subtract).then_inc(dve, 1)


TT = TX // P
LOW = -3.0e38


def phase_route(nc, a, b):
    with ExitStack() as ctx:
        sb = alloc(nc, ctx)

        def sem(name):
            return b.semaphore(nc, name)

        keys = sb("keys", [P, 2 * PH, NK])
        ring = sb("wq_ring", [P, 2, KT, P])
        wh, wl = sb("wq_hi", [P, 2, KT, P], F32R), sb("wq_lo", [P, 2, KT, P], F32R)
        qT = sb("q_T", [P, 2, TX])
        S = sb("scores", [P, 2, 2, TT, NK])
        left = sb("scores_left", [P, 2, TT, 2, NK])
        top = sb("top", [P, 2, TT, 2, TOPK])
        ix = sb("top_ix", [P, 2, TT, 2, TOPK], U32)
        cand = sb("cand", [P, 2, TT, TOPK, TOPK])
        cleft = sb("cand_left", [P, 2, TT, TOPK * TOPK])
        ctop = sb("cand_top", [P, 2, TT, TOPK])
        cix = sb("cand_top_ix", [P, 2, TT, TOPK], U32)
        pos = sb("cand_pos", [P, 2, 2, TT * TOPK], U32)
        pos_f = sb("cand_pos_f", [P, 2, 2, TT * TOPK])
        ix_f = sb("top_ix_f", [P, 2, 2, TT, TOPK])
        pick = sb("pick", [P, 2, 2, TT, TOPK, TOPK])
        picked = sb("picked", [P, 2, 2, TT * TOPK])
        iota = sb("iota16", [P, TOPK])
        ps_q = [ctx.enter_context(nc.psum_tensor(f"ps_q{k}", [P, TX], F32)) for k in range(2)]
        ps_s = [ctx.enter_context(nc.psum_tensor(f"ps_sc{k}", [P, TT, NK], F32)) for k in range(2)]
        keys_in, iota_in = sem("rt_keys"), sem("rt_iota")
        ring_in = [sem(f"rt_ring{k}") for k in range(2)]
        w_hi = [sem(f"rt_w_hi{k}") for k in range(2)]
        w_lo = [sem(f"rt_w_lo{k}") for k in range(2)]
        q_mm = [sem(f"rt_q_mm{k}") for k in range(2)]
        q_out = [sem(f"rt_q_out{k}") for k in range(2)]
        s_mm = [sem(f"rt_s_mm{k}") for k in range(2)]
        s_out = [sem(f"rt_s_out{k}") for k in range(2)]
        s_free = [sem(f"rt_s_free{k}") for k in range(2)]
        groups = (("max1",), ("ix1", "left"), ("max2",), ("ix2", "cand"), ("cmax1",), ("cix1", "cleft"), ("cmax2",),
                  ("cix2",), ("pos",), ("posf",), ("eq",))
        dve_s = Steps(sem("rt_dve"), [f"{x}{hh}" for names in groups for hh in range(2) for x in names]
                      + ["pick1", "sum1", "sum0", "out0", "out1"])
        pool_s = Steps(sem("rt_pool"), ["pick0"])
        turn, turn_g = sem("rt_turn"), sem("rt_turn_pool")
        block = ctx.enter_context(nc.Block())

        @block.sync
        def _(sp):
            for k in range(2):
                sp.dma_start(ring[:, k], a["w_q"][k]).then_inc(ring_in[k], 16)
            sp.dma_start(iota[:], a["iota"][:, 0:TOPK]).then_inc(iota_in, 16)
            sp.dma_start(keys[:], a["keys"]).then_inc(keys_in, 16)
            with sp.Fori(1, PH) as i:
                for k in range(2):
                    sp.wait_ge(w_lo[k], i)
                    sp.dma_start(ring[:, k], a["w_q"][i * 2 + k]).then_inc(ring_in[k], 16)

        def indices(eng, hh):
            for side in range(2):
                m = eng.tensor_tensor(pick[:, hh, side], pick[:, hh, side], ix_f[:, hh, side].unsqueeze(2)
                                      .to_broadcast([P, TT, TOPK, TOPK]), ALU.mult)
            return m

        @block.gpsimd
        def _(g):
            def rests(i, hh):
                for k in range(2):
                    g.wait_ge(w_hi[k], i * 2 + (hh + 1))
                    g.tensor_tensor(wl[:, k], ring[:, k], wh[:, k], ALU.subtract).then_inc(w_lo[k], 1)

            def choices(i):
                dve_s.wait(g, i, "eq0")
                g.sem_inc(turn_g, 1)
                pool_s.mark(indices(g, 0))

            pool_s.start(g)
            for hh in range(2):
                rests(0, hh)
            with g.Fori(0, PH // 2 - 1) as i:
                for hh in range(2):
                    rests(i + 1, hh)
                choices(i)
            choices(PH // 2 - 1)

        @block.tensor
        def _(pe):
            pe.wait_ge(keys_in, 16)
            with pe.Fori(0, PH) as i:
                for k in range(2):
                    pe.wait_ge(w_lo[k], i + 1)
                    pe.wait_ge(q_out[k], i + 1)
                    for j in range(KT):
                        mm = product(pe, ps_q[k][:], wh[:, k, j, :], wl[:, k, j, :], b.h2h[:, j, :], b.h2l[:, j, :],
                                     j == 0, j == KT - 1)
                    mm.then_inc(q_mm[k], 1)
                for k in range(2):
                    pe.wait_ge(q_out[k], i + 2)
                    pe.wait_ge(s_out[k], i + 1)
                    for t in range(TT):
                        mm = pe.matmul(ps_s[k][:, t, :], qT[:, k, t * P:(t + 1) * P],
                                       keys[:, bass.ds(i * 2 + k, 1), :].rearrange("p o n -> p (o n)"),
                                       start=True, stop=True)
                    mm.then_inc(s_mm[k], 1)

        @block.scalar
        def _(act):
            for k in range(2):
                act.sem_inc(q_out[k], 1)
                act.sem_inc(s_out[k], 1)
            with act.Fori(0, PH // 2) as i:
                for hh in range(2):
                    for k in range(2):
                        act.wait_ge(ring_in[k], i * 32 + (hh + 1) * 16)
                        act.wait_ge(q_out[k], i * 2 + (hh + 1))
                        act.activation(wh[:, k], ring[:, k], ACT.Copy).then_inc(w_hi[k], 1)
                    for k in range(2):
                        act.wait_ge(q_mm[k], i * 2 + (hh + 1))
                        act.activation(qT[:, k], ps_q[k][:], ACT.Copy).then_inc(q_out[k], 1)
                    act.wait_ge(s_free[hh], i + 1)
                    for k in range(2):
                        act.wait_ge(s_mm[k], i * 2 + (hh + 1))
                        act.activation(S[:, hh, k], ps_s[k][:], ACT.Copy).then_inc(s_out[k], 1)

        @block.vector
        def _(v):
            dve_s.start(v)
            v.wait_ge(iota_in, 16)
            for hh in range(2):
                v.sem_inc(s_free[hh], 1)
            both = [(t, p) for t in range(TT) for p in range(2)]

            def when(i, name, gate=None):
                dve_s.wait(v, i, name)
                v.sem_inc(turn if gate is None else gate, 1)

            with v.Fori(0, PH // 2) as i:
                for hh in range(2):
                    for k in range(2):
                        v.wait_ge(s_out[k], i * 2 + (hh + 2))
                        v.sem_inc(turn, 1)
                    for t, p in both:
                        m = v.max(top[:, hh, t, p, 0:8], S[:, hh, p, t, :])
                    dve_s.mark(m)
                for hh in range(2):
                    when(i, f"max1{hh}")
                    for t, p in both:
                        m = v.max_index(ix[:, hh, t, p, 0:8], top[:, hh, t, p, 0:8], S[:, hh, p, t, :])
                    dve_s.mark(m)
                    for t, p in both:
                        m = v.match_replace(left[:, hh, t, p], top[:, hh, t, p, 0:8], S[:, hh, p, t, :], LOW)
                    dve_s.mark(m)
                for hh in range(2):
                    when(i, f"left{hh}", s_free[hh])
                    for t, p in both:
                        m = v.max(top[:, hh, t, p, 8:16], left[:, hh, t, p])
                    dve_s.mark(m)
                for hh in range(2):
                    when(i, f"max2{hh}")
                    for t, p in both:
                        m = v.max_index(ix[:, hh, t, p, 8:16], top[:, hh, t, p, 8:16], left[:, hh, t, p])
                    dve_s.mark(m)
                    for t in range(TT):
                        m = v.tensor_tensor(cand[:, hh, t], top[:, hh, t, 0, :].unsqueeze(2).to_broadcast([P, TOPK, TOPK]),
                                            top[:, hh, t, 1, :].unsqueeze(1).to_broadcast([P, TOPK, TOPK]), ALU.add)
                    dve_s.mark(m)
                flat = cand[:].rearrange("p h t a c -> p h t (a c)")
                for hh in range(2):
                    when(i, f"cand{hh}")
                    for t in range(TT):
                        m = v.max(ctop[:, hh, t, 0:8], flat[:, hh, t])
                    dve_s.mark(m)
                for hh in range(2):
                    when(i, f"cmax1{hh}")
                    for t in range(TT):
                        m = v.max_index(cix[:, hh, t, 0:8], ctop[:, hh, t, 0:8], flat[:, hh, t])
                    dve_s.mark(m)
                    for t in range(TT):
                        m = v.match_replace(cleft[:, hh, t], ctop[:, hh, t, 0:8], flat[:, hh, t], LOW)
                    dve_s.mark(m)
                for hh in range(2):
                    when(i, f"cleft{hh}")
                    for t in range(TT):
                        m = v.max(ctop[:, hh, t, 8:16], cleft[:, hh, t])
                    dve_s.mark(m)
                for hh in range(2):
                    when(i, f"cmax2{hh}")
                    for t in range(TT):
                        m = v.max_index(cix[:, hh, t, 8:16], ctop[:, hh, t, 8:16], cleft[:, hh, t])
                    dve_s.mark(m)
                for hh in range(2):
                    dve_s.wait(v, i, f"cix2{hh}")
                    ci = cix[:, hh].rearrange("p t k -> p (t k)")
                    v.tensor_scalar(pos[:, hh, 0], ci, 4, None, ALU.logical_shift_right)
                    dve_s.mark(v.tensor_scalar(pos[:, hh, 1], ci, TOPK - 1, None, ALU.bitwise_and))
                for hh in range(2):
                    dve_s.wait(v, i, f"pos{hh}")
                    v.tensor_copy(pos_f[:, hh], pos[:, hh])
                    v.tensor_copy(b.SC[:, :, bass.ds(i * 2 + hh, 1), :].rearrange("p t o k -> p t (o k)"), ctop[:, hh])
                    dve_s.mark(v.tensor_copy(ix_f[:, hh].rearrange("p s t k -> p t s k"), ix[:, hh]))
                for hh in range(2):
                    dve_s.wait(v, i, f"posf{hh}")
                    for side in range(2):
                        m = v.tensor_tensor(
                            pick[:, hh, side].rearrange("p t k m -> p (t k) m"),
                            pos_f[:, hh, side].unsqueeze(2).to_broadcast([P, TT * TOPK, TOPK]),
                            iota[:].unsqueeze(1).to_broadcast([P, TT * TOPK, TOPK]), ALU.is_equal)
                    dve_s.mark(m)
                dve_s.wait(v, i, "eq1")
                dve_s.mark(indices(v, 1))
                for hh in (1, 0):
                    if hh:
                        dve_s.wait(v, i, "pick1")
                    else:
                        pool_s.wait(v, i, "pick0")
                    v.sem_inc(turn, 1)
                    for side in range(2):
                        m = v.tensor_reduce(picked[:, hh, side], pick[:, hh, side].rearrange("p t k m -> p (t k) m"),
                                            AX.X, ALU.add)
                    dve_s.mark(m)
                for hh in range(2):
                    dve_s.wait(v, i, f"sum{hh}")
                    dve_s.mark(v.tensor_copy(b.src[:, :, :, bass.ds(i * 2 + hh, 1), :].rearrange(
                        "p s t o k -> p s t (o k)"), picked[:, hh].rearrange("p s (t k) -> p s t k", k=TOPK)))


def phase_slots(nc, a, b):
    N = TT * PH
    with ExitStack() as ctx:
        sb = alloc(nc, ctx)

        def sem(name):
            return b.semaphore(nc, name)

        weight = sb("slot_weight", [P, TT, PH * TOPK])
        total = sb("soft_total", [P, N])
        ps = [ctx.enter_context(nc.psum_tensor(f"ps_sl{k}", [P, TX], F32)) for k in range(3)]
        sub_done, exp_done, dve, src_done, turned, out = (
            sem(f"sl_{n}") for n in ("sub", "exp", "dve", "src", "turned", "out"))
        block = ctx.enter_context(nc.Block())
        sc = b.SC[:].rearrange("p t h k -> p (t h) k")
        w = weight[:].rearrange("p t (h k) -> p (t h) k", k=TOPK)

        @block.scalar
        def _(act):
            act.wait_ge(sub_done, 1)
            act.activation(w, w, ACT.Exp).then_inc(exp_done, 1)

        @block.vector
        def _(v):
            link = Count(v, dve)
            v.tensor_tensor(w, sc, sc[:, :, 0:1].to_broadcast([P, N, TOPK]), ALU.subtract).then_inc(sub_done, 1)
            v.wait_ge(exp_done, 1)
            link(v.tensor_reduce(total[:], w, AX.X, ALU.add))
            link(v.reciprocal(total[:], total[:]))
            v.tensor_tensor(w, w, total[:].unsqueeze(2).to_broadcast([P, N, TOPK]), ALU.mult).then_inc(src_done, 1)
            v.memset(b.slots[:, :, TX:], 0.0).then_inc(out, 1)
            for k in range(3):
                v.wait_ge(turned, k + 1)
                v.tensor_copy(b.slots[:, k, 0:TX], ps[k][:]).then_inc(out, 1)
                if k != 1:
                    v.tensor_scalar(b.slots[:, 3 + k // 2, 0:TX], ps[k][:], -1.0, None, ALU.mult).then_inc(out, 1)

        @block.tensor
        def _(pe):
            for k in range(3):
                if k == 2:
                    pe.wait_ge(src_done, 1)
                for t in range(TT):
                    m = pe.transpose(ps[k][:, t * P:(t + 1) * P], weight[:, t, :] if k == 2 else
                                     b.src[:, k, t].rearrange("p h k -> p (h k)"), b.ident[:])
                m.then_inc(turned, 1)


def phase_weights(nc, a, b, w_dram):
    SUB = 4
    HALF = 128
    S = 4
    LOOPS = HALF // (S * SUB)
    with ExitStack() as ctx:
        sb = alloc(nc, ctx)

        def sem(name):
            return b.semaphore(nc, name)

        oi = b.acc[:, 0:S].rearrange("p s (k n) -> p s k n", n=NK)
        oj = b.acc[:, S:2 * S].rearrange("p s (k n) -> p s k n", n=NK)
        iota = sb("iota128", [P, NK])[:]
        away = sb("w_away", [P, S, NK])
        cur = sb("w_token", [P, S, 2])
        wb = sb("w_block", [P, 2, NK, HALF])
        ps = [ctx.enter_context(nc.psum_tensor(f"ps_w{k}", [P, SUB, NK], F32)) for k in range(S)]
        small_in = sem("w_in")
        built, built_a, mm, evac = ([sem(f"w_{n}{k}") for k in range(S)] for n in ("built", "built_act", "mm", "evac"))
        dist = sem("w_dist")
        built_p, fetched, turn = sem("w_built_pool"), sem("w_fetched"), sem("w_turn")
        stored = [sem(f"w_stored{k}") for k in range(2)]
        block = ctx.enter_context(nc.Block())
        dst = w_dram.rearrange("j i (n t) -> n i j t", t=HALF)
        n_outer = TX // (2 * HALF)

        @block.sync
        def _(sp):
            sp.dma_start(iota, a["iota"]).then_inc(small_in, 16)
            for half in range(2):
                sp.sem_inc(stored[half], 16)
            with sp.Fori(0, n_outer) as o:
                for half in range(2):
                    for s in range(S):
                        sp.wait_ge(evac[s], o * (2 * LOOPS) + ((half + 1) * LOOPS + 1))
                    sp.dma_start(dst[o * 2 + half], wb[:, half]).then_inc(stored[half], 16)
            for half in range(2):
                sp.wait_ge(stored[half], 16 * (n_outer + 1))

        def tokens(eng, body):
            with eng.Fori(0, n_outer) as o:
                for half in range(2):
                    with eng.Fori(0, LOOPS) as g:
                        for s in range(S):
                            body(o, half, g, s, o * (2 * LOOPS) + g + half * LOOPS)

        @block.vector
        def _(v):
            v.wait_ge(small_in, 16)

            def body(o, half, g, s, n):
                v.wait_ge(mm[s], n + 1)
                t = o * (2 * HALF) + g * (S * SUB) + (half * HALF + s * SUB)
                for k in range(SUB - 2):
                    v.tensor_scalar(oi[:, s, k], iota, b.slots[:, 0, bass.ds(t + k, 1)],
                                    b.slots[:, 2, bass.ds(t + k, 1)], ALU.is_equal, ALU.mult)
                v.tensor_tensor(oj[:, s], iota.unsqueeze(1).to_broadcast([P, SUB, NK]),
                                b.slots[:, 1, bass.ds(t, SUB)].unsqueeze(2).to_broadcast([P, SUB, NK]),
                                ALU.is_equal).then_inc(built[s], 1)

            tokens(v, body)

        @block.gpsimd
        def _(g_):
            g_.wait_ge(small_in, 16)
            g_.sem_inc(built_p, S)

            def body(o, half, g, s, n):
                t = o * (2 * HALF) + g * (S * SUB) + (half * HALF + s * SUB + SUB - 1)
                g_.wait_ge(built_p, n * S + (s + 1))
                g_.sem_inc(turn, 1)
                g_.tensor_copy(cur[:, s], b.slots[:, 0:3:2, bass.ds(t, 1)].rearrange("p k o -> p (k o)")).then_inc(fetched, 1)
                g_.wait_ge(fetched, n * S + (s + 1))
                g_.wait_ge(mm[s], n + 1)
                g_.sem_inc(turn, 1)
                g_.tensor_scalar(oi[:, s, SUB - 1], iota, cur[:, s, 0:1], cur[:, s, 1:2],
                                 ALU.is_equal, ALU.mult).then_inc(built_p, 1)

            tokens(g_, body)

        @block.tensor
        def _(pe):
            for s in range(S):
                pe.sem_inc(mm[s], 1)

            def body(o, half, g, s, n):
                pe.wait_ge(built[s], n + 1)
                pe.wait_ge(built_a[s], n + 1)
                pe.wait_ge(built_p, n * S + (s + S + 1))
                pe.wait_ge(evac[s], n + 1)
                for k in range(SUB):
                    m = pe.matmul(ps[s][:, k, :], oi[:, s, k], oj[:, s, k], start=True, stop=True)
                m.then_inc(mm[s], 1)

            tokens(pe, body)

        @block.scalar
        def _(act):
            def measure(t, s):
                act.activation(away[:, s], iota, ACT.Abs, bias=b.slots[:, 3, bass.ds(t, 1)]).then_inc(dist, 1)

            def build(t, s, turn_):
                act.wait_ge(dist, turn_ * S + (s + 1))
                act.activation(oi[:, s, SUB - 2], away[:, s], ACT.Relu, bias=b.slots[:, 2, bass.ds(t, 1)],
                               scale=b.slots[:, 4, bass.ds(t, 1)]).then_inc(built_a[s], 1)

            act.wait_ge(small_in, 16)
            for s in range(S):
                act.sem_inc(evac[s], 1)
                measure(s * SUB + (SUB - 2), s)
                build(s * SUB + (SUB - 2), s, 0)

            def body(o, half, g, s, n):
                t_next = o * (2 * HALF) + g * (S * SUB) + (half * HALF + S * SUB + s * SUB + SUB - 2)
                measure(t_next, s)
                act.wait_ge(mm[s], n + 2)
                act.wait_ge(stored[half], o * 16 + 16)
                act.activation(wb[:, half, :, bass.ds(g * (S * SUB) + s * SUB, SUB)].rearrange("p j t -> p t j"),
                               ps[s][:], ACT.Copy).then_inc(evac[s], 1)
                build(t_next, s, n + 1)

            tokens(act, body)


def phase_experts(nc, a, b, w_dram):
    G = 4
    RAW = 2
    rounds = NK // G
    half = G // RAW
    with ExitStack() as ctx:
        sb = alloc(nc, ctx)

        def sem(name):
            return b.semaphore(nc, name)

        u_raw, v_raw = sb("u_raw", [P, RAW, KT * P]), sb("v_raw", [P, RAW, D])
        uh, ul = sb("u_hi", [P, G, KT * P], F32R), sb("u_lo", [P, G, KT * P], F32R)
        vh, vl = sb("v_hi", [P, G, D], F32R), sb("v_lo", [P, G, D], F32R)
        wr = sb("w_ring", [P, G, TX])
        ga = sb("act", [P, G, TX])
        gh, gl = sb("act_hi", [P, G, TX], F32R), sb("act_lo", [P, G, TX], F32R)
        ps_a = [ctx.enter_context(nc.psum_tensor(f"ps_a{g}", [P, TX], F32)) for g in range(G)]
        ps_y = [ctx.enter_context(nc.psum_tensor(f"ps_y{k}", [P, TX], F32)) for k in range(4)]
        u_in, v_in = ([sem(f"ex_{n}{k}") for k in range(RAW)] for n in ("u_in", "v_in"))
        w_in = [sem(f"ex_w_in{g}") for g in range(G)]
        u_hi, u_lo, v_hi, v_lo, a_mm, gelu, gated, g_hi, g_lo, y_mm, y_add, zeroed = (sem(f"ex_{n}") for n in (
            "u_hi", "u_lo", "v_hi", "v_lo", "a_mm", "gelu", "gated", "g_hi", "g_lo", "y_mm", "y_add", "zeroed"))
        block = ctx.enter_context(nc.Block())

        def in_rounds(eng, body):
            with eng.Fori(0, rounds - 1) as i:
                body(i, True)
            body(rounds - 1, False)

        def j_tile(ap, i, g):
            return ap[i * G + g]

        @block.sync
        def _(sp):
            def load_u(i, g, wait=True):
                if wait:
                    sp.wait_ge(u_lo, i * G + (g - RAW + 1))
                sp.dma_start(u_raw[:, g % RAW], j_tile(a["uT"], i, g)).then_inc(u_in[g % RAW], 16)

            def load_vw(i, first=False):
                for g in range(G):
                    if not first:
                        sp.wait_ge(gated, i * G + (g - G + 1))
                    sp.dma_start(wr[:, g], j_tile(w_dram, i, g)).then_inc(w_in[g], 16)
                for g in range(G):
                    if not first or g >= RAW:
                        sp.wait_ge(v_lo, i * G + (g - RAW + 1))
                    sp.dma_start(v_raw[:, g % RAW], j_tile(a["v"], i, g)).then_inc(v_in[g % RAW], 16)

            for g in range(G):
                load_u(0, g, g >= RAW)
            load_vw(0, first=True)
            with sp.Fori(1, rounds) as i:
                for g in range(G):
                    load_u(i, g)
                load_vw(i)

        @block.scalar
        def _(act):
            def split_u(i, g):
                act.wait_ge(u_in[g % RAW], (i * half + (g // RAW + 1)) * 16)
                act.activation(uh[:, g], u_raw[:, g % RAW], ACT.Copy).then_inc(u_hi, 1)

            for g in range(G):
                split_u(0, g)

            def body(i, more):
                for g in range(G):
                    act.wait_ge(a_mm, i * G + (g + 1))
                    act.activation(ga[:, g], ps_a[g][:], ACT.Gelu).then_inc(gelu, 1)
                    act.wait_ge(v_in[g % RAW], (i * half + (g // RAW + 1)) * 16)
                    act.activation(vh[:, g], v_raw[:, g % RAW], ACT.Copy).then_inc(v_hi, 1)
                    act.wait_ge(gated, i * G + (g + 1))
                    act.activation(gh[:, g], ga[:, g], ACT.Copy).then_inc(g_hi, 1)
                if more:
                    for g in range(G):
                        split_u(i + 1, g)

            in_rounds(act, body)

        @block.vector
        def _(v):
            def split_u(i, g):
                v.wait_ge(u_hi, i * G + (g + 1))
                v.tensor_tensor(ul[:, g], u_raw[:, g % RAW], uh[:, g], ALU.subtract).then_inc(u_lo, 1)

            for g in range(G):
                split_u(0, g)
            v.memset(b.acc[:], 0.0).then_inc(zeroed, 1)
            v.wait_ge(zeroed, 1)
            v.sem_inc(y_add, KT)

            def body(i, more):
                for g in range(G):
                    v.wait_ge(w_in[g], i * 16 + 16)
                    v.wait_ge(gelu, i * G + (g + 1))
                    v.tensor_tensor(ga[:, g], ga[:, g], wr[:, g], ALU.mult).then_inc(gated, 1)
                    v.wait_ge(v_hi, i * G + (g + 1))
                    v.tensor_tensor(vl[:, g], v_raw[:, g % RAW], vh[:, g], ALU.subtract).then_inc(v_lo, 1)
                    v.wait_ge(g_hi, i * G + (g + 1))
                    v.tensor_tensor(gl[:, g], ga[:, g], gh[:, g], ALU.subtract).then_inc(g_lo, 1)
                for m in range(KT):
                    v.wait_ge(y_mm, i * KT + (m + 1))
                    v.wait_ge(y_add, i * KT + (m + 1))
                    v.tensor_tensor(b.acc[:, m], b.acc[:, m], ps_y[m % 4][:], ALU.add).then_inc(y_add, 1)
                    if more and m % 2:
                        split_u(i + 1, m // 2)

            in_rounds(v, body)

        @block.tensor
        def _(pe):
            def body(i, more):
                for g in range(G):
                    pe.wait_ge(u_lo, i * G + (g + 1))
                    for j in range(KT):
                        w = slice(j * P, (j + 1) * P)
                        mm = product(pe, ps_a[g][:], uh[:, g, w], ul[:, g, w], b.h2h[:, j, :], b.h2l[:, j, :],
                                     j == 0, j == KT - 1)
                    mm.then_inc(a_mm, 1)
                for m0 in range(0, KT, 4):
                    for gs in ((0, 1, 2), (3,)) if m0 == 0 else ((0, 1, 2, 3),):
                        for m in range(m0, m0 + 4):
                            if gs[0] == 0:
                                pe.wait_ge(y_add, i * KT + (m + 5))
                            for g in gs:
                                if m == 0 or g == 3:
                                    pe.wait_ge(g_lo, i * G + (g + 1))
                                w = slice(m * P, (m + 1) * P)
                                mm = product(pe, ps_y[m % 4][:], vh[:, g, w], vl[:, g, w], gh[:, g], gl[:, g],
                                             g == 0, g == G - 1)
                            if gs[-1] == G - 1:
                                mm.then_inc(y_mm, 1)

            in_rounds(pe, body)


def phase_final(nc, a, b, out):
    with ExitStack() as ctx:
        sb = alloc(nc, ctx)

        def sem(name):
            return b.semaphore(nc, name)

        fg = sb("final_g", [P, KT])
        sq = sb("fin_sq", [P, KT, TX])
        rs = sb("fin_rs", [P, TX])
        ps = ctx.enter_context(nc.psum_tensor("ps_fin", [P, TX], F32))
        small_in, x_done, squared, summed, rooted, y_done, stored = (
            sem(f"fin_{n}") for n in ("in", "x", "sq", "sum", "root", "y", "stored"))
        block = ctx.enter_context(nc.Block())

        @block.sync
        def _(sp):
            sp.dma_start(fg[:], a["final_g"]).then_inc(small_in, 16)
            for j in range(KT):
                sp.wait_ge(y_done, j + 1)
                sp.dma_start(out[:, j, :], b.acc[:, j]).then_inc(stored, 16)
            sp.wait_ge(stored, 16 * KT)

        @block.vector
        def _(v):
            for j in range(KT):
                v.scalar_tensor_tensor(out=b.x1[:, j], in0=b.acc[:, j], scalar=b.mod[:, 5 * KT + j, 0:1],
                                       in1=b.x1[:, j], op0=ALU.mult, op1=ALU.add).then_inc(x_done, 1)
            v.wait_ge(small_in, 16)
            v.wait_ge(rooted, 2)
            v.wait_ge(x_done, KT)
            for j in range(KT):
                v.scalar_tensor_tensor(out=b.acc[:, j], in0=b.x1[:, j], scalar=fg[:, j:j + 1], in1=rs[:],
                                       op0=ALU.mult, op1=ALU.mult).then_inc(y_done, 1)

        @block.scalar
        def _(act):
            for j in range(KT):
                act.wait_ge(x_done, j + 1)
                act.activation(sq[:, j], b.x1[:, j], ACT.Square).then_inc(squared, 1)
            act.wait_ge(summed, 1)
            act.activation(rs[:], ps[:], ACT.Ln, bias=b.eps[:, 0:1], scale=1.0 / D).then_inc(rooted, 1)
            act.wait_ge(rooted, 1)
            act.activation(rs[:], rs[:], ACT.Exp, scale=-0.5).then_inc(rooted, 1)

        @block.tensor
        def _(pe):
            for j in range(KT):
                pe.wait_ge(squared, j + 1)
                mm = pe.matmul(ps[:], b.ones[:], sq[:, j], start=(j == 0), stop=(j == KT - 1))
            mm.then_inc(summed, 1)


def build_program(nc, a, out):
    with ExitStack() as ctx:
        sb = alloc(nc, ctx)
        b = Buffers()
        b.ones = sb("ones", [P, P])
        b.eps = sb("eps", [P, 4])
        b.ident = sb("ident", [P, P])
        b.mod = sb("mod", [P, N_MOD * KT, 2])
        b.silu_c = sb("silu_c", [P, KT, 2])
        b.acc = sb("mixed", [P, KT, TX])
        b.ya, b.yb = b.acc[:, 0:PAIRS], b.acc[:, PAIRS:]
        mixers = ExitStack()
        b.masks = alloc(nc, mixers)("rwkv_masks", [P, 2, N_MASKS, C])
        b.unit = alloc(nc, mixers)("unit", [P, C])
        b.block_ones = alloc(nc, mixers)("block_ones", [P, P])
        const = ctx.enter_context(nc.semaphore("const_done"))
        const_in = ctx.enter_context(nc.semaphore("const_in"))
        with nc.Block() as block:
            @block.gpsimd
            def _(g):
                g.memset(b.ones[:], 1.0).then_inc(const, 1)
                g.memset(b.eps[:, 0:1], NORM_EPS).then_inc(const, 1)
                g.memset(b.eps[:, 1:2], GN_EPS).then_inc(const, 1)
                g.memset(b.eps[:, 2:3], -HALF_DECAY).then_inc(const, 1)
                g.wait_ge(const, 4)

            @block.sync
            def _(sp):
                sp.dma_start(b.masks[:], a["rwkv_masks"]).then_inc(const_in, 16)
                sp.dma_start(b.unit[:], a["unit"]).then_inc(const_in, 16)
                sp.dma_start(b.block_ones[:], a["block_ones"]).then_inc(const_in, 16)
                sp.dma_start(b.ident[:], a["ident"]).then_inc(const_in, 16)
                sp.wait_ge(const_in, 64)
        h_dram = nc.dram_tensor("h_scratch", [P, KT, TX], F32, kind="Internal").ap()
        with mixers:
            sm = alloc(nc, mixers)
            b.fX = sm("fX", [P, RW_TILES, TX])
            b.fC = sm("fC", [P, RW_TILES, TC])
            with ExitStack() as ml:
                sl = alloc(nc, ml)
                b.qX = sl("qX", [P, QK_TILES, TX])
                b.qC = sl("qC", [P, QK_TILES, TC])
                b.vM = sl("vM", [P, (TX + TC) // MC, MH, DV + 1])
                b.gates = sl("gates", [GROWS, 2, TX + TC])
                with ExitStack() as norm:
                    sn = alloc(nc, norm)
                    b.hh, b.hl = sn("h_hi", [P, KT, TX + TC], F32R), sn("h_lo", [P, KT, TX + TC], F32R)
                    phase_modulation(nc, a, b, h_dram)
                    b.hf = sn("h_both", [P, KT, TX + TC])
                    phase_projection(nc, a, b)
                    phase_values(nc, a, b)
                b.g_rows = sl("g_rows", [GROWS, 3, TX + TC])
                b.g_turn = sl("g_turn", [GROWS, 2, TX + TC])
                b.g_cols = sl("g_cols", [P, (TX + TC) // MC, 2, GROWS])
                b.select = sl("select", [GROWS, UNITS, P])
                b.m_mask = sl("m_mask", [P, 2, MC])
                b.mC = sl("mC", [P, UNITS, DV + 1])
                b.mh = sl("mh", [P, 2, MH, TX])
                phase_mlstm_gates(nc, a, b)
                phase_mlstm(nc, a, b, b.qC, TC, TX // MC, 0, "_c", False)
                phase_mlstm(nc, a, b, b.qX, TX, 0, TC // MC, "_x", True)
                phase_mlstm_output(nc, a, b)
            with ExitStack() as rw:
                sr = alloc(nc, rw)
                b.kk = sr("kk", [P, PAIRS, TX])
                b.ke = sr("ke", [P, 2, PAIRS, TX])
                b.qa = sr("qa", [P, 2, PAIRS, TX])
                b.G = sr("G", [P, 2, PAIRS, TX // C * (C + 1)])
                b.state = sr("rw_state", [P, 2, PAIRS, C])
                phase_rwkv_features(nc, a, b, b.fC, TC, "_c")
                phase_rwkv_scan(nc, a, b, b.fC, TC, "_c", False)
                phase_rwkv_features(nc, a, b, b.fX, TX, "_x")
                b.rwo = sr("rwo", [P, 2, PAIRS, TX])
                phase_rwkv_scan(nc, a, b, b.fX, TX, "_x", True)
                phase_rwkv_output(nc, a, b)
        w_dram = nc.dram_tensor("w_scratch", [NK, P, TX], F32, kind="Internal").ap()
        b.x1 = sb("x1", [P, KT, TX])
        b.h2h = sb("h2_hi", [P, KT, TX], F32R)
        b.h2l = sb("h2_lo", [P, KT, TX], F32R)
        b.clear_semaphores(nc)
        phase_merge(nc, a, b, h_dram)
        with ExitStack() as route:
            st = alloc(nc, route)
            b.slots = st("slots", [P, 5, TX + 16])
            with ExitStack() as choice:
                b.src = alloc(nc, choice)("slot_src", [P, 2, TT, PH, TOPK])
                b.SC = alloc(nc, choice)("SC", [P, TT, PH, TOPK])
                phase_route(nc, a, b)
                phase_slots(nc, a, b)
            phase_weights(nc, a, b, w_dram)
        b.clear_semaphores(nc)
        phase_experts(nc, a, b, w_dram)
        phase_final(nc, a, b, out)


def column(v):
    return v.reshape(-1, P).T


def weight_tiles(w):
    k, n = w.shape
    return w.reshape(k // P, P, n // P, P).transpose(2, 1, 0, 3)


def turned(x):
    return x.T.reshape(-1, P, x.shape[0]).transpose(1, 0, 2)


def laid_out(x, c, ctx, c_ctx, ada_w, ada_b, norm1_g, w_in, rwkv_conv, rwkv_w0, rwkv_w_up, rwkv_a0,
             rwkv_a_up, rwkv_g_up, rwkv_k_k, rwkv_k_a, rwkv_r_k, rwkv_ln_w, rwkv_ln_b, mlstm_conv,
             mlstm_i_b, mlstm_f_b, mlstm_norm_g, w_branch_a, w_branch_b, w_out, norm2_g, peer_wq,
             peer_keys, peer_u, peer_v, final_g):
    rw_cols = RW_TILES * P
    ends = np.cumsum([rw_cols, 2 * MH * DQK, MH * DV, 2 * MH, 2 * MH, MH * DV, D, D])
    w_rw, w_qk, w_mv, w_i, w_f, w_o, w_ga, w_gb = np.split(w_in[0], ends[:-1], axis=1)
    gates = np.zeros((D, 2, GROWS), w_in.dtype)
    gate_bias = np.zeros((GROWS, 2), w_in.dtype)
    for k, (w, bias) in enumerate(((w_i, mlstm_i_b[0]), (w_f, mlstm_f_b[0]))):
        for z in range(2):
            gates[:, k, 32 * z:32 * z + MH] = w[:, z * MH:(z + 1) * MH]
            gate_bias[32 * z:32 * z + MH, k] = bias[z]
    w_ab = np.concatenate([w_branch_a[0], w_branch_b[0]], 0)
    merge = np.stack([weight_tiles(w_ga), weight_tiles(w_gb), weight_tiles(w_ab)], 1)
    merge = np.concatenate([weight_tiles(w_o), merge.reshape(3 * KT, P, KT, P), weight_tiles(w_out[0])])
    r = np.arange(P)
    mask = np.zeros((P, 2, MC), np.float32)
    mask[:, 0] = np.where(r[:, None] <= r[None, :], 0.0, NEG)
    mask[:, 1] = np.where(r[:, None] >= r[None, :], 0.0, NEG)
    resets = np.zeros((GROWS, 2, (TX + TC) // MC, MC), np.float32)
    resets[:, 0, :, 1:] = 1.0
    resets[:, 1, :, 0] = NEG
    select = np.zeros((GROWS, UNITS, P), np.float32)
    for u in range(UNITS):
        select[u % MH + 32 * (u // MH), u] = 1.0
    return {
        "xT": turned(x[0]), "ctxT": turned(ctx[0]),
        "cc": np.stack([c[0], c_ctx], -1).reshape(KT, P, 2).transpose(1, 0, 2),
        "ada_w": ada_w[0].reshape(KT, P, MOD_TILES, MOD_W).transpose(2, 1, 0, 3), "ada_b": column(ada_b[0]), "norm1_g": column(norm1_g[0]),
        "w_rw": weight_tiles(np.concatenate([w_rw, w_qk], 1)),
        "w_mv": w_mv.reshape(KT, P, MH * DV).transpose(1, 0, 2),
        "w_gates": gates.reshape(KT, P, 2, GROWS).transpose(1, 0, 2, 3),
        "rwkv_conv": rwkv_conv[0].reshape(3, RW_TILES, P).transpose(2, 1, 0),
        "mlstm_conv": mlstm_conv[0].reshape(3, QK_TILES, P).transpose(2, 1, 0),
        "wa_up": np.concatenate([rwkv_w_up[0], rwkv_a_up[0]], 1).transpose(1, 0, 2),
        "rw_vecs": np.stack([column(v) for v in (rwkv_w0[0, 0], rwkv_w0[0, 1], rwkv_a0[0, 0], rwkv_a0[0, 1],
                                                 rwkv_k_k[0], rwkv_k_a[0])], 1),
        "g_up": rwkv_g_up[0],
        "rwo_vecs": np.stack([column(v[0]) for v in (rwkv_r_k, rwkv_ln_w, rwkv_ln_b)], 1),
        "gate_bias": gate_bias, "mlstm_g": column(mlstm_norm_g[0]),
        "w_merge": merge,
        "norm2_g": column(norm2_g[0]),
        "w_q": weight_tiles(peer_wq[0]),
        "keys": peer_keys[0].transpose(3, 0, 1, 2).reshape(P, 2 * PH, NK),
        "uT": peer_u[0].reshape(NK, NK, KT, P).transpose(1, 3, 2, 0),
        "v": peer_v[0].reshape(NK, NK, D).transpose(1, 0, 2),
        "final_g": column(final_g),
        "rwkv_masks": rwkv_masks(), "unit": np.tile(np.eye(C, dtype=np.float32), (2, 1)),
        "block_ones": np.kron(np.eye(2, dtype=np.float32), np.ones((C, C), np.float32)),
        "ident": np.eye(P, dtype=np.float32), "gate_resets": resets, "select": select, "m_mask": mask,
        "iota": np.tile(np.arange(NK, dtype=np.float32), (P, 1)),
    }


def kernel(**inputs):
    import concourse.bacc as _bacc
    from concourse.bass_utils import run_bass_kernel_spmd as _run

    nc = _bacc.Bacc("TRN2", target_bir_lowering=False, num_devices=1)
    arrays, args = {}, {}
    for name, v in laid_out(**inputs).items():
        v = np.ascontiguousarray(v)
        arrays[f"in_{name}"] = v
        args[name] = nc.dram_tensor(f"in_{name}", v.shape, mybir.dt.from_np(v.dtype), kind="ExternalInput").ap()
    out = nc.dram_tensor("out_y", (P, KT, TX), F32, kind="ExternalOutput").ap()
    build_program(nc, args, out)
    y = _run(nc, [arrays], core_ids=[0]).results[0]["out_y"]
    return y.transpose(1, 0, 2).reshape(D, TX).T[None]
```
